# Optimizing a Trainium2 kernel written in Bass

```python
import math
import jax, jax.numpy as jnp
from jax import lax
import numpy as np

D_MODEL = 1024
BATCH = 1
SEQ = 256
DEPTH = 2

N_MIXERS = 2
N_DIFF_LAYERS = (DEPTH + 1) // 2
N_SWA_LAYERS = DEPTH // 2

DIFF_HEADS = 8
DIFF_HEAD_DIM = D_MODEL // DIFF_HEADS // 2
DIFF_Q_BLOCK = 128

SWA_Q_HEADS = 16
SWA_KV_HEADS = 4
SWA_GROUP = SWA_Q_HEADS // SWA_KV_HEADS
SWA_HEAD_DIM = D_MODEL // SWA_Q_HEADS
WINDOW = 128
SWA_BLOCK = WINDOW

ROPE_DIM = 64
ROPE_THETA = 10000.0

D_FF = 2816
CONV_WIDTH = 3
PLE_DIM = 256
EPS = 1e-6


def rms_norm(x, g):
    xf = x.astype(jnp.float32)
    y = xf * lax.rsqrt(jnp.mean(xf * xf, axis=-1, keepdims=True) + EPS)
    return (y * g.astype(jnp.float32)).astype(x.dtype)

def rope_tables(positions):
    inv_freq = ROPE_THETA ** (-jnp.arange(0, ROPE_DIM, 2, dtype=jnp.float32) / ROPE_DIM)
    ang = positions.astype(jnp.float32)[..., None] * inv_freq
    return jnp.cos(ang), jnp.sin(ang)

def apply_rope(x, cos, sin):
    xf = x.astype(jnp.float32)
    x1, x2 = jnp.split(xf, 2, axis=-1)
    c, s = cos[:, :, None, :], sin[:, :, None, :]
    return jnp.concatenate([x1 * c - x2 * s, x2 * c + x1 * s], axis=-1).astype(x.dtype)

def diff_attention(h, w_qkv, w_o, lam, subln, cos, sin, layer_idx):
    B, S, _ = h.shape
    H, d = DIFF_HEADS, DIFF_HEAD_DIM
    q, k, v = jnp.split(h @ w_qkv, 3, axis=-1)
    q = apply_rope(q.reshape(B, S, 2 * H, d), cos, sin)
    k = apply_rope(k.reshape(B, S, 2 * H, d), cos, sin)
    v = v.reshape(B, S, H, 2 * d)
    lam_init = 0.8 - 0.6 * math.exp(-0.3 * layer_idx)
    lf = lam.astype(jnp.float32)
    lam_full = jnp.exp(jnp.sum(lf[0] * lf[1])) - jnp.exp(jnp.sum(lf[2] * lf[3])) + lam_init
    scale = d ** -0.5
    nb = S // DIFF_Q_BLOCK
    q_blocks = jnp.moveaxis(q.reshape(B, nb, DIFF_Q_BLOCK, 2 * H, d), 1, 0)

    def one_block(qb):
        s = jnp.einsum('bqhd,bkhd->bhqk', qb, k).astype(jnp.float32) * scale
        pr = jax.nn.softmax(s, axis=-1).reshape(B, H, 2, DIFF_Q_BLOCK, S)
        a = (pr[:, :, 0] - lam_full * pr[:, :, 1]).astype(v.dtype)
        return jnp.einsum('bhqk,bkhe->bqhe', a, v)

    o = lax.map(one_block, q_blocks)
    o = jnp.moveaxis(o, 0, 1).reshape(B, S, H, 2 * d)
    o = rms_norm(o, subln) * (1.0 - lam_init)
    return o.reshape(B, S, H * 2 * d) @ w_o

def windowed_gqa(h, w_qkv, w_o, sinks, cos, sin):
    B, S, _ = h.shape
    Hq, Hkv, G, d, L = SWA_Q_HEADS, SWA_KV_HEADS, SWA_GROUP, SWA_HEAD_DIM, SWA_BLOCK
    nb = S // L
    q, k, v = jnp.split(h @ w_qkv, [Hq * d, Hq * d + Hkv * d], axis=-1)
    q = apply_rope(q.reshape(B, S, Hq, d), cos, sin).reshape(B, nb, L, Hkv, G, d)
    k = apply_rope(k.reshape(B, S, Hkv, d), cos, sin)
    v = v.reshape(B, S, Hkv, d)

    def band(t):
        tp = jnp.pad(t, ((0, 0), (L, L), (0, 0), (0, 0))).reshape(B, nb + 2, L, Hkv, d)
        return jnp.concatenate([tp[:, :-2], tp[:, 1:-1], tp[:, 2:]], axis=2)

    kb, vb = band(k), band(v)
    s = jnp.einsum('bnqhgd,bnchd->bnhgqc', q, kb).astype(jnp.float32) * (d ** -0.5)
    blk = jnp.arange(nb)[:, None, None] * L
    qpos = blk + jnp.arange(L)[None, :, None]
    kpos = blk - L + jnp.arange(3 * L)[None, None, :]
    mask = (jnp.abs(kpos - qpos) <= WINDOW) & (kpos >= 0) & (kpos < S)
    s = jnp.where(mask[None, :, None, None], s, -jnp.inf)
    sink = sinks.astype(jnp.float32).reshape(1, 1, Hkv, G, 1, 1)
    m = jnp.maximum(jnp.max(s, axis=-1, keepdims=True), sink)
    e = jnp.exp(s - m)
    pr = e / (jnp.sum(e, axis=-1, keepdims=True) + jnp.exp(sink - m))
    o = jnp.einsum('bnhgqc,bnchd->bnqhgd', pr.astype(v.dtype), vb).reshape(B, S, Hq * d)
    return o @ w_o

def conv_ffn(h, w_up, conv_w, conv_b, w_down):
    S = h.shape[1]
    u = h @ w_up
    pad = CONV_WIDTH // 2
    up = jnp.pad(u, ((0, 0), (pad, pad), (0, 0)))
    u = sum(up[:, t:t + S] * conv_w[t] for t in range(CONV_WIDTH)) + conv_b
    gate, val = jnp.split(u, 2, axis=-1)
    return (jax.nn.silu(gate) * val) @ w_down

def first_inputs(seed: int = 0) -> dict:
    key = jax.random.key(seed)
    ks = jax.random.split(key, 24)
    D = D_MODEL

    def nrm(k, shape, scale):
        return jax.random.normal(k, shape, jnp.float32) * scale

    return {
        "x": nrm(ks[0], (BATCH, SEQ, D), 1.0),
        "p": nrm(ks[1], (DEPTH, BATCH, SEQ, PLE_DIM), 1.0),
        "positions": jnp.broadcast_to(jnp.arange(SEQ, dtype=jnp.int32), (BATCH, SEQ)),
        "attn_norm": 1.0 + nrm(ks[2], (DEPTH, D), 0.05),
        "ffn_norm": 1.0 + nrm(ks[3], (DEPTH, D), 0.05),
        "ple_norm": 1.0 + nrm(ks[4], (DEPTH, D), 0.05),
        "final_norm": 1.0 + nrm(ks[5], (D,), 0.05),
        "diff_w_qkv": nrm(ks[6], (N_DIFF_LAYERS, D, 3 * D), D ** -0.5),
        "diff_w_o": nrm(ks[7], (N_DIFF_LAYERS, D, D), D ** -0.5),
        "diff_lambda": nrm(ks[8], (N_DIFF_LAYERS, 4, DIFF_HEAD_DIM), 0.1),
        "diff_subln": 1.0 + nrm(ks[9], (N_DIFF_LAYERS, 2 * DIFF_HEAD_DIM), 0.05),
        "swa_w_qkv": nrm(ks[10], (N_SWA_LAYERS, D, (SWA_Q_HEADS + 2 * SWA_KV_HEADS) * SWA_HEAD_DIM), D ** -0.5),
        "swa_w_o": nrm(ks[11], (N_SWA_LAYERS, SWA_Q_HEADS * SWA_HEAD_DIM, D), D ** -0.5),
        "swa_sinks": nrm(ks[12], (N_SWA_LAYERS, SWA_Q_HEADS), 0.5),
        "ffn_w_up": nrm(ks[13], (DEPTH, D, 2 * D_FF), D ** -0.5),
        "ffn_conv_w": nrm(ks[14], (DEPTH, CONV_WIDTH, 2 * D_FF), CONV_WIDTH ** -0.5),
        "ffn_conv_b": nrm(ks[15], (DEPTH, 2 * D_FF), 0.02),
        "ffn_w_down": nrm(ks[16], (DEPTH, D_FF, D), D_FF ** -0.5),
        "ple_w_proj": nrm(ks[17], (DEPTH, PLE_DIM, D), PLE_DIM ** -0.5),
        "ple_w_gate": nrm(ks[18], (DEPTH, D, D), D ** -0.5),
    }

def first_block(x, p, positions, attn_norm, ffn_norm, ple_norm, final_norm,
              diff_w_qkv, diff_w_o, diff_lambda, diff_subln,
              swa_w_qkv, swa_w_o, swa_sinks,
              ffn_w_up, ffn_conv_w, ffn_conv_b, ffn_w_down,
              ple_w_proj, ple_w_gate):
    cos, sin = rope_tables(positions)
    h = x
    for i in range(DEPTH):
        j = i // N_MIXERS
        hn = rms_norm(h, attn_norm[i])
        if i % N_MIXERS == 0:
            mix = diff_attention(hn, diff_w_qkv[j], diff_w_o[j], diff_lambda[j], diff_subln[j], cos, sin, i)
        else:
            mix = windowed_gqa(hn, swa_w_qkv[j], swa_w_o[j], swa_sinks[j], cos, sin)
        h = h + mix
        h = h + conv_ffn(rms_norm(h, ffn_norm[i]), ffn_w_up[i], ffn_conv_w[i], ffn_conv_b[i], ffn_w_down[i])
        gate = jax.nn.sigmoid(rms_norm(h, ple_norm[i]) @ ple_w_gate[i])
        h = h + (p[i] @ ple_w_proj[i]) * gate
    return rms_norm(h, final_norm)


DEPTH_2 = 1

HEAD_DIM = 64
DIL_GROUPS = ((128, 1), (512, 4), (2048, 16))
DIL_HEADS_PER_GROUP = 4
N_DIL_HEADS = DIL_HEADS_PER_GROUP * len(DIL_GROUPS)
N_SB_HEADS = 8
DIL_WIDTH = N_DIL_HEADS * HEAD_DIM
DIL_OUT_WIDTH = DIL_HEADS_PER_GROUP * HEAD_DIM
SB_WIDTH = N_SB_HEADS * HEAD_DIM
D_FF_2 = 4 * D_MODEL
BLOCK = 128
RMS_EPS = 1e-6
NEG_INF = -1e30
IN_COLS = 3 * DIL_WIDTH + 3 * SB_WIDTH + 2 * D_MODEL
SPLITS = (DIL_WIDTH, 2 * DIL_WIDTH, 3 * DIL_WIDTH,
          3 * DIL_WIDTH + SB_WIDTH, 3 * DIL_WIDTH + 2 * SB_WIDTH, 3 * DIL_WIDTH + 3 * SB_WIDTH,
          3 * DIL_WIDTH + 3 * SB_WIDTH + D_MODEL)


def rmsnorm(x, g):
    xf = x.astype(jnp.float32)
    y = xf * lax.rsqrt(jnp.mean(xf * xf, axis=-1, keepdims=True) + RMS_EPS)
    return (y * g.astype(jnp.float32)).astype(x.dtype)

def alibi_slopes(n):
    return jnp.exp2(-8.0 * jnp.arange(1, n + 1, dtype=jnp.float32) / n)

def dilated_window_group(q, k, v, slopes, window, dilation):
    b, s, h, dh = q.shape
    n_steps = window // dilation
    nb = -(-s // (dilation * BLOCK))
    sub_len = nb * BLOCK
    s_pad = sub_len * dilation

    def to_blocks(t):
        t = jnp.pad(t, ((0, 0), (0, s_pad - s), (0, 0), (0, 0)))
        t = t.reshape(b, sub_len, dilation, h, dh)
        t = t.transpose(0, 2, 3, 1, 4)
        return t.reshape(b, dilation, h, nb, BLOCK, dh)

    qb, kb, vb = to_blocks(q), to_blocks(k), to_blocks(v)

    def with_prev(t):
        prev = jnp.pad(t[:, :, :, :-1], ((0, 0), (0, 0), (0, 0), (1, 0), (0, 0), (0, 0)))
        return jnp.concatenate([prev, t], axis=4)

    kk, vv = with_prev(kb), with_prev(vb)
    scores = jnp.einsum('brhnqd,brhnkd->brhnqk', qb, kk).astype(jnp.float32) / math.sqrt(dh)
    qi = jnp.arange(BLOCK)[:, None]
    kj = jnp.arange(2 * BLOCK)[None, :]
    steps = qi + BLOCK - kj
    key_sub_idx = jnp.arange(nb)[:, None, None] * BLOCK + kj[None] - BLOCK
    valid = (steps >= 0) & (steps <= n_steps) & (key_sub_idx >= 0)
    bias = -slopes[:, None, None].astype(jnp.float32) * (steps * dilation).astype(jnp.float32)
    logits = scores + bias[None, None, :, None]
    logits = jnp.where(valid[None, None, None], logits, NEG_INF)
    lse = jax.nn.logsumexp(logits, axis=-1)
    p = jnp.exp(logits - lse[..., None])
    o = jnp.einsum('brhnqk,brhnkd->brhnqd', p.astype(v.dtype), vv)

    def from_blocks(t):
        extra = t.shape[5:]
        t = t.reshape((b, dilation, h, sub_len) + extra)
        t = jnp.moveaxis(t, 3, 1)
        t = t.reshape((b, s_pad, h) + extra)
        return t[:, :s]

    return from_blocks(o), from_blocks(lse)

def dilated_attention(q, k, v):
    b, s = q.shape[:2]
    slopes = alibi_slopes(N_DIL_HEADS)
    outs, lses = [], []
    for g, (window, dilation) in enumerate(DIL_GROUPS):
        sl = slice(g * DIL_HEADS_PER_GROUP, (g + 1) * DIL_HEADS_PER_GROUP)
        o, l = dilated_window_group(q[:, :, sl], k[:, :, sl], v[:, :, sl], slopes[sl], window, dilation)
        outs.append(o)
        lses.append(l)
    o_all = jnp.stack(outs, axis=0).astype(jnp.float32)
    w = jax.nn.softmax(jnp.stack(lses, axis=0), axis=0)
    out = jnp.sum(w[..., None] * o_all, axis=0).astype(q.dtype)
    return out.reshape(b, s, DIL_OUT_WIDTH)

def stick_breaking_attention(q, k, v):
    b, s, h, dh = q.shape
    nb = s // BLOCK
    scale = 1.0 / math.sqrt(dh)
    kt = k.transpose(0, 2, 1, 3)
    vt = v.transpose(0, 2, 1, 3)
    q_blocks = q.transpose(0, 2, 1, 3).reshape(b, h, nb, BLOCK, dh).transpose(2, 0, 1, 3, 4)
    key_pos = jnp.arange(s)

    def one_block(args):
        i, q_blk = args
        z = jnp.einsum('bhqd,bhkd->bhqk', q_blk, kt).astype(jnp.float32) * scale
        q_pos = i * BLOCK + jnp.arange(BLOCK)
        causal = key_pos[None, :] < q_pos[:, None]
        log_one_minus = jnp.where(causal, jax.nn.log_sigmoid(-z), 0.0)
        suffix = lax.cumsum(log_one_minus, axis=3, reverse=True) - log_one_minus
        log_a = jax.nn.log_sigmoid(z) + suffix
        a = jnp.where(causal, jnp.exp(log_a), 0.0)
        return jnp.einsum('bhqk,bhkd->bhqd', a.astype(vt.dtype), vt)

    o_blocks = lax.map(one_block, (jnp.arange(nb), q_blocks))
    return o_blocks.transpose(1, 0, 3, 2, 4).reshape(b, s, h * dh)

def second_inputs(seed: int = 0) -> dict:
    key = jax.random.key(seed)
    ks = jax.random.split(key, 12)
    f32 = jnp.float32
    x = jax.random.normal(ks[0], (BATCH, SEQ, D_MODEL), f32)
    norm_mix_g = 1.0 + 0.02 * jax.random.normal(ks[1], (DEPTH_2, D_MODEL), f32)
    w_in = jax.random.normal(ks[2], (DEPTH_2, D_MODEL, IN_COLS), f32) * D_MODEL ** -0.5
    b_gate = 0.02 * jax.random.normal(ks[3], (DEPTH_2, 2 * D_MODEL), f32)
    w_up_dil = jax.random.normal(ks[4], (DEPTH_2, DIL_OUT_WIDTH, D_MODEL), f32) * DIL_OUT_WIDTH ** -0.5
    w_up_sb = jax.random.normal(ks[5], (DEPTH_2, SB_WIDTH, D_MODEL), f32) * SB_WIDTH ** -0.5
    w_out = jax.random.normal(ks[6], (DEPTH_2, D_MODEL, D_MODEL), f32) * D_MODEL ** -0.5
    norm_mlp_g = 1.0 + 0.02 * jax.random.normal(ks[7], (DEPTH_2, D_MODEL), f32)
    w_mlp_in = jax.random.normal(ks[8], (DEPTH_2, D_MODEL, D_FF_2), f32) * D_MODEL ** -0.5
    w_mlp_out = jax.random.normal(ks[9], (DEPTH_2, D_FF_2, D_MODEL), f32) * D_FF_2 ** -0.5
    norm_final_g = 1.0 + 0.02 * jax.random.normal(ks[10], (D_MODEL,), f32)
    return {"x": x, "norm_mix_g": norm_mix_g, "w_in": w_in, "b_gate": b_gate,
            "w_up_dil": w_up_dil, "w_up_sb": w_up_sb, "w_out": w_out,
            "norm_mlp_g": norm_mlp_g, "w_mlp_in": w_mlp_in, "w_mlp_out": w_mlp_out,
            "norm_final_g": norm_final_g}

def second_block(x, norm_mix_g, w_in, b_gate, w_up_dil, w_up_sb, w_out,
              norm_mlp_g, w_mlp_in, w_mlp_out, norm_final_g):
    b, s, _ = x.shape
    for layer in range(DEPTH_2):
        h = rmsnorm(x, norm_mix_g[layer])
        proj = h @ w_in[layer]
        q_a, k_a, v_a, q_b, k_b, v_b, gl_a, gl_b = jnp.split(proj, SPLITS, axis=-1)
        heads_a = lambda t: t.reshape(b, s, N_DIL_HEADS, HEAD_DIM)
        heads_b = lambda t: t.reshape(b, s, N_SB_HEADS, HEAD_DIM)
        o_a = dilated_attention(heads_a(q_a), heads_a(k_a), heads_a(v_a))
        o_b = stick_breaking_attention(heads_b(q_b), heads_b(k_b), heads_b(v_b))
        bg_a, bg_b = jnp.split(b_gate[layer], 2)
        g_a = jax.nn.sigmoid(gl_a + bg_a)
        g_b = jax.nn.sigmoid(gl_b + bg_b)
        merged = g_a * (o_a @ w_up_dil[layer]) + g_b * (o_b @ w_up_sb[layer])
        x = x + merged @ w_out[layer]
        h2 = rmsnorm(x, norm_mlp_g[layer])
        x = x + jnp.square(jax.nn.relu(h2 @ w_mlp_in[layer])) @ w_mlp_out[layer]
    return rmsnorm(x, norm_final_g)


def setup_inputs(seed=0):
    out = dict(first_inputs(seed))
    for name, value in second_inputs(seed + 1).items():
        if name != "x":
            out[name + "_2"] = value
    return out


def reference(
    x, p, positions, attn_norm, ffn_norm, ple_norm, final_norm, diff_w_qkv, diff_w_o,
    diff_lambda, diff_subln, swa_w_qkv, swa_w_o, swa_sinks, ffn_w_up, ffn_conv_w, ffn_conv_b,
    ffn_w_down, ple_w_proj, ple_w_gate, norm_mix_g_2, w_in_2, b_gate_2, w_up_dil_2, w_up_sb_2,
    w_out_2, norm_mlp_g_2, w_mlp_in_2, w_mlp_out_2, norm_final_g_2,
):
    x = first_block(
        x, p, positions, attn_norm, ffn_norm, ple_norm, final_norm, diff_w_qkv, diff_w_o,
        diff_lambda, diff_subln, swa_w_qkv, swa_w_o, swa_sinks, ffn_w_up, ffn_conv_w,
        ffn_conv_b, ffn_w_down, ple_w_proj, ple_w_gate,
    )
    return second_block(
        x, norm_mix_g_2, w_in_2, b_gate_2, w_up_dil_2, w_up_sb_2, w_out_2, norm_mlp_g_2,
        w_mlp_in_2, w_mlp_out_2, norm_final_g_2,
    )


_drawn_inputs = setup_inputs


def setup_inputs(seed=0):
    import zlib

    import numpy as np

    out = dict(_drawn_inputs(seed))
    spreads = {}
    factors = {'ple_norm': 5.33,
     'swa_sinks': 8.0,
     'ffn_conv_b': 3.091,
     'norm_mix_g_2': 5.211,
     'b_gate_2': 8.0,
     'norm_mlp_g_2': 3.229,
     'norm_final_g_2': 2.871}
    for name, (base, spread) in spreads.items():
        noise = np.random.default_rng([zlib.crc32(name.encode()), seed]).standard_normal(out[name].shape)
        drawn = base * np.exp(spread * noise) if base else spread * noise
        out[name] = __import__('jax').numpy.asarray(drawn.astype(out[name].dtype))
    for name, factor in factors.items():
        out[name] = (out[name] * factor).astype(out[name].dtype)
    return out
```

```python
import math
from contextlib import ExitStack

import numpy as np
import concourse.bass as bass
from concourse import mybir

F32 = mybir.dt.float32
F32R = mybir.dt.float32r
I32 = mybir.dt.int32
ALU = mybir.AluOpType
ACT = mybir.ActivationFunctionType
AX = mybir.AxisListType

P = 128
SEQ = 256
T = SEQ // P
D = 1024
KD = D // P
HALF = 512
HD = 64
FF = 2816
FT = FF // P
FF2 = 4096
PLE = 256
EPS = 1e-6
UNIT = 2048
RAW = 3
RING = 3
LAM_INIT = 0.8 - 0.6 * math.exp(0.0)
DIL_GROUPS = ((128, 1), (512, 4), (2048, 16))
N_DIL = 12
SLOPES = [2.0 ** (-8.0 * (n + 1) / N_DIL) for n in range(N_DIL)]
NEG = -1e30
FAR = 1e33

STAGES = [("qkv0", 12), ("wo0", 4), ("pp0", 1), ("ffn0", 33), ("gate0", 4),
          ("qkv1", 6), ("wo1", 4), ("pp1", 1), ("ffn1", 33), ("gate1", 4),
          ("in2", 15), ("gl2", 8), ("sbup", 2), ("dilup", 1), ("wout", 4), ("mlp", 32)]
U0 = {}
_n = 0
for _name, _count in STAGES:
    U0[_name] = _n
    _n += _count
NU = _n

TM_ORDER = [f"qkv0.{c}" for c in range(6)] + ["wo0", "pp0", "ffn0", "gate0"] \
    + [f"qkv1.{c}" for c in range(3)] + ["wo1", "pp1", "ffn1", "gate1"] \
    + ["in2.vb", "in2.va0", "in2.va1", "wout", "mlp"]
TM = {name: i + 1 for i, name in enumerate(TM_ORDER)}

GAIN = {0: 0, 1: 16, 2: 32, 3: 8, 4: 24, 5: 40, 6: 48, 7: 56}
V_BGATE, V_SUBLN, V_ROWS = 64, 80, 81
NORM_BANK = {0: 4, 1: 0, 2: 4, 3: 4, 4: 0, 5: 4, 6: 4, 7: 0}

C_ID = 0
C_SWA = C_ID + P
C_DIL0 = C_SWA + 2 * P
C_DIL1 = C_DIL0 + 3 * P
C_SB = C_DIL1 + 3 * SEQ
C_FREQ = C_SB + SEQ
C_COLS = C_FREQ + HD // 2


def at(value, step, i):
    return value if i is None else i * step + value


def constants():
    t = np.zeros((P, C_COLS), np.float32)
    q = np.arange(P)[:, None]
    k = np.arange(P)[None, :]
    t[:, C_ID:C_ID + P] = np.eye(P)
    t[:, C_SWA:C_SWA + P] = np.where(k <= q, 0.0, NEG)
    t[:, C_SWA + P:C_SWA + 2 * P] = np.where(q <= k, 0.0, NEG)
    for qt, (c0, nk) in enumerate(((C_DIL0, P), (C_DIL1, SEQ))):
        dist = qt * P + q - np.arange(nk)[None, :]
        for g, (window, dil) in enumerate(DIL_GROUPS):
            ok = (dist >= 0) & (dist % dil == 0) & (dist <= window)
            t[:, c0 + g * nk:c0 + (g + 1) * nk] = np.where(ok, dist, FAR)
    t[:, C_SB:C_SB + SEQ] = np.arange(SEQ)[None, :] < P + q
    t[:, C_FREQ:] = (10000.0 ** (-np.arange(0, HD, 2) / HD)).astype(np.float32)
    return t


def three_layer_kernel(nc, x, p, positions, attn_norm, ffn_norm, ple_norm, final_norm, diff_w_qkv,
                       diff_w_o, diff_lambda, diff_subln, swa_w_qkv, swa_w_o, swa_sinks, ffn_w_up,
                       ffn_conv_w, ffn_conv_b, ffn_w_down, ple_w_proj, ple_w_gate, norm_mix_g_2,
                       w_in_2, b_gate_2, w_up_dil_2, w_up_sb_2, w_out_2, norm_mlp_g_2, w_mlp_in_2,
                       w_mlp_out_2, norm_final_g_2, table, out):
    with ExitStack() as ctx:
        def sb(name, shape, dt=F32):
            return ctx.enter_context(nc.sbuf_tensor(name, shape, dt))

        def sem(name):
            return ctx.enter_context(nc.semaphore(name))

        raw = sb("raw", [P, RAW, UNIT])
        whi = sb("whi", [P, RING, UNIT], F32R)
        wlo = sb("wlo", [P, RING, UNIT], F32R)
        h = sb("h", [P, T, D])
        xn = sb("xn", [P, T, D])
        xhi = sb("xhi", [P, KD, SEQ], F32R)
        xlo = sb("xlo", [P, KD, SEQ], F32R)
        ohi = sb("ohi", [P, KD, SEQ], F32R)
        olo = sb("olo", [P, KD, SEQ], F32R)
        phi = sb("phi", [P, 4, SEQ], F32R)
        plo = sb("plo", [P, 4, SEQ], F32R)
        pp = sb("pp", [P, T, D])
        tab = sb("tab", [P, C_COLS])
        vecT = sb("vecT", [P, V_ROWS])
        cwT = sb("cwT", [P, 2, 4, 2 * FT])
        cosd = sb("cosd", [P, T, HD])
        sind = sb("sind", [P, T, HD])
        posi = sb("posi", [P, T], I32)
        lamb = sb("lamb", [P, 4, HD])
        sinks = sb("sinks", [P, 16])
        stat = sb("stat", [P, 400])
        scr = sb("scr", [P, 13056])
        ps = ctx.enter_context(nc.psum_tensor("ps", [P, 8, HALF], F32))

        ident = tab[:, C_ID:C_ID + P]

        def region(first, size, pattern=None, **kw):
            v = scr[:, first:first + size]
            return v.rearrange(pattern, **kw) if pattern else v

        ss = stat[:, 0:18]
        rstd = stat[:, 18:36]
        nhalf = stat[:, 36:44]
        nlam = stat[:, 44:45]
        subg = stat[:, 45:46]
        lam2 = stat[:, 46:48]
        posf = stat[:, 48:50]
        nsink = stat[:, 50:66]
        nmax = stat[:, 66:98].rearrange("p (b j) -> p b j", j=2)
        esum = stat[:, 98:130].rearrange("p (b j) -> p b j", j=2)
        rsum = stat[:, 130:162].rearrange("p (b j) -> p b j", j=2)
        mixc = stat[:, 162:178]
        oss = stat[:, 178:194].rearrange("p (s q d) -> p s q d", s=2, q=2)
        ors = stat[:, 194:210].rearrange("p (s q d) -> p s q d", s=2, q=2)
        sinkd = stat[:, 210:242].rearrange("p (b j) -> p b j", j=2)
        nmax1 = stat[:, 242:274].rearrange("p (b j) -> p b j", j=2)
        esum1 = stat[:, 274:306].rearrange("p (b j) -> p b j", j=2)
        rsum1 = stat[:, 306:338].rearrange("p (b j) -> p b j", j=2)
        nmax2 = stat[:, 338:346]
        esum2 = stat[:, 346:354]
        rsum2 = stat[:, 354:362]
        epsc = stat[:, 362:363]
        ssg = stat[:, 363:365]
        rboth = stat[:, 365:367]
        rtmp = stat[:, 367:369]

        stg = region(0, 5 * P, "p (a c) -> p a c", a=5)
        pst = region(640, 1024, "p (l t c) -> p l t c", l=2, t=2)
        trg = region(1664, 6 * 128, "p (a c) -> p a c", a=6)
        qT = region(2560, 2048, "p (a c) -> p a c", c=SEQ)
        kT = region(4608, 2048, "p (a c) -> p a c", c=SEQ)
        vtm = region(6656, 2048, "p (t c) -> p t c", t=T)
        rotA = region(8704, 1024, "p (t c) -> p t c", t=T)
        rotB = region(9728, 1024, "p (t c) -> p t c", t=T)
        Eb = region(10752, 1024, "p (b j c) -> p b j c", b=2, j=2)
        Ac = region(11776, 512, "p (b c) -> p b c", b=2)
        ATd = region(12288, 512, "p (b k c) -> p b k c", b=2, k=2)
        ATs = region(11776, 1024, "p (b k c) -> p b k c", b=2, k=4)
        junk = region(0, P)
        cgv = region(0, 2048, "p (b g c) -> p b g c", b=2, g=2)
        sgl = region(2048, 1024, "p (b c) -> p b c", b=2)
        hid = region(3072, 1024, "p (b c) -> p b c", b=2)
        ga = pp[:, :, :].rearrange("p t (m c) -> p (t m) c", c=SEQ)
        gb = region(0, 2048, "p (m c) -> p m c", c=SEQ)
        mB = region(2048, 2048, "p (j c) -> p j c", c=HALF)
        qTa = region(2048, 1536, "p (a c) -> p a c", c=SEQ)
        kTa = region(3584, 1536, "p (a c) -> p a c", c=SEQ)
        va = region(5120, 1536, "p (t c) -> p t c", t=T)
        qTb = region(6656, 1024, "p (a c) -> p a c", c=SEQ)
        kTb = region(7680, 1024, "p (a c) -> p a c", c=SEQ)
        vb = region(8704, 1024, "p (t c) -> p t c", t=T)
        sbe = region(9728, 512)
        sbl = region(10240, 512)
        sbs = region(10752, 512)
        sbc = region(11264, 512)
        sba = region(11776, 512)
        dlL = region(9728, 1536, "p (b c) -> p b c", b=2)
        ETb = region(12288, 768)
        rel = region(0, 1536, "p (b c) -> p b c", b=3)
        rsq = region(1536, 1536, "p (b c) -> p b c", b=3)
        gfin = region(4096, D)
        gmid = region(4096, D)

        raw_full = [sem(f"raw_full{s}") for s in range(RAW)]
        hi_ready = sem("hi_ready")
        lo_ready = sem("lo_ready")
        weights_used = sem("weights_used")
        tile0_done = sem("tile0_done")
        h_loaded = sem("h_loaded")
        table_loaded = sem("table_loaded")
        vecs_loaded = sem("vecs_loaded")
        p_loaded = sem("p_loaded")
        gmid_loaded = sem("gmid_loaded")
        hg_ready = sem("hg_ready")
        sumsqg_ready = sem("sumsqg_ready")
        h_final = sem("h_final")
        rboth_ready = sem("rboth_ready")
        gfin_loaded = sem("gfin_loaded")
        consts_set = sem("consts_set")
        vecs_T = sem("vecs_T")
        vecs_ready = sem("vecs_ready")
        pT_ready = sem("pT_ready")
        phi_ready = sem("phi_ready")
        plo_ready = sem("plo_ready")
        pp_ready = sem("pp_ready")
        trig_arg = sem("trig_arg")
        trig_ready = sem("trig_ready")
        lam_sums = sem("lam_sums")
        lam_exps = sem("lam_exps")
        h_ready = sem("h_ready")
        sumsq_ready = sem("sumsq_ready")
        rstd_ready = sem("rstd_ready")
        xn_ready = sem("xn_ready")
        xT_ready = sem("xT_ready")
        xhi_ready = sem("xhi_ready")
        xlo_ready = sem("xlo_ready")
        rope_read = sem("rope_read")
        rope_ready = sem("rope_ready")
        v_ready = sem("v_ready")
        t_ready = sem("t_ready")
        t_free = sem("t_free")
        s_ready = sem("s_ready")
        max_ready = sem("max_ready")
        exp_ready = sem("exp_ready")
        mix_ready = sem("mix_ready")
        o_ready = sem("o_ready")
        o_read = sem("o_read")
        sinkarg_ready = sem("sinkarg_ready")
        sinkexp_ready = sem("sinkexp_ready")
        orstd_ready = sem("orstd_ready")
        on_ready = sem("on_ready")
        oT_ready = sem("oT_ready")
        ohi_ready = sem("ohi_ready")
        olo_ready = sem("olo_ready")
        mid_ready = [sem(f"mid_ready{l}") for l in range(2)]
        tap_done = [sem(f"tap_done{l}") for l in range(2)]
        conv_done = [sem(f"conv_done{l}") for l in range(2)]
        silu_ready = [sem(f"silu_ready{l}") for l in range(2)]
        hid_ready = [sem(f"hid_ready{l}") for l in range(2)]
        hhi_ready = [sem(f"hhi_ready{l}") for l in range(2)]
        hlo_ready = [sem(f"hlo_ready{l}") for l in range(2)]
        gate_ready = sem("gate_ready")
        in2_read = sem("in2_read")
        sb_l = sem("sb_l")
        sb_arg = sem("sb_arg")
        sb_sel = sem("sb_sel")
        up_read = sem("up_read")
        merged = sem("merged")
        mhi_ready = sem("mhi_ready")
        mlo_ready = sem("mlo_ready")
        relu_ready = sem("relu_ready")
        sq_ready = sem("sq_ready")
        rhi_ready = sem("rhi_ready")
        rlo_ready = sem("rlo_ready")
        dve_step = sem("dve_step")
        act_step = sem("act_step")
        pool_step = sem("pool_step")
        out_ready = sem("out_ready")
        stored = sem("stored")

        def column(m, i):
            return slice(m, m + 1) if i is None else bass.ds(i * 4 + m, 1)

        def rows(w, k0, kk, c0, n):
            return w[k0 * P:(k0 + kk) * P, c0:c0 + n].rearrange("(k p) n -> p k n", p=P)

        IN2 = []
        u = U0["in2"]
        for kind, cols in (("qb", 512), ("kb", 512)):
            for j in range(cols // 256):
                IN2.append((kind, j, u, 1))
                u += 1
        IN2.append(("vb", 0, u, 2))
        u += 2
        for kind in ("qa", "ka"):
            for j in range(3):
                IN2.append((kind, j, u, 1))
                u += 1
        IN2.append(("va0", 0, u, 2))
        IN2.append(("va1", 0, u + 2, 2))
        u += 3
        for j in range(8):
            IN2.append(("gl", j, u, 1))
            u += 1
        in2_bank, in2_need, in2_count = [], [], []
        last_use, next_bank, done = {}, 0, 0
        for kind, j, u, nb in IN2:
            if nb == 2 and next_bank % 2:
                next_bank += 1
            banks = [(next_bank + i) % 4 for i in range(nb)]
            next_bank += nb
            in2_bank.append(banks[0])
            in2_need.append(max(last_use.get(b, 0) for b in banks))
            done += nb
            in2_count.append(done)
            for b in banks:
                last_use[b] = done
        in2_at = {f"{kind}{j}": n for n, (kind, j, _, _) in enumerate(IN2)}

        SB_BLOCKS = [(pr, qt) for qt in range(2) for pr in range(4)]
        DIL_BLOCKS = [(j, qt) for qt in range(2) for j in range(4)]
        BLOCKS = [(qt, i) for qt in range(2) for i in range(4)]
        N_A = 8

        T_USE = {}

        def t_use(name):
            T_USE[name] = len(T_USE)

        for name in ("q0", "k0"):
            for t in range(T):
                t_use(f"0{name}{t}")
        for s in range(N_A):
            t_use(f"0A{s}")
        for name in ("q1", "k1"):
            for t in range(T):
                t_use(f"0{name}{t}")
        for s in range(N_A):
            t_use(f"0B{s}")
        for name in ("k", "q0"):
            for t in range(T):
                t_use(f"1{name}{t}")
        for s in range(2 * N_A):
            t_use(f"1A{s}")
            if s == 1:
                for t in range(T):
                    t_use(f"1q1{t}")
        for s in range(8):
            t_use(f"2S{s}")
        for s, (j, qt) in enumerate(DIL_BLOCKS):
            t_use(f"2D{s}a")
            if qt:
                t_use(f"2D{s}b")

        TB, OB = 4, 5
        S_AT = {"A": 0, "B": 8, "1": 16, "S": 32, "D": 40}

        with nc.Block() as block:

            @block.sync
            def _(sp):
                sp.dma_start(h[:, :, :], x[0].rearrange("(t p) d -> p t d", p=P)).then_inc(h_loaded, 16)

                def load(u, src, kk, i=None):
                    if u >= RAW:
                        sp.wait_ge(lo_ready, at(u - RAW + 1, 6, i))
                    sp.dma_start(raw[:, u % RAW, :].rearrange("p (k n) -> p k n", k=kk), src)\
                        .then_inc(raw_full[u % RAW], 16)

                def load_rows(stage, w, u0=0):
                    for j in range(4):
                        load(U0[stage] + j, rows(w, 2 * j, 2, 0, D), 2)

                def load_ffn(l):
                    u0 = U0[f"ffn{l}"]
                    up = ffn_w_up[l].rearrange("(k p) n -> p k n", p=P)
                    down = ffn_w_down[l].rearrange("(g k p) n -> g p k n", k=2, p=P)
                    load(u0, up[:, :, 0:256], KD)
                    load(u0 + 1, up[:, :, FF:FF + 256], KD)
                    for it in (1, 2):
                        load(u0 + 3 * it - 1, up[:, :, 256 * it:256 * (it + 1)], KD)
                        load(u0 + 3 * it, up[:, :, FF + 256 * it:FF + 256 * (it + 1)], KD)
                        load(u0 + 3 * it + 1, rows(ffn_w_down[l], 2 * (it - 1), 2, 0, D), 2)
                    with sp.Fori(0, 4) as i:
                        gate_at = [sp.snap(i * 512 + 256 * (3 + n)) for n in range(2)]
                        val_at = [sp.snap(i * 512 + FF + 256 * (3 + n)) for n in range(2)]
                        down_at = [sp.snap(i * 2 + (2 + n)) for n in range(2)]
                        for n in range(2):
                            u = u0 + 3 * (3 + n) - 1
                            for what, src in enumerate((up[:, :, bass.ds(gate_at[n], 256)], up[:, :, bass.ds(val_at[n], 256)],
                                                        down[bass.ds(down_at[n], 1)].rearrange("g p k n -> p (g k) n"))):
                                load(u + what, src, (KD, KD, 2)[what], i)
                    load(u0 + 32, rows(ffn_w_down[l], 20, 2, 0, D), 2)

                wq = diff_w_qkv[0]
                u = U0["qkv0"]
                for c0 in (0, D, 2 * D, 2 * D + HALF, HALF, D + HALF):
                    for j in range(2):
                        load(u, rows(wq, 4 * j, 4, c0, HALF), 4)
                        u += 1
                load_rows("wo0", diff_w_o[0])
                load(U0["pp0"], rows(ple_w_proj[0], 0, 2, 0, D), 2)
                load_ffn(0)
                load_rows("gate0", ple_w_gate[0])
                u = U0["qkv1"]
                for c0 in (D, 0, HALF):
                    for j in range(2):
                        load(u, rows(swa_w_qkv[0], 4 * j, 4, c0, HALF), 4)
                        u += 1
                load_rows("wo1", swa_w_o[0])
                load(U0["pp1"], rows(ple_w_proj[1], 0, 2, 0, D), 2)
                load_ffn(1)
                load_rows("gate1", ple_w_gate[1])
                w = w_in_2[0]
                c_qa, c_ka, c_va = 0, 768, 1536
                c_qb, c_kb, c_vb, c_gl = 2304, 2816, 3328, 3840
                for kind, j, u, nb in IN2:
                    c0 = {"qb": c_qb, "kb": c_kb, "vb": c_vb, "qa": c_qa, "ka": c_ka, "va0": c_va,
                          "va1": c_va + HALF, "gl": c_gl}[kind]
                    if kind in ("vb", "va0"):
                        for i in range(2):
                            load(u + i, rows(w, 4 * i, 4, c0, HALF), 4)
                    else:
                        load(u, rows(w, 0, KD, c0 + 256 * j, 256), KD)
                for j in range(2):
                    load(U0["sbup"] + j, rows(w_up_sb_2[0], 0, 4, HALF * j, HALF), 4)
                load(U0["dilup"], rows(w_up_dil_2[0], 0, 2, 0, D), 2)
                load_rows("wout", w_out_2[0])
                u0 = U0["mlp"]
                up = w_mlp_in_2[0].rearrange("(k p) n -> p k n", p=P)
                down = w_mlp_out_2[0].rearrange("(g k p) n -> g p k n", k=2, p=P)
                load(u0, up[:, :, 0:256], KD)

                def mlp_units(it):
                    load(u0 + 2 * it - 1, up[:, :, 256 * it:256 * (it + 1)], KD)
                    load(u0 + 2 * it, rows(w_mlp_out_2[0], 2 * (it - 1), 2, 0, D), 2)

                mlp_units(1)
                with sp.Fori(0, 4) as i:
                    up_at = [sp.snap(i * 768 + 256 * (2 + n)) for n in range(3)]
                    down_at = [sp.snap(i * 3 + (1 + n)) for n in range(3)]
                    for n in range(3):
                        u = u0 + 2 * (2 + n) - 1
                        load(u, up[:, :, bass.ds(up_at[n], 256)], KD, i)
                        load(u + 1, down[bass.ds(down_at[n], 1)].rearrange("g p k n -> p (g k) n"), 2, i)
                mlp_units(14)
                mlp_units(15)
                load(u0 + 31, rows(w_mlp_out_2[0], 30, 2, 0, D), 2)
                for t in range(T):
                    sp.wait_ge(out_ready, t + 1)
                    sp.dma_start(out[0, t * P:(t + 1) * P, :], xn[:, t, :]).then_inc(stored, 16)
                sp.wait_ge(stored, 16 * T)

            @block.gpsimd
            def _(pool):
                steps = [0]

                def settle(ins):
                    steps[0] += 1
                    ins.then_inc(pool_step, 1)
                    pool.wait_ge(pool_step, steps[0])

                pool.memset(epsc, EPS)
                settle(pool.memset(nhalf, -0.5))

                def norm_rstd(n):
                    for t in range(T):
                        c = 2 * n + t
                        pool.wait_ge(sumsq_ready, c + 1)
                        settle(pool.tensor_scalar(rstd[:, c:c + 1], ss[:, c:c + 1], 1.0 / D, EPS, ALU.mult, ALU.add))
                        pool.tensor_tensor(rstd[:, c:c + 1], rstd[:, c:c + 1], nhalf[:, 0:1], ALU.pow)\
                            .then_inc(rstd_ready, 1)

                def rope_add(c, w):
                    for t in range(T):
                        pool.wait_ge(rope_read, 2 * c + t + 1)
                        pool.tensor_tensor(rotA[:, t, 0:w], rotA[:, t, 0:w], rotB[:, t, 0:w], ALU.add)\
                            .then_inc(rope_ready, 1)

                def o_rstd(st, qt):
                    pool.wait_ge(o_read, 8 * st + 4 * qt + 4)
                    settle(pool.tensor_scalar(ors[:, st, qt, :], oss[:, st, qt, :], 1.0 / P, EPS, ALU.mult, ALU.add))
                    pool.tensor_tensor(ors[:, st, qt, :], ors[:, st, qt, :], nhalf[:, 0:4], ALU.pow)\
                        .then_inc(orstd_ready, 1)

                norm_rstd(0)
                rope_add(0, HALF)
                rope_add(1, HALF)
                o_rstd(0, 0)
                rope_add(2, HALF)
                o_rstd(0, 1)
                rope_add(3, HALF)
                o_rstd(1, 0)
                o_rstd(1, 1)
                for n in (1, 2, 3):
                    norm_rstd(n)
                rope_add(4, 256)
                rope_add(5, HALF)
                rope_add(6, HALF)
                for n in (4, 5, 6):
                    norm_rstd(n)
                for t in range(T):
                    r, v = rstd[:, 12 + t:13 + t], rtmp[:, t:t + 1]
                    pool.wait_ge(rstd_ready, 13 + t)
                    pool.wait_ge(sumsqg_ready, t + 1)
                    settle(pool.tensor_scalar(v, ssg[:, t:t + 1], r, r, ALU.mult, ALU.mult))
                    settle(pool.tensor_scalar(v, v, 1.0 / D, EPS, ALU.mult, ALU.add))
                    settle(pool.tensor_tensor(v, v, nhalf[:, 0:1], ALU.pow))
                    pool.tensor_tensor(rboth[:, t:t + 1], v, r, ALU.mult).then_inc(rboth_ready, 1)
                for s, (pr, qt) in enumerate(SB_BLOCKS):
                    nk = P * (qt + 1)
                    pool.wait_ge(sb_arg, s + 1)
                    v = sba[:, 0:2 * nk].rearrange("p (j c) -> p j c", j=2)[:, :, nk - P:nk]
                    pool.affine_select(out=v, in_=v, compare_op=ALU.is_gt, fill=NEG, base=0,
                                       pattern=[[0, 2], [-1, P]], channel_multiplier=1).then_inc(sb_sel, 1)
                norm_rstd(7)
                norm_rstd(8)

            @block.scalar
            def _(act):
                split = [0]
                steps = [0]
                tcount = [0]

                def settle(ins):
                    steps[0] += 1
                    ins.then_inc(act_step, 1)
                    act.wait_ge(act_step, steps[0])

                def split_hi(u, i=None):
                    act.wait_ge(raw_full[u % RAW], at(16 * (u // RAW + 1), 16 * 6 // RAW, i))
                    if u >= RING:
                        act.wait_ge(weights_used, at(u - RING + 1, 6, i))
                    act.activation(whi[:, u % RING, :], raw[:, u % RAW, :], ACT.Copy).then_inc(hi_ready, 1)

                def ahead(u):
                    while split[0] < min(u + RING, NU):
                        split_hi(split[0])
                        split[0] += 1

                def keep_ahead(u, i):
                    if i is None:
                        ahead(u)
                    else:
                        split_hi(u + RING - 1, i)

                def copy_T(dst, src, scale=1.0):
                    act.wait_ge(t_ready, tcount[0] + 1)
                    if scale == 1.0:
                        act.activation(dst, src, ACT.Copy).then_inc(t_free, 1)
                    else:
                        act.activation(dst, src, ACT.Copy, scale=scale).then_inc(t_free, 1)
                    tcount[0] += 1

                def tile_done(name, u, t):
                    if t == 0:
                        act.wait_ge(tile0_done, TM[name])
                    else:
                        act.wait_ge(weights_used, u + 1)

                def norm_sumsq(n):
                    for t in range(T):
                        if n == 0:
                            act.wait_ge(h_loaded, 16)
                        else:
                            act.wait_ge(h_ready, 2 * (n - 1) + t + 1)
                        c = 2 * n + t
                        act.activation(xn[:, t, :], h[:, t, :], ACT.Square, accum_out=ss[:, c:c + 1])\
                            .then_inc(sumsq_ready, 1)

                def norm_hi(n):
                    if n == 0:
                        act.wait_ge(vecs_ready, 1)
                    for k in range(KD):
                        act.wait_ge(xT_ready, KD * n + k + 1)
                        g = GAIN[n] + k
                        act.activation(xhi[:, k, :], ps[:, NORM_BANK[n] + k % 4, 0:SEQ], ACT.Identity, scale=vecT[:, g:g + 1])\
                            .then_inc(xhi_ready, 1)

                def ple_proj(l):
                    u = U0[f"pp{l}"]
                    for t in range(T):
                        tile_done(f"pp{l}", u, t)
                        for hf in range(2):
                            act.activation(pp[:, t, hf * HALF:(hf + 1) * HALF], ps[:, 4 + 2 * t + hf, :], ACT.Copy)\
                                .then_inc(pp_ready, 1)

                def gate(l):
                    u = U0[f"gate{l}"] + 3
                    for t in range(T):
                        tile_done(f"gate{l}", u, t)
                        for hf in range(2):
                            act.activation(xn[:, t, hf * HALF:(hf + 1) * HALF], ps[:, 2 * t + hf, :], ACT.Sigmoid)\
                                .then_inc(gate_ready, 1)

                def ffn(l):
                    u0 = U0[f"ffn{l}"]

                    def mid(it, gv, buf, wait, i=None):
                        act.wait_ge(weights_used, wait)
                        for j in range(2):
                            m = column(2 * it + j + FT * gv, i)
                            ins = act.activation(cgv[:, buf, gv, j * SEQ:(j + 1) * SEQ],
                                                 ps[:, 4 + 2 * buf + gv, j * SEQ:(j + 1) * SEQ], ACT.Identity,
                                                 scale=cwT[:, l, 1, m], bias=cwT[:, l, 3, m])
                        ins.then_inc(mid_ready[l], 1)

                    def silu(buf, wait):
                        act.wait_ge(conv_done[l], wait)
                        act.activation(sgl[:, buf, :], cgv[:, buf, 0, :], ACT.Silu).then_inc(silu_ready[l], 1)

                    def hidden_hi(buf, wait):
                        act.wait_ge(hid_ready[l], wait)
                        act.activation(ohi[:, 2 * buf:2 * buf + 2, :].rearrange("p a c -> p (a c)"), hid[:, buf, :],
                                       ACT.Copy).then_inc(hhi_ready[l], 1)

                    def iteration(it, i=None):
                        ug, buf = u0 + 3 * it - 1, it % 2
                        for gv in range(2):
                            keep_ahead(ug + gv, i)
                            mid(it, gv, buf, at(ug + gv + 1, 6, i), i)
                        silu(buf, at(2 * it + 1, 4, i))
                        keep_ahead(ug + 2, i)
                        hidden_hi(buf, at(it + 1, 2, i))

                    for gv in range(2):
                        ahead(u0 + gv)
                        mid(0, gv, 0, u0 + gv + 1)
                    silu(0, 1)
                    hidden_hi(0, 1)
                    iteration(1)
                    iteration(2)
                    with act.Fori(0, 4) as i:
                        iteration(3, i)
                        iteration(4, i)
                    split[0] = u0 + 31 + RING
                    ahead(u0 + 32)

                def block_exp(lset, s, nm, es, base):
                    act.wait_ge(max_ready, S_AT[lset] + s + 1)
                    for j in range(2):
                        ins = act.activation(Eb[:, s % 2, j, :], ps[:, base + j, 0:SEQ], ACT.Exp,
                                             bias=nm[:, j:j + 1], scale=1.0, accum_out=es[:, j:j + 1])
                    ins.then_inc(exp_ready, 1)

                def o_copy0(st, s):
                    qt, i = BLOCKS[s]
                    b = 8 * st + s
                    act.wait_ge(o_ready, b + 1)
                    c = (4 * st + i) * P
                    act.activation(junk, ps[:, OB, 0:P], ACT.Square, scale=rsum[:, b, 0:1],
                                   accum_out=oss[:, st, qt, i:i + 1])
                    act.activation(xn[:, qt, c:c + P], ps[:, OB, 0:P], ACT.Identity, scale=rsum[:, b, 0:1])\
                        .then_inc(o_read, 1)

                act.dma_start(tab[:, :], table).then_inc(table_loaded, 16)
                vec_rows = [(attn_norm, 0, 16), (ffn_norm, 16, 16), (ple_norm, 32, 16), (norm_mix_g_2, 48, 8),
                            (norm_mlp_g_2, 56, 8), (b_gate_2, V_BGATE, 16), (diff_subln, V_SUBLN, 1)]
                for src, r0, n in vec_rows:
                    act.dma_start(stg[r0:r0 + n, 0, :], src.rearrange("l (r c) -> (l r) c", c=P)).then_inc(vecs_loaded, 16)
                for l in range(2):
                    act.dma_start(stg[0:2 * 2 * FT, 1 + 2 * l, :],
                                  ffn_conv_w[l, 0:2].rearrange("t (m c) -> (t m) c", c=P)).then_inc(vecs_loaded, 16)
                    act.dma_start(stg[0:2 * FT, 2 + 2 * l, :],
                                  ffn_conv_w[l, 2].rearrange("(m c) -> m c", c=P)).then_inc(vecs_loaded, 16)
                    act.dma_start(stg[2 * FT:4 * FT, 2 + 2 * l, :],
                                  ffn_conv_b[l].rearrange("(m c) -> m c", c=P)).then_inc(vecs_loaded, 16)
                act.dma_start(posi[:, :], positions[0].rearrange("(t p) -> p t", p=P),
                              allow_slow_non_contiguous=True).then_inc(vecs_loaded, 16)
                act.dma_start(lamb[:, :, :], diff_lambda[0].partition_broadcast(P)).then_inc(vecs_loaded, 16)
                act.dma_start(sinks[:, :], swa_sinks[0].partition_broadcast(P)).then_inc(vecs_loaded, 16)
                for l in range(2):
                    act.dma_start(pst[:, l], p[l, 0].rearrange("(t q) c -> q t c", q=P)).then_inc(p_loaded, 16)

                norm_sumsq(0)
                act.wait_ge(trig_arg, 1)
                act.activation(trg[:, 0, :], trg[:, 0, :], ACT.Sin).then_inc(trig_ready, 1)
                act.wait_ge(lam_sums, 1)
                act.activation(lam2, lam2, ACT.Exp).then_inc(lam_exps, 1)
                ahead(0)
                norm_hi(0)
                u = U0["qkv0"]
                ahead(u + 1)
                ahead(u + 2)
                for b in range(2):
                    act.wait_ge(pT_ready, b + 1)
                    act.activation(phi[:, 2 * b:2 * b + 2, :].rearrange("p a c -> p (a c)"), ps[:, 6 + b, :], ACT.Copy)\
                        .then_inc(phi_ready, 1)
                ahead(u + 3)

                def copy_qk(dst, tiles, t, scale):
                    copy_T(dst[:, tiles, t * P:(t + 1) * P], ps[:, TB, :].rearrange("p (a c) -> p a c", c=P)[:, 0:tiles.stop - tiles.start, :], scale)

                def v_copy(c, name, u, banks):
                    for t in range(T):
                        tile_done(name, u, t)
                        act.activation(vtm[:, t, c:c + HALF], ps[:, banks + t, :], ACT.Copy).then_inc(v_ready, 1)

                for t in range(T):
                    copy_qk(qT, slice(0, 4), t, 0.125)
                ahead(u + 4)
                for t in range(T):
                    copy_qk(kT, slice(0, 4), t, 1.0)
                ahead(u + 5)
                v_copy(0, "qkv0.2", u + 5, 0)

                def at_copy0(s):
                    copy_T(ATd[:, s % 2].rearrange("p k c -> p (k c)"), ps[:, TB, 0:2 * P])

                for s in range(N_A + 1):
                    if s:
                        at_copy0(s - 1)
                    ahead(u + 6 + s // 2)
                    if s < N_A:
                        block_exp("A", s, nmax[:, s], esum[:, s], 6)
                    if s == 5:
                        v_copy(HALF, "qkv0.3", u + 7, 2)
                    if s:
                        o_copy0(0, s - 1)
                for t in range(T):
                    copy_qk(qT, slice(4, 8), t, 0.125)
                ahead(u + 11)

                def o_hi(first, nt, count, scaled):
                    for qt in range(2):
                        act.wait_ge(oT_ready, count + qt + 1)
                        src = ps[:, 6 + qt, 0:nt * P].rearrange("p (a c) -> p a c", c=P)
                        dst = ohi[:, first:first + nt, qt * P:(qt + 1) * P]
                        if scaled:
                            act.activation(dst, src, ACT.Identity, scale=subg).then_inc(ohi_ready, 1)
                        else:
                            act.activation(dst, src, ACT.Copy).then_inc(ohi_ready, 1)

                o_hi(0, 4, 0, True)
                for t in range(T):
                    copy_qk(kT, slice(4, 8), t, 1.0)
                ahead(U0["wo0"])
                block_exp("B", 0, nmax[:, 8], esum[:, 8], 6)
                for s in range(N_A):
                    if s + 1 < N_A:
                        block_exp("B", s + 1, nmax[:, 9 + s], esum[:, 9 + s], (6, 2)[(s + 1) % 2])
                    at_copy0(s)
                    if s:
                        o_copy0(1, s - 1)
                o_copy0(1, N_A - 1)
                o_hi(4, 4, 2, True)
                for j in range(4):
                    ahead(U0["wo0"] + j)
                ahead(U0["pp0"])
                norm_sumsq(1)
                ple_proj(0)
                ahead(U0["ffn0"])
                norm_hi(1)
                ffn(0)
                norm_sumsq(2)
                ahead(U0["gate0"])
                norm_hi(2)
                for j in range(4):
                    ahead(U0["gate0"] + j)
                gate(0)

                norm_sumsq(3)
                u = U0["qkv1"]
                ahead(u)
                norm_hi(3)
                ahead(u + 1)
                ahead(u + 2)
                ahead(u + 3)
                for t in range(T):
                    copy_qk(kT, slice(0, 2), t, 1.0)
                ahead(u + 4)
                for t in range(T):
                    copy_qk(qT, slice(0, 4), t, 0.125)
                ahead(u + 5)

                def swa_exp(s):
                    block_exp("1", s, nmax1[:, s], esum1[:, s], (6, 2)[s % 2])
                    act.wait_ge(sinkarg_ready, s + 1)
                    act.activation(sinkd[:, s], sinkd[:, s], ACT.Exp).then_inc(sinkexp_ready, 1)

                swa_exp(0)
                for s in range(2 * N_A):
                    if s + 1 < 2 * N_A:
                        swa_exp(s + 1)
                    copy_T(ATs[:, s % 2].rearrange("p k c -> p (k c)"), ps[:, TB, :])
                    if s == 1:
                        for t in range(T):
                            copy_qk(qT, slice(4, 8), t, 0.125)
                ahead(U0["wo1"])
                o_hi(0, 4, 4, False)
                o_hi(4, 4, 6, False)
                for j in range(4):
                    ahead(U0["wo1"] + j)
                ahead(U0["pp1"])
                norm_sumsq(4)
                act.dma_start(gmid, final_norm.partition_broadcast(P)).then_inc(gmid_loaded, 16)
                ple_proj(1)
                ahead(U0["ffn1"])
                norm_hi(4)
                ffn(1)
                norm_sumsq(5)
                ahead(U0["gate1"])
                norm_hi(5)
                for j in range(4):
                    ahead(U0["gate1"] + j)
                gate(1)

                norm_sumsq(6)
                for t in range(T):
                    act.wait_ge(hg_ready, t + 1)
                    act.wait_ge(sumsq_ready, 13 + t)
                    act.activation(xn[:, t, :], pp[:, t, :], ACT.Square, accum_out=ssg[:, t:t + 1]).then_inc(sumsqg_ready, 1)
                ahead(U0["in2"])
                norm_hi(6)

                def in2_evac(n):
                    kind, j, u, nb = IN2[n]
                    bank = in2_bank[n]
                    if nb == 2:
                        w = 256 if kind == "va1" else HALF
                        dst, c0 = (vb, 0) if kind == "vb" else (va, HALF if kind == "va1" else 0)
                        ul = u if kind == "va1" else u + 1
                        ahead(ul)
                        for t in range(T):
                            tile_done("in2." + kind, ul, t)
                            act.activation(dst[:, t, c0:c0 + w], ps[:, bank + t, 0:w], ACT.Copy).then_inc(in2_read, 1)
                        return
                    act.wait_ge(weights_used, u + 1)
                    if kind == "gl":
                        dst = ga if j < 4 else gb
                        for m in range(2):
                            c = V_BGATE + 2 * j + m
                            ins = act.activation(dst[:, 2 * (j % 4) + m, :], ps[:, bank, m * SEQ:(m + 1) * SEQ], ACT.Sigmoid,
                                                 bias=vecT[:, c:c + 1], scale=1.0)
                        ins.then_inc(in2_read, 1)
                        return
                    dst = {"qa": qTa, "ka": kTa, "qb": qTb, "kb": kTb}[kind]
                    dst = dst[:, 2 * j:2 * j + 2, :].rearrange("p a c -> p (a c)")
                    if kind[0] == "q":
                        act.activation(dst, ps[:, bank, :], ACT.Copy, scale=0.125).then_inc(in2_read, 1)
                    else:
                        act.activation(dst, ps[:, bank, :], ACT.Copy).then_inc(in2_read, 1)

                def sb_first(s):
                    pr, qt = SB_BLOCKS[s]
                    nk = P * (qt + 1)
                    act.wait_ge(s_ready, S_AT["S"] + s + 1)
                    e = sbe[:, 0:2 * nk]
                    settle(act.activation(e.rearrange("p (j c) -> p j c", j=2), ps[:, 6:8, 0:nk], ACT.Abs))
                    settle(act.activation(e, e, ACT.Exp, scale=-1.0))
                    act.activation(sbl[:, 0:2 * nk], e, ACT.Ln, bias=1.0, scale=1.0).then_inc(sb_l, 1)

                def sb_second(s):
                    pr, qt = SB_BLOCKS[s]
                    nk = P * (qt + 1)
                    act.wait_ge(sb_sel, s + 1)
                    act.activation(sba[:, 0:2 * nk], sba[:, 0:2 * nk], ACT.Exp).then_inc(mix_ready, 1)

                def sb_copy(s):
                    pr, qt = SB_BLOCKS[s]
                    n = 2 * (qt + 1) * P
                    copy_T(ETb[:, 0:n], ps[:, TB, 0:n])

                def dil_exp(s):
                    j, qt = DIL_BLOCKS[s]
                    n = 3 * (qt + 1) * P
                    act.wait_ge(max_ready, MAX2 + s + 1)
                    act.activation(dlL[:, s % 2, 0:n], dlL[:, s % 2, 0:n], ACT.Exp, bias=nmax2[:, s:s + 1], scale=1.0,
                                   accum_out=esum2[:, s:s + 1]).then_inc(exp_ready, 1)

                def dil_copy(s):
                    j, qt = DIL_BLOCKS[s]
                    if qt:
                        copy_T(ETb[:, 0:HALF], ps[:, TB, :])
                        copy_T(ETb[:, HALF:HALF + 256], ps[:, TB, 0:256])
                    else:
                        copy_T(ETb[:, 0:3 * P], ps[:, TB, 0:3 * P])

                MAX2 = 32
                for n in range(5):
                    ahead(IN2[n][2])
                    in2_evac(n)
                for s in range(9):
                    if s:
                        sb_copy(s - 1)
                    ahead(IN2[5 + s][2])
                    if s < 8:
                        sb_first(s)
                        sb_second(s)
                    in2_evac(5 + s)
                o_hi(0, 4, 8, False)
                for s in range(9):
                    if s:
                        dil_copy(s - 1)
                    ahead(U0["gl2"] + 1 + s)
                    if s < 8:
                        dil_exp(s)
                    if s < 7:
                        in2_evac(in2_at["gl1"] + s)
                o_hi(4, 2, 10, False)
                ahead(U0["dilup"])
                for j in range(4):
                    act.wait_ge(merged, j + 1)
                    act.activation(xhi[:, 2 * j:2 * j + 2, :].rearrange("p a c -> p (a c)"), mB[:, j, :], ACT.Copy)\
                        .then_inc(mhi_ready, 1)
                    ahead(U0["wout"] + j - 1)
                ahead(U0["wout"] + 3)
                norm_sumsq(7)
                ahead(U0["mlp"])
                act.wait_ge(mlo_ready, 4)
                act.dma_start(gfin, norm_final_g_2.partition_broadcast(P)).then_inc(gfin_loaded, 16)
                norm_hi(7)
                u0 = U0["mlp"]

                def relu_hi(it, i=None):
                    b = it % 3
                    act.wait_ge(weights_used, at(u0 + 2 * it if it else u0 + 1, 6, i))
                    act.activation(rel[:, b, :], ps[:, 4 + b, :], ACT.Relu).then_inc(relu_ready, 1)
                    act.wait_ge(relu_ready, at(it + 1, 3, i))
                    act.activation(ohi[:, 2 * b:2 * b + 2, :].rearrange("p a c -> p (a c)"), rel[:, b, :], ACT.Square)\
                        .then_inc(rhi_ready, 1)

                def mlp_iteration(it, i=None):
                    keep_ahead(u0 + 2 * it - 1, i)
                    relu_hi(it, i)
                    keep_ahead(u0 + 2 * it, i)

                relu_hi(0)
                mlp_iteration(1)
                with act.Fori(0, 4) as i:
                    for n in range(3):
                        mlp_iteration(2 + n, i)
                split[0] = u0 + 27 + RING - 1
                mlp_iteration(14)
                mlp_iteration(15)
                norm_sumsq(8)

            @block.vector
            def _(dve):
                split = [0]
                steps = [0]

                def settle(ins):
                    steps[0] += 1
                    ins.then_inc(dve_step, 1)
                    dve.wait_ge(dve_step, steps[0])

                def split_lo(u, i=None):
                    dve.wait_ge(hi_ready, at(u + 1, 6, i))
                    dve.tensor_tensor(wlo[:, u % RING, :], raw[:, u % RAW, :], whi[:, u % RING, :].bitcast(F32),
                                      ALU.subtract).then_inc(lo_ready, 1)

                def ahead(u):
                    while split[0] < min(u + RING, NU):
                        split_lo(split[0])
                        split[0] += 1

                def keep_ahead(u, i):
                    if i is None:
                        ahead(u)
                    else:
                        split_lo(u + RING - 1, i)

                def tile_done(name, u, t):
                    if t == 0:
                        dve.wait_ge(tile0_done, TM[name])
                    else:
                        dve.wait_ge(weights_used, u + 1)

                def residual(name, u):
                    for t in range(T):
                        tile_done(name, u, t)
                        for hf in range(2):
                            v = h[:, t, hf * HALF:(hf + 1) * HALF]
                            ins = dve.tensor_tensor(v, ps[:, 2 * t + hf, :], v, ALU.add)
                        ins.then_inc(h_ready, 1)

                def norm_scale(n):
                    for t in range(T):
                        c = 2 * n + t
                        dve.wait_ge(rstd_ready, c + 1)
                        dve.tensor_scalar(xn[:, t, :], h[:, t, :], rstd[:, c:c + 1], None, ALU.mult).then_inc(xn_ready, 1)

                def norm_lo(n):
                    for k in range(KD):
                        dve.wait_ge(xhi_ready, KD * n + k + 1)
                        g = GAIN[n] + k
                        dve.scalar_tensor_tensor(xlo[:, k, :], ps[:, NORM_BANK[n] + k % 4, 0:SEQ], vecT[:, g:g + 1],
                                                 xhi[:, k, :].bitcast(F32), ALU.mult, ALU.subtract).then_inc(xlo_ready, 1)

                def rope_mul(c, name, u, bank, heads):
                    w = heads * HD
                    for t in range(T):
                        tile_done(name, u, t)
                        if c:
                            dve.wait_ge(t_ready, ROPE_T[c - 1] + t + 1)
                        src = ps[:, bank + t, 0:w]
                        n = 1 if heads == 4 or name[3] == "0" else 2
                        i = heads // n
                        per_head = lambda v: v.rearrange("p (a i d) -> p a i d", a=n, d=HD)
                        paired = lambda v: v.rearrange("p (i a d) -> p a i d", a=n, d=HD)
                        wide = lambda v: v.unsqueeze(1).unsqueeze(1).broadcast_to([P, n, i, v.shape[-1]])
                        dve.tensor_tensor(paired(rotA[:, t, 0:w]), per_head(src), wide(cosd[:, t, :]), ALU.mult)
                        for hf in range(2):
                            a = hf * HD // 2
                            b = HD // 2 - a
                            ins = dve.tensor_tensor(paired(rotB[:, t, 0:w])[:, :, :, a:a + HD // 2],
                                                    per_head(src)[:, :, :, b:b + HD // 2],
                                                    wide(sind[:, t, a:a + HD // 2]), ALU.mult)
                        if name == "qkv1.0":
                            ins = dve.tensor_copy(vtm[:, t, 0:256], ps[:, bank + t, 256:512])
                        ins.then_inc(rope_read, 1)

                ROPE_T = [T_USE[n] for n in ("0q00", "0k00", "0q10", "0k10", "1k0", "1q00", "1q10")]

                def gate(l):
                    dve.wait_ge(pp_ready, 4 * l + 4)
                    for t in range(T):
                        for hf in range(2):
                            dve.wait_ge(gate_ready, 4 * l + 2 * t + hf + 1)
                            v = xn[:, t, hf * HALF:(hf + 1) * HALF]
                            ins = dve.tensor_tensor(v, v, pp[:, t, hf * HALF:(hf + 1) * HALF], ALU.mult)
                        settle(ins)
                        dve.tensor_tensor(h[:, t, :], h[:, t, :], xn[:, t, :], ALU.add).then_inc(h_ready, 1)

                def ffn(l):
                    u0 = U0[f"ffn{l}"]

                    def taps(it, gv, i=None):
                        buf = it % 2
                        bank = 4 + 2 * buf + gv
                        dve.wait_ge(mid_ready[l], at(2 * it + gv + 1, 4, i))
                        for j in range(2):
                            o = j * SEQ
                            m = column(2 * it + j + FT * gv, i)
                            v = cgv[:, buf, gv, o + 1:o + SEQ]
                            dve.scalar_tensor_tensor(v, ps[:, bank, o:o + SEQ - 1], cwT[:, l, 0, m], v,
                                                     ALU.mult, ALU.add).then_inc(tap_done[l], 1)
                        for j in range(2):
                            o = j * SEQ
                            m = column(2 * it + j + FT * gv, i)
                            dve.wait_ge(tap_done[l], at(4 * it + 2 * gv + j + 1, 8, i))
                            v = cgv[:, buf, gv, o:o + SEQ - 1]
                            ins = dve.scalar_tensor_tensor(v, ps[:, bank, o + 1:o + SEQ], cwT[:, l, 2, m], v,
                                                           ALU.mult, ALU.add)
                        ins.then_inc(conv_done[l], 1)

                    def mult(buf, conv, n):
                        dve.wait_ge(conv_done[l], conv)
                        dve.wait_ge(silu_ready[l], n)
                        dve.tensor_tensor(hid[:, buf, :], sgl[:, buf, :], cgv[:, buf, 1, :], ALU.mult).then_inc(hid_ready[l], 1)

                    def hidden_lo(buf, n):
                        dve.wait_ge(hhi_ready[l], n)
                        dve.tensor_tensor(olo[:, 2 * buf:2 * buf + 2, :].rearrange("p a c -> p (a c)"), hid[:, buf, :],
                                          ohi[:, 2 * buf:2 * buf + 2, :].rearrange("p a c -> p (a c)").bitcast(F32),
                                          ALU.subtract).then_inc(hlo_ready[l], 1)

                    def iteration(it, i=None):
                        ug, buf = u0 + 3 * it - 1, it % 2
                        for gv in range(2):
                            keep_ahead(ug + gv, i)
                            taps(it, gv, i)
                        mult(buf, at(2 * it + 2, 4, i), at(it + 1, 2, i))
                        keep_ahead(ug + 2, i)
                        hidden_lo(buf, at(it + 1, 2, i))

                    for gv in range(2):
                        ahead(u0 + gv)
                        taps(0, gv)
                    mult(0, 2, 1)
                    hidden_lo(0, 1)
                    iteration(1)
                    iteration(2)
                    with dve.Fori(0, 4) as i:
                        iteration(3, i)
                        iteration(4, i)
                    split[0] = u0 + 31 + RING
                    ahead(u0 + 32)
                    residual(f"ffn{l}", u0 + 32)

                def block_max(lset, s, nm, base):
                    dve.wait_ge(s_ready, S_AT[lset] + s + 1)
                    dve.tensor_reduce(nm, ps[:, base:base + 2, 0:SEQ], AX.X, ALU.max, negate=True).then_inc(max_ready, 1)

                def block_mix(s8):
                    s = s8
                    dve.wait_ge(exp_ready, s8 + 1)
                    settle(dve.reciprocal(rsum[:, s], esum[:, s]))
                    settle(dve.scalar_tensor_tensor(mixc[:, s:s + 1], esum[:, s, 0:1], nlam, rsum[:, s, 1:2], ALU.mult, ALU.mult))
                    dve.scalar_tensor_tensor(Ac[:, s % 2, :], Eb[:, s % 2, 1, :], mixc[:, s:s + 1], Eb[:, s % 2, 0, :],
                                             ALU.mult, ALU.add).then_inc(mix_ready, 1)

                def o_norm(st, qt):
                    dve.wait_ge(orstd_ready, 2 * st + qt + 1)
                    v = xn[:, qt, st * HALF:(st + 1) * HALF].rearrange("p (d e) -> p d e", e=P)
                    dve.tensor_tensor(v, v, ors[:, st, qt, :].unsqueeze(2).broadcast_to([P, 4, P]), ALU.mult).then_inc(on_ready, 1)

                def o_lo(first, nt, count, scaled):
                    for qt in range(2):
                        dve.wait_ge(ohi_ready, count + qt + 1)
                        src = ps[:, 6 + qt, 0:nt * P].rearrange("p (a c) -> p a c", c=P)
                        dst = olo[:, first:first + nt, qt * P:(qt + 1) * P]
                        hi = ohi[:, first:first + nt, qt * P:(qt + 1) * P].bitcast(F32)
                        if scaled:
                            dve.scalar_tensor_tensor(dst, src, subg, hi, ALU.mult, ALU.subtract).then_inc(olo_ready, 1)
                        else:
                            dve.tensor_tensor(dst, src, hi, ALU.subtract).then_inc(olo_ready, 1)

                ang = trg[:, 1, 0:2 * HD // 2].rearrange("p (t f) -> p t f", t=T)
                turns = trg[:, 2, :]
                both = trg[:, 0, :].rearrange("p (a t f) -> p a t f", a=2, t=T)
                dve.wait_ge(table_loaded, 16)
                dve.wait_ge(vecs_loaded, 16 * 16)
                settle(dve.tensor_copy(posf, posi[:, :]))
                for t in range(T):
                    ins = dve.tensor_scalar(ang[:, t, :], tab[:, C_FREQ:C_FREQ + HD // 2], posf[:, t:t + 1], None, ALU.mult)
                settle(ins)
                flat = ang.rearrange("p t f -> p (t f)")
                MAGIC = 1.5 * 2.0 ** 23
                pieces = (6.28125, 0.0019350051879882812, 2 * math.pi - 6.28125 - 0.0019350051879882812)
                for a in range(2):
                    arg = trg[:, 0, a * HD:(a + 1) * HD]
                    settle(dve.tensor_scalar(turns[:, 0:HD], flat, 1.0 / (2 * math.pi), 0.25 * a, ALU.mult, ALU.add))
                    settle(dve.tensor_scalar(turns[:, 0:HD], turns[:, 0:HD], MAGIC, None, ALU.add))
                    settle(dve.tensor_scalar(turns[:, 0:HD], turns[:, 0:HD], MAGIC, None, ALU.subtract))
                    src = flat
                    for c in pieces:
                        settle(dve.scalar_tensor_tensor(arg, turns[:, 0:HD], -c, src, ALU.mult, ALU.add))
                        src = arg
                    if a:
                        settle(dve.tensor_scalar(arg, arg, math.pi / 2, None, ALU.add))
                    settle(dve.tensor_scalar(arg, arg, 3.1415925, -3.1415925, ALU.min, ALU.max))
                dve.tensor_copy(turns[:, 0:2], posf).then_inc(trig_arg, 1)
                settle(dve.tensor_tensor(trg[:, 3, :].rearrange("p (a d) -> p a d", a=2), lamb[:, 0::2, :], lamb[:, 1::2, :], ALU.mult))
                dve.tensor_reduce(lam2, trg[:, 3, :].rearrange("p (a d) -> p a d", a=2), AX.X, ALU.add).then_inc(lam_sums, 1)
                dve.tensor_scalar(nsink, sinks[:, :], -1.0, None, ALU.mult)
                dve.wait_ge(vecs_T, 1)
                dve.tensor_copy(vecT[:, :], ps[:, 0, 0:V_ROWS])
                for l in range(2):
                    for a in range(2):
                        ins = dve.tensor_copy(cwT[:, l, 2 * a:2 * a + 2, :].rearrange("p a m -> p (a m)"),
                                              ps[:, 1 + l, a * 4 * FT:(a + 1) * 4 * FT])
                settle(ins)
                dve.tensor_scalar(subg, vecT[:, V_SUBLN:V_SUBLN + 1], 1.0 - LAM_INIT, None, ALU.mult).then_inc(vecs_ready, 1)
                norm_scale(0)
                ahead(0)
                norm_lo(0)
                dve.wait_ge(trig_ready, 1)
                for t in range(T):
                    for a in range(2):
                        dve.tensor_copy(cosd[:, t, a * 32:a * 32 + 32], both[:, 1, t, :])
                        ins = dve.tensor_scalar(sind[:, t, a * 32:a * 32 + 32], both[:, 0, t, :], (-1.0, 1.0)[a], None, ALU.mult)
                settle(ins)
                dve.wait_ge(lam_exps, 1)
                settle(dve.scalar_tensor_tensor(nlam, lam2[:, 1:2], -LAM_INIT, lam2[:, 0:1], ALU.add, ALU.subtract))

                u = U0["qkv0"]
                ahead(u + 1)
                ahead(u + 2)
                rope_mul(0, "qkv0.0", u + 1, 0, 8)
                for b in range(2):
                    dve.wait_ge(phi_ready, b + 1)
                    dve.tensor_tensor(plo[:, 2 * b:2 * b + 2, :].rearrange("p a c -> p (a c)"), ps[:, 6 + b, :],
                                      phi[:, 2 * b:2 * b + 2, :].rearrange("p a c -> p (a c)").bitcast(F32), ALU.subtract)\
                        .then_inc(plo_ready, 1)
                ahead(u + 3)
                rope_mul(1, "qkv0.1", u + 3, 2, 8)
                ahead(u + 4)
                ahead(u + 5)
                for s in range(N_A):
                    ahead(u + 6 + s // 2)
                    block_max("A", s, nmax[:, s], 6)
                    block_mix(s)
                    if s == 5:
                        o_norm(0, 0)
                ahead(u + 10)
                rope_mul(2, "qkv0.4", u + 9, 0, 8)
                o_norm(0, 1)
                ahead(u + 11)
                rope_mul(3, "qkv0.5", u + 11, 2, 8)
                o_lo(0, 4, 0, True)
                ahead(U0["wo0"])
                block_max("B", 0, nmax[:, 8], 6)
                for s in range(N_A):
                    if s + 1 < N_A:
                        block_max("B", s + 1, nmax[:, 9 + s], (6, 2)[(s + 1) % 2])
                    block_mix(8 + s)
                    if s == 5:
                        o_norm(1, 0)
                o_norm(1, 1)
                o_lo(4, 4, 2, True)
                for j in range(4):
                    ahead(U0["wo0"] + j)
                residual("wo0", U0["wo0"] + 3)
                ahead(U0["pp0"])
                norm_scale(1)
                ahead(U0["ffn0"])
                norm_lo(1)
                ffn(0)
                ahead(U0["gate0"])
                norm_scale(2)
                norm_lo(2)
                for j in range(4):
                    ahead(U0["gate0"] + j)
                gate(0)

                u = U0["qkv1"]
                ahead(u)
                norm_scale(3)
                norm_lo(3)
                ahead(u + 1)
                ahead(u + 2)
                rope_mul(4, "qkv1.0", u + 1, 0, 4)
                ahead(u + 3)
                ahead(u + 4)
                rope_mul(5, "qkv1.1", u + 3, 2, 8)
                ahead(u + 5)

                def swa_max(s):
                    g, (qt, i) = s // N_A, BLOCKS[s % N_A]
                    base = (6, 2)[s % 2]
                    dve.wait_ge(s_ready, S_AT["1"] + s + 1)
                    c = (1 - qt) * P
                    v = ps[:, base:base + 2, c:c + P]
                    settle(dve.tensor_tensor(v, v, tab[:, C_SWA + qt * P:C_SWA + (qt + 1) * P].unsqueeze(1).broadcast_to([P, 2, P]), ALU.add))
                    settle(dve.tensor_reduce(nmax1[:, s], ps[:, base:base + 2, 0:SEQ], AX.X, ALU.max, negate=True))
                    pair = nsink.rearrange("p (g a i) -> p g i a", g=2, a=2)[:, g, i, :]
                    spair = sinks[:, :].rearrange("p (g a i) -> p g i a", g=2, a=2)[:, g, i, :]
                    dve.tensor_tensor(nmax1[:, s], nmax1[:, s], pair, ALU.min).then_inc(max_ready, 1)
                    dve.wait_ge(max_ready, S_AT["1"] + s + 1)
                    dve.tensor_tensor(sinkd[:, s], nmax1[:, s], spair, ALU.add).then_inc(sinkarg_ready, 1)

                def swa_sum(s):
                    dve.wait_ge(exp_ready, S_AT["1"] + s + 1)
                    dve.wait_ge(sinkexp_ready, s + 1)
                    settle(dve.tensor_tensor(esum1[:, s], esum1[:, s], sinkd[:, s], ALU.add))
                    settle(dve.reciprocal(rsum1[:, s], esum1[:, s]))

                def swa_out(s):
                    g, (qt, i) = s // N_A, BLOCKS[s % N_A]
                    dve.wait_ge(o_ready, S_AT["1"] + s + 1)
                    dst = xn[:, qt, :].rearrange("p (g a i d) -> p g i a d", g=2, a=2, d=HD)[:, g, i]
                    dve.tensor_tensor(dst, ps[:, OB, 0:2 * HD].rearrange("p (a d) -> p a d", d=HD),
                                      rsum1[:, s].unsqueeze(2).broadcast_to([P, 2, HD]), ALU.mult).then_inc(o_read, 1)

                swa_max(0)
                for s in range(2 * N_A):
                    if s + 1 < 2 * N_A:
                        swa_max(s + 1)
                    swa_sum(s)
                    if s == 0:
                        rope_mul(6, "qkv1.2", U0["qkv1"] + 5, 0, 8)
                    if s:
                        swa_out(s - 1)
                swa_out(2 * N_A - 1)
                ahead(U0["wo1"])
                o_lo(0, 4, 4, False)
                o_lo(4, 4, 6, False)
                for j in range(4):
                    ahead(U0["wo1"] + j)
                residual("wo1", U0["wo1"] + 3)
                ahead(U0["pp1"])
                norm_scale(4)
                ahead(U0["ffn1"])
                norm_lo(4)
                ffn(1)
                ahead(U0["gate1"])
                norm_scale(5)
                norm_lo(5)
                for j in range(4):
                    ahead(U0["gate1"] + j)
                gate(1)

                dve.wait_ge(gmid_loaded, 16)
                for t in range(T):
                    dve.wait_ge(h_ready, 11 + t)
                    dve.tensor_tensor(pp[:, t, :], h[:, t, :], gmid, ALU.mult).then_inc(hg_ready, 1)
                ahead(U0["in2"])
                for t in range(T):
                    dve.wait_ge(rboth_ready, t + 1)
                    dve.tensor_scalar(xn[:, t, :], pp[:, t, :], rboth[:, t:t + 1], None, ALU.mult).then_inc(xn_ready, 1)
                for t in range(T):
                    c = 12 + t
                    dve.wait_ge(rstd_ready, c + 1)
                    dve.tensor_scalar(h[:, t, :], pp[:, t, :], rstd[:, c:c + 1], None, ALU.mult).then_inc(h_final, 1)
                norm_lo(6)

                def sb_block(s):
                    pr, qt = SB_BLOCKS[s]
                    nk = P * (qt + 1)
                    z = ps[:, 6:8, 0:nk]
                    dve.wait_ge(sb_l, s + 1)
                    pair = lambda v: v[:, 0:2 * nk].rearrange("p (j c) -> p j c", j=2)
                    settle(dve.scalar_tensor_tensor(pair(sbs), z, 0.0, pair(sbl), ALU.max, ALU.add))
                    mask = tab[:, C_SB + SEQ - nk:C_SB + SEQ]
                    for j in range(2):
                        ins = dve.tensor_tensor_scan(sbc[:, j * nk:(j + 1) * nk][:, ::-1], sbs[:, j * nk:(j + 1) * nk][:, ::-1],
                                                     mask[:, ::-1], 0.0, ALU.add, ALU.mult)
                    settle(ins)
                    dve.tensor_tensor(pair(sba), z, pair(sbc), ALU.subtract).then_inc(sb_arg, 1)

                def sb_out(s):
                    pr, qt = SB_BLOCKS[s]
                    dve.wait_ge(o_ready, S_AT["S"] + s + 1)
                    dve.tensor_copy(xn[:, qt, 2 * pr * HD:(2 * pr + 2) * HD], ps[:, OB, 0:2 * HD]).then_inc(o_read, 1)

                def dil_max(s):
                    j, qt = DIL_BLOCKS[s]
                    nk = P * (qt + 1)
                    dve.wait_ge(s_ready, S_AT["D"] + s + 1)
                    for g in range(3):
                        c0 = (C_DIL0, C_DIL1)[qt] + g * nk
                        ins = dve.scalar_tensor_tensor(dlL[:, s % 2, g * nk:(g + 1) * nk], tab[:, c0:c0 + nk], -SLOPES[4 * g + j],
                                                       ps[:, 6 + g // 2, (g % 2) * nk:(g % 2 + 1) * nk], ALU.mult, ALU.add)
                    settle(ins)
                    dve.tensor_reduce(nmax2[:, s:s + 1], dlL[:, s % 2, 0:3 * nk], AX.X, ALU.max, negate=True).then_inc(max_ready, 1)

                def dil_sum(s):
                    dve.wait_ge(exp_ready, 32 + s + 1)
                    settle(dve.reciprocal(rsum2[:, s:s + 1], esum2[:, s:s + 1]))

                def dil_out(s):
                    j, qt = DIL_BLOCKS[s]
                    dve.wait_ge(o_ready, S_AT["D"] + s + 1)
                    dve.tensor_scalar(xn[:, qt, HALF + j * HD:HALF + (j + 1) * HD], ps[:, OB, 0:HD], rsum2[:, s:s + 1], None,
                                      ALU.mult).then_inc(o_read, 1)

                for n in range(5):
                    kind, j, u, nb = IN2[n]
                    ahead(u + nb - 1)
                for s in range(9):
                    kind, j, u, nb = IN2[5 + s]
                    ahead(u)
                    if s < 8:
                        sb_block(s)
                    if kind == "va0":
                        ahead(u + 1)
                    if s:
                        sb_out(s - 1)
                o_lo(0, 4, 8, False)
                for s in range(9):
                    ahead(U0["gl2"] + 1 + s)
                    if s < 8:
                        dil_max(s)
                        dil_sum(s)
                    if s:
                        dil_out(s - 1)
                o_lo(4, 2, 10, False)
                ahead(U0["dilup"])
                for j in range(4):
                    if j % 2 == 0:
                        dve.wait_ge(weights_used, U0["sbup"] + j // 2 + 1)
                    dve.wait_ge(in2_read, in2_count[-1])
                    dve.tensor_tensor(mB[:, j, :], ps[:, j, :], gb[:, 2 * j:2 * j + 2, :].rearrange("p a c -> p (a c)"), ALU.mult)\
                        .then_inc(up_read, 1)
                dve.wait_ge(weights_used, U0["dilup"] + 1)
                for j in range(4):
                    v = ga[:, 2 * j:2 * j + 2, :].rearrange("p a c -> p (a c)")
                    settle(dve.tensor_tensor(v, ps[:, 4 + j, :], v, ALU.mult))
                    dve.tensor_tensor(mB[:, j, :], mB[:, j, :], v, ALU.add).then_inc(merged, 1)
                    dve.wait_ge(mhi_ready, j + 1)
                    dve.tensor_tensor(xlo[:, 2 * j:2 * j + 2, :].rearrange("p a c -> p (a c)"), mB[:, j, :],
                                      xhi[:, 2 * j:2 * j + 2, :].rearrange("p a c -> p (a c)").bitcast(F32), ALU.subtract)\
                        .then_inc(mlo_ready, 1)
                for j in range(4):
                    ahead(U0["wout"] + j)
                residual("wout", U0["wout"] + 3)
                ahead(U0["mlp"])
                norm_scale(7)
                norm_lo(7)
                u0 = U0["mlp"]

                def square_lo(it, i=None):
                    b, n = it % 3, at(it + 1, 3, i)
                    dve.wait_ge(relu_ready, n)
                    dve.tensor_tensor(rsq[:, b, :], rel[:, b, :], rel[:, b, :], ALU.mult).then_inc(sq_ready, 1)
                    dve.wait_ge(sq_ready, n)
                    dve.wait_ge(rhi_ready, n)
                    dve.tensor_tensor(olo[:, 2 * b:2 * b + 2, :].rearrange("p a c -> p (a c)"), rsq[:, b, :],
                                      ohi[:, 2 * b:2 * b + 2, :].rearrange("p a c -> p (a c)").bitcast(F32),
                                      ALU.subtract).then_inc(rlo_ready, 1)

                def mlp_iteration(it, i=None):
                    keep_ahead(u0 + 2 * it - 1, i)
                    square_lo(it, i)
                    keep_ahead(u0 + 2 * it, i)

                square_lo(0)
                mlp_iteration(1)
                with dve.Fori(0, 4) as i:
                    for n in range(3):
                        mlp_iteration(2 + n, i)
                split[0] = u0 + 27 + RING - 1
                mlp_iteration(14)
                mlp_iteration(15)
                residual("mlp", u0 + 31)
                dve.wait_ge(gfin_loaded, 16)
                for t in range(T):
                    c = 16 + t
                    dve.wait_ge(rstd_ready, c + 1)
                    dve.scalar_tensor_tensor(xn[:, t, :], h[:, t, :], rstd[:, c:c + 1], gfin, ALU.mult, ALU.mult)\
                        .then_inc(out_ready, 1)

            @block.tensor
            def _(pe):
                tuse = [0]

                def mm(o, l, r, start, stop):
                    return pe.matmul(o, l, r, start=start, stop=stop, skip_group_check=True)

                def slot(ring, u, kk):
                    return ring[:, u % RING, :].rearrange("p (k n) -> p k n", k=kk)

                def tm_half(u, t, hi, lo, kk, bank, start, stop, xwait=None, uwait=None, k0=0):
                    n = UNIT // kk
                    w = min(n, HALF)
                    nb = n // w
                    wh, wl = slot(whi, u, kk), slot(wlo, u, kk)
                    if t == 0:
                        pe.wait_ge(lo_ready, u + 1 if uwait is None else uwait)
                    for k in range(kk):
                        if xwait is not None and t == 0:
                            pe.wait_ge(xlo_ready, xwait + k + 1)
                        xh = hi[:, k0 + k, t * P:(t + 1) * P]
                        xl = lo[:, k0 + k, t * P:(t + 1) * P]
                        for b in range(nb):
                            mm(ps[:, bank + b, 0:w], xh, wh[:, k, b * w:(b + 1) * w], start and k == 0, False)
                        for b in range(nb):
                            mm(ps[:, bank + b, 0:w], xh, wl[:, k, b * w:(b + 1) * w], False, False)
                        for b in range(nb):
                            ins = mm(ps[:, bank + b, 0:w], xl, wh[:, k, b * w:(b + 1) * w], False, stop and k == kk - 1)
                    if t == 1:
                        ins.then_inc(weights_used, 1)
                    elif stop:
                        ins.then_inc(tile0_done, 1)

                def fm_half(u, m, hi, lo, kk, bank, xwait=None, uwait=None, k0=0, last=1, n=256):
                    wh, wl = slot(whi, u, kk), slot(wlo, u, kk)
                    if m == 0:
                        pe.wait_ge(lo_ready, u + 1 if uwait is None else uwait)
                    o = ps[:, bank, (m % 2) * SEQ:(m % 2 + 1) * SEQ]
                    for k in range(kk):
                        if xwait is not None and m == 0:
                            pe.wait_ge(xlo_ready, xwait + k + 1)
                        mm(o, wh[:, k, m * P:(m + 1) * P], hi[:, k0 + k, :], k == 0, False)
                        mm(o, wh[:, k, m * P:(m + 1) * P], lo[:, k0 + k, :], False, False)
                        ins = mm(o, wl[:, k, m * P:(m + 1) * P], hi[:, k0 + k, :], False, k == kk - 1)
                    if m == last:
                        ins.then_inc(weights_used, 1)

                def norm_T(n):
                    for g in range(2):
                        for t in range(T):
                            for k in range(4 * g, 4 * g + 4):
                                if t == 0 and k >= 4:
                                    pe.wait_ge(xlo_ready, KD * n + k - 3)
                                if k == 0:
                                    pe.wait_ge(xn_ready, 2 * n + t + 1)
                                ins = pe.transpose(ps[:, NORM_BANK[n] + k % 4, t * P:(t + 1) * P], xn[:, t, k * P:(k + 1) * P], ident)
                                if t == T - 1:
                                    ins.then_inc(xT_ready, 1)

                def rows_stage(stage, hi, lo, name, waits=None):
                    for j in range(4):
                        if waits:
                            pe.wait_ge(*waits(j))
                        for t in range(T):
                            tm_half(U0[stage] + j, t, hi, lo, 2, 2 * t, j == 0, j == 3, k0=2 * j)

                def t_begin():
                    if tuse[0]:
                        pe.wait_ge(t_free, tuse[0])
                    tuse[0] += 1

                def qk_T(c, t, srcs):
                    t_begin()
                    pe.wait_ge(rope_ready, 2 * c + t + 1)
                    for n, src in enumerate(srcs):
                        ins = pe.transpose(ps[:, TB, n * P:(n + 1) * P], src, ident)
                    ins.then_inc(t_ready, 1)

                def flat_tiles(t, n):
                    return [rotA[:, t, i * P:(i + 1) * P] for i in range(n)]

                pe.wait_ge(table_loaded, 16)
                pe.wait_ge(vecs_loaded, 16 * 16)
                pe.transpose(ps[:, 0, 0:V_ROWS], stg[0:V_ROWS, 0, :], ident[0:V_ROWS, 0:V_ROWS])
                for l in range(2):
                    for a in range(2):
                        n = 4 * FT
                        ins = pe.transpose(ps[:, 1 + l, a * n:(a + 1) * n], stg[0:n, 1 + 2 * l + a, :], ident[0:n, 0:n])
                ins.then_inc(vecs_T, 1)

                norm_T(0)
                pe.wait_ge(vecs_ready, 1)
                u = U0["qkv0"]

                def chunk_half(base, c, j, t, xwait=None):
                    tm_half(base + 2 * c + j, t, xhi, xlo, 4, 2 * (c % 2) + t, j == 0, j == 1, xwait, k0=4 * j)

                for j in range(2):
                    for t in range(T):
                        chunk_half(u, 0, j, t, 4 * j)
                pe.wait_ge(p_loaded, 32)
                for b in range(2):
                    for k in range(2):
                        for t in range(T):
                            ins = pe.transpose(ps[:, 6 + b, k * SEQ + t * P:k * SEQ + (t + 1) * P],
                                               pst[:, b, t, k * P:(k + 1) * P], ident)
                    ins.then_inc(pT_ready, 1)
                for t in range(T):
                    chunk_half(u, 1, 0, t)
                for t in range(T):
                    qk_T(0, t, flat_tiles(t, 4))
                for t in range(T):
                    chunk_half(u, 1, 1, t)
                pe.wait_ge(rope_read, 2)
                for t in range(T):
                    chunk_half(u, 2, 0, t)
                for t in range(T):
                    qk_T(1, t, flat_tiles(t, 4))
                for t in range(T):
                    chunk_half(u, 2, 1, t)
                pe.wait_ge(plo_ready, 2)

                def scores0(st, s, base):
                    qt, i = BLOCKS[s]
                    tile = 4 * st + i
                    for j in range(2):
                        r = slice(j * HD, (j + 1) * HD)
                        ins = mm(ps[:, base + j, 0:SEQ], qT[r, tile, qt * P:(qt + 1) * P], kT[r, tile, :], True, True)
                    ins.then_inc(s_ready, 1)

                def probs_T0(st, s):
                    b = 8 * st + s
                    t_begin()
                    pe.wait_ge(mix_ready, b + 1)
                    for k in range(2):
                        ins = pe.transpose(ps[:, TB, k * P:(k + 1) * P], Ac[:, s % 2, k * P:(k + 1) * P], ident)
                    ins.then_inc(t_ready, 1)

                def pv0(st, s):
                    qt, i = BLOCKS[s]
                    b = 8 * st + s
                    c = (4 * st + i) * P
                    pe.wait_ge(t_free, T_USE["0" + "AB"[st] + str(s)] + 1)
                    pe.wait_ge(v_ready, 2 * st + 2)
                    if b:
                        pe.wait_ge(o_read, b)
                    for k in range(2):
                        ins = mm(ps[:, OB, 0:P], ATd[:, s % 2, k, :], vtm[:, k, c:c + P], k == 0, k == 1)
                    ins.then_inc(o_ready, 1)

                def o_T(nt, count, src, final):
                    if count:
                        pe.wait_ge(olo_ready, count)
                    for qt in range(2):
                        pe.wait_ge(*final(qt))
                        for n in range(nt):
                            ins = pe.transpose(ps[:, 6 + qt, n * P:(n + 1) * P], src(qt, n), ident)
                        ins.then_inc(oT_ready, 1)

                pe.wait_ge(t_free, 4)
                halves = [(3, 0, 0), (3, 0, 1), (3, 1, 0), (3, 1, 1), (4, 0, 0), (4, 0, 1), (4, 1, 0), (4, 1, 1),
                          (5, 0, 0), (5, 0, 1), (5, 1, 0), (5, 1, 1)]

                def half(n):
                    c, j, t = halves[n]
                    if n == 0:
                        pe.wait_ge(rope_read, 4)
                    if n == 4:
                        pe.wait_ge(v_ready, 2)
                    if n == 8:
                        pe.wait_ge(v_ready, 4)
                    chunk_half(u, c, j, t)

                for s in range(N_A + 1):
                    if s:
                        probs_T0(0, s - 1)
                    if s < N_A:
                        scores0(0, s, 6)
                    half(s)
                    if s:
                        pv0(0, s - 1)
                half(9)
                for t in range(T):
                    qk_T(2, t, flat_tiles(t, 4))
                half(10)
                half(11)
                o_T(4, 0, lambda qt, n: xn[:, qt, n * P:(n + 1) * P], lambda qt: (on_ready, qt + 1))
                for t in range(T):
                    qk_T(3, t, flat_tiles(t, 4))
                pe.wait_ge(t_free, T_USE["0k11"] + 1)
                pe.wait_ge(olo_ready, 2)
                scores0(1, 0, 6)
                scores0(1, 1, 2)
                for s in range(N_A):
                    probs_T0(1, s)
                    if s:
                        pv0(1, s - 1)
                    if s + 2 < N_A:
                        scores0(1, s + 2, (6, 2)[s % 2])
                pv0(1, N_A - 1)
                o_T(4, 2, lambda qt, n: xn[:, qt, HALF + n * P:HALF + (n + 1) * P], lambda qt: (on_ready, 2 + qt + 1))
                rows_stage("wo0", ohi, olo, "wo0", lambda j: (olo_ready, 2 if j < 2 else 4))

                def ple_proj(l):
                    for t in range(T):
                        tm_half(U0[f"pp{l}"], t, phi, plo, 2, 4 + 2 * t, True, True, k0=2 * l)

                def ffn(l):
                    u0 = U0[f"ffn{l}"]

                    def up(ug, buf, gv, i=None, xwait=None):
                        for m in range(2):
                            fm_half(ug, m, xhi, xlo, KD, 4 + 2 * buf + gv, xwait, at(ug + 1, 6, i))

                    def down(ud, it, start, stop, i=None):
                        pe.wait_ge(hlo_ready[l], at(it + 1, 2, i))
                        for t in range(T):
                            tm_half(ud, t, ohi, olo, 2, 2 * t, start, stop, None, at(ud + 1, 6, i), k0=2 * (it % 2))

                    def iteration(it, i=None):
                        ug = u0 + 3 * it - 1
                        for gv in range(2):
                            up(ug + gv, it % 2, gv, i)
                        down(ug + 2, it - 1, it == 1, False, i)

                    up(u0, 0, 0, xwait=KD * (1 + 3 * l))
                    up(u0 + 1, 0, 1)
                    iteration(1)
                    iteration(2)
                    with pe.Fori(0, 4) as i:
                        iteration(3, i)
                        iteration(4, i)
                    down(u0 + 32, 10, False, True)

                ple_proj(0)
                norm_T(1)
                pe.wait_ge(pp_ready, 4)
                ffn(0)
                norm_T(2)
                rows_stage("gate0", xhi, xlo, "gate0", lambda j: (xlo_ready, KD * 2 + 2 * j + 2))

                norm_T(3)
                u = U0["qkv1"]
                for j in range(2):
                    for t in range(T):
                        chunk_half(u, 0, j, t, KD * 3 + 4 * j)
                for t in range(T):
                    chunk_half(u, 1, 0, t)
                for t in range(T):
                    qk_T(4, t, flat_tiles(t, 2))
                for t in range(T):
                    chunk_half(u, 1, 1, t)
                pe.wait_ge(rope_read, 10)

                for t in range(T):
                    chunk_half(u, 2, 0, t)
                for t in range(T):
                    qk_T(5, t, flat_tiles(t, 4))
                for t in range(T):
                    chunk_half(u, 2, 1, t)

                def scores1(s):
                    g, (qt, i) = s // N_A, BLOCKS[s % N_A]
                    base = (6, 2)[s % 2]
                    if s == 0:
                        pe.wait_ge(t_free, T_USE["1q01"] + 1)
                    if s == 1:
                        pe.wait_ge(rope_read, 12)
                    if s == N_A:
                        pe.wait_ge(t_free, T_USE["1q11"] + 1)
                    for j in range(2):
                        r = slice(j * HD, (j + 1) * HD)
                        ins = mm(ps[:, base + j, 0:SEQ], qT[r, 4 * g + i, qt * P:(qt + 1) * P], kT[r, g, :], True, True)
                    ins.then_inc(s_ready, 1)

                def probs_T1(s):
                    t_begin()
                    pe.wait_ge(exp_ready, S_AT["1"] + s + 1)
                    for j in range(2):
                        for k in range(2):
                            n = 2 * j + k
                            ins = pe.transpose(ps[:, TB, n * P:(n + 1) * P], Eb[:, s % 2, j, k * P:(k + 1) * P], ident)
                    ins.then_inc(t_ready, 1)

                def pv1(s):
                    g = s // N_A
                    pe.wait_ge(t_free, T_USE[f"1A{s}"] + 1)
                    pe.wait_ge(o_read, S_AT["1"] + s)
                    for j in range(2):
                        c = (2 * g + j) * HD
                        for k in range(2):
                            ins = mm(ps[:, OB, j * HD:(j + 1) * HD], ATs[:, s % 2, 2 * j + k, :], vtm[:, k, c:c + HD],
                                     k == 0, k == 1)
                    ins.then_inc(o_ready, 1)

                scores1(0)
                scores1(1)
                for s in range(2 * N_A):
                    probs_T1(s)
                    if s:
                        pv1(s - 1)
                    if s == 1:
                        for t in range(T):
                            qk_T(6, t, flat_tiles(t, 4))
                    if s + 2 < 2 * N_A:
                        scores1(s + 2)
                pv1(2 * N_A - 1)
                for st in range(2):
                    o_T(4, 4 + 2 * st, lambda qt, n: xn[:, qt, (4 * st + n) * P:(4 * st + n + 1) * P], lambda qt: (o_read, 32))
                rows_stage("wo1", ohi, olo, "wo1", lambda j: (olo_ready, 6 if j < 2 else 8))
                ple_proj(1)
                norm_T(4)
                pe.wait_ge(pp_ready, 8)
                ffn(1)
                norm_T(5)
                rows_stage("gate1", xhi, xlo, "gate1", lambda j: (xlo_ready, KD * 5 + 2 * j + 2))

                norm_T(6)

                def in2(n):
                    kind, j, u, nb = IN2[n]
                    bank = in2_bank[n]
                    if in2_need[n]:
                        pe.wait_ge(in2_read, in2_need[n])
                    if kind in ("vb", "va0"):
                        for i in range(2):
                            for t in range(T):
                                tm_half(u + i, t, xhi, xlo, 4, bank + t, i == 0, i == 1, k0=4 * i)
                    elif kind == "va1":
                        for t in range(T):
                            tm_half(u, t, xhi, xlo, KD, bank + t, True, True)
                    else:
                        for m in range(2):
                            fm_half(u, m, xhi, xlo, KD, bank, KD * 6 if n == 0 else None)

                def scores_sb(s):
                    pr, qt = SB_BLOCKS[s]
                    nk = P * (qt + 1)
                    for j in range(2):
                        r = slice(j * HD, (j + 1) * HD)
                        ins = mm(ps[:, 6 + j, 0:nk], qTb[r, pr, qt * P:(qt + 1) * P], kTb[r, pr, 0:nk], True, True)
                    ins.then_inc(s_ready, 1)

                def weights_T_sb(s):
                    pr, qt = SB_BLOCKS[s]
                    t_begin()
                    pe.wait_ge(mix_ready, 16 + s + 1)
                    for n in range(2 * (qt + 1)):
                        ins = pe.transpose(ps[:, TB, n * P:(n + 1) * P], sba[:, n * P:(n + 1) * P], ident)
                    ins.then_inc(t_ready, 1)

                def pv_sb(s):
                    pr, qt = SB_BLOCKS[s]
                    pe.wait_ge(t_free, T_USE[f"2S{s}"] + 1)
                    pe.wait_ge(o_read, S_AT["S"] + s)
                    for j in range(2):
                        c = (2 * pr + j) * HD
                        for k in range(qt + 1):
                            n = j * (qt + 1) + k
                            ins = mm(ps[:, OB, j * HD:(j + 1) * HD], ETb[:, n * P:(n + 1) * P], vb[:, k, c:c + HD],
                                     k == 0, k == qt)
                    ins.then_inc(o_ready, 1)

                for n in range(5):
                    in2(n)
                pe.wait_ge(in2_read, in2_count[4])
                for s in range(9):
                    if s:
                        weights_T_sb(s - 1)
                    if s < 8:
                        scores_sb(s)
                    in2(5 + s)
                    if s:
                        pv_sb(s - 1)
                o_T(4, 8, lambda qt, n: xn[:, qt, n * P:(n + 1) * P], lambda qt: (o_read, S_AT["S"] + 8))

                def scores_dil(s):
                    j, qt = DIL_BLOCKS[s]
                    nk = P * (qt + 1)
                    for g in range(3):
                        hd = 4 * g + j
                        r = slice((hd % 2) * HD, (hd % 2 + 1) * HD)
                        ins = mm(ps[:, 6 + g // 2, (g % 2) * nk:(g % 2 + 1) * nk], qTa[r, hd // 2, qt * P:(qt + 1) * P],
                                 kTa[r, hd // 2, 0:nk], True, True)
                    ins.then_inc(s_ready, 1)

                def probs_T_dil(s, part):
                    j, qt = DIL_BLOCKS[s]
                    n = 3 * (qt + 1)
                    t_begin()
                    pe.wait_ge(exp_ready, 32 + s + 1)
                    for a in range(4 * part, min(n, 4 * part + 4)):
                        b = a - 4 * part
                        ins = pe.transpose(ps[:, TB, b * P:(b + 1) * P], dlL[:, s % 2, a * P:(a + 1) * P], ident)
                    ins.then_inc(t_ready, 1)

                def pv_dil(s):
                    j, qt = DIL_BLOCKS[s]
                    pe.wait_ge(t_free, T_USE[f"2D{s}" + "ab"[qt]] + 1)
                    pe.wait_ge(o_read, S_AT["D"] + s)
                    n = 3 * (qt + 1)
                    for a in range(n):
                        g, k = a // (qt + 1), a % (qt + 1)
                        c = (4 * g + j) * HD
                        ins = mm(ps[:, OB, 0:HD], ETb[:, a * P:(a + 1) * P], va[:, k, c:c + HD], a == 0, a == n - 1)
                    ins.then_inc(o_ready, 1)

                def sb_up(c):
                    for m in range(4):
                        fm_half(U0["sbup"] + c, m, ohi, olo, 4, 2 * c + m // 2, last=3)

                pe.wait_ge(olo_ready, 10)
                pe.wait_ge(in2_read, in2_count[in2_at["va10"]])
                for s in range(9):
                    if s:
                        probs_T_dil(s - 1, 0)
                    if s < 8:
                        scores_dil(s)
                    if s and DIL_BLOCKS[s - 1][1]:
                        probs_T_dil(s - 1, 1)
                    if s < 7:
                        in2(in2_at["gl1"] + s)
                    else:
                        pe.wait_ge(in2_read, in2_count[-1])
                        sb_up(s - 7)
                    if s:
                        pv_dil(s - 1)
                o_T(2, 10, lambda qt, n: xn[:, qt, HALF + n * P:HALF + (n + 1) * P], lambda qt: (o_read, S_AT["D"] + 8))
                pe.wait_ge(olo_ready, 12)
                for m in range(8):
                    fm_half(U0["dilup"], m, ohi, olo, 2, 4 + m // 2, k0=4, last=7)
                rows_stage("wout", xhi, xlo, "wout", lambda j: (mlo_ready, j + 1))

                norm_T(7)
                u0 = U0["mlp"]

                def mlp_up(u, it, i=None, xwait=None):
                    for m in range(2):
                        fm_half(u, m, xhi, xlo, KD, 4 + it % 3, xwait, at(u + 1, 6, i))

                def mlp_down(u, it, start, stop, i=None):
                    pe.wait_ge(rlo_ready, at(it + 1, 3, i))
                    for t in range(T):
                        tm_half(u, t, ohi, olo, 2, 2 * t, start, stop, None, at(u + 1, 6, i), k0=2 * (it % 3))

                def mlp_iteration(it, i=None):
                    mlp_up(u0 + 2 * it - 1, it, i)
                    mlp_down(u0 + 2 * it, it - 1, it == 1, False, i)

                mlp_up(u0, 0, xwait=KD * 7)
                mlp_iteration(1)
                with pe.Fori(0, 4) as i:
                    for n in range(3):
                        mlp_iteration(2 + n, i)
                mlp_iteration(14)
                mlp_iteration(15)
                mlp_down(u0 + 31, 15, False, True)


NAMES = ["x", "p", "positions", "attn_norm", "ffn_norm", "ple_norm", "final_norm", "diff_w_qkv", "diff_w_o",
         "diff_lambda", "diff_subln", "swa_w_qkv", "swa_w_o", "swa_sinks", "ffn_w_up", "ffn_conv_w", "ffn_conv_b",
         "ffn_w_down", "ple_w_proj", "ple_w_gate", "norm_mix_g_2", "w_in_2", "b_gate_2", "w_up_dil_2", "w_up_sb_2",
         "w_out_2", "norm_mlp_g_2", "w_mlp_in_2", "w_mlp_out_2", "norm_final_g_2"]


def kernel(**inputs):
    import concourse.bacc as bacc
    from concourse.bass_utils import run_bass_kernel_spmd

    nc = bacc.Bacc("TRN2", target_bir_lowering=False, num_devices=1)
    arrays, args = {}, []
    for name in NAMES:
        a = np.ascontiguousarray(inputs[name])
        arrays[f"in_{name}"] = a
        args.append(nc.dram_tensor(f"in_{name}", a.shape, mybir.dt.from_np(a.dtype), kind="ExternalInput").ap())
    table = constants()
    arrays["in_table"] = table
    args.append(nc.dram_tensor("in_table", table.shape, F32, kind="ExternalInput").ap())
    args.append(nc.dram_tensor("out_0", (1, SEQ, D), F32, kind="ExternalOutput").ap())
    three_layer_kernel(nc, *args)
    r = run_bass_kernel_spmd(nc, [arrays], core_ids=[0])
    return r.results[0]["out_0"]
```

```python
import math
from contextlib import ExitStack

import numpy as np
import concourse.bass as bass
from concourse import mybir

F32 = mybir.dt.float32
F32R = mybir.dt.float32r
BF16 = mybir.dt.bfloat16
I32 = mybir.dt.int32
ALU = mybir.AluOpType
ACT = mybir.ActivationFunctionType
AX = mybir.AxisListType

P = 128
SEQ = 256
T = SEQ // P
D = 1024
KD = D // P
HALF = 512
HD = 64
FF = 2816
FT = FF // P
FF2 = 4096
PLE = 256
EPS = 1e-6
UNIT = 2048
RAW = 3
TURN = 12
FFN_TURN = TURN // 3
MLP_TURN = TURN // 2
RING = 4
LAM_INIT = 0.8 - 0.6 * math.exp(0.0)
DIL_GROUPS = ((128, 1), (512, 4), (2048, 16))
N_DIL = 12
SLOPES = [2.0 ** (-8.0 * (n + 1) / N_DIL) for n in range(N_DIL)]
NEG = -1e30
FAR = 1e33

STAGES = [("qkv0", 12), ("pp0", 1), ("wo0", 4), ("ffn0", 33), ("gate0", 4),
          ("qkv1", 6), ("pp1", 1), ("wo1", 4), ("ffn1", 33), ("gate1", 4),
          ("in2", 15), ("gl2", 8), ("sbup", 2), ("dilup", 1), ("wout", 4), ("mlp", 32)]
U0 = {}
_n = 0
for _name, _count in STAGES:
    U0[_name] = _n
    _n += _count
NU = _n

TM_ORDER = [f"qkv0.{c}" for c in range(6)] + ["pp0"] + [f"qkv1.{c}" for c in range(3)] + ["pp1"] \
    + ["in2.vb", "in2.va0", "in2.va1"]
TM = {name: i + 1 for i, name in enumerate(TM_ORDER)}
RES_ORDER = ["wo0", "ffn0", "gate0", "wo1", "ffn1", "gate1", "wout", "mlp"]

V_BGATE, V_SUBLN, V_MID, V_ROWS = 48, 64, 65, 73
V_ATTN = 80
V_MIX = 96
V_COLS = 104
GAIN = {0: V_ATTN, 1: 0, 2: 16, 3: V_ATTN + 8, 4: 8, 5: 24, 6: V_MIX, 7: 40}
V_MIXG = 32
C_ID = 0
C_SWA = C_ID + P
C_DIL = C_SWA + 2 * P
C_FREQ = C_DIL + 3 * SEQ
C_COLS = C_FREQ + HD // 2


def at(value, step, i):
    return value if i is None else i * step + value


def constants():
    t = np.zeros((P, C_COLS), np.float32)
    q = np.arange(P)[:, None]
    k = np.arange(P)[None, :]
    t[:, C_ID:C_ID + P] = np.eye(P)
    t[:, C_SWA:C_SWA + P] = np.where(k <= q, 0.0, NEG)
    t[:, C_SWA + P:C_SWA + 2 * P] = np.where(q <= k, 0.0, NEG)
    dist = P + q - np.arange(SEQ)[None, :]
    for g, (window, dil) in enumerate(DIL_GROUPS):
        ok = (dist >= 0) & (dist % dil == 0) & (dist <= window)
        t[:, C_DIL + g * SEQ:C_DIL + (g + 1) * SEQ] = np.where(ok, dist, FAR)
    t[:, C_FREQ:] = (10000.0 ** (-np.arange(0, HD, 2) / HD)).astype(np.float32)
    return t


def three_layer_kernel(nc, x, p, positions, attn_norm, ffn_norm, ple_norm, final_norm, diff_w_qkv,
                       diff_w_o, diff_lambda, diff_subln, swa_w_qkv, swa_w_o, swa_sinks, ffn_w_up,
                       ffn_conv_w, ffn_conv_b, ffn_w_down, ple_w_proj, ple_w_gate, norm_mix_g_2,
                       w_in_2, b_gate_2, w_up_dil_2, w_up_sb_2, w_out_2, norm_mlp_g_2, w_mlp_in_2,
                       w_mlp_out_2, norm_final_g_2, table, out):
    with ExitStack() as ctx:
        def sb(name, shape, dt=F32):
            return ctx.enter_context(nc.sbuf_tensor(name, shape, dt))

        def sem(name):
            return ctx.enter_context(nc.semaphore(name))

        raw = sb("raw", [P, RAW, UNIT])
        whi = sb("whi", [P, RING, UNIT], F32R)
        wlo = sb("wlo", [P, RING, UNIT], F32R)
        h = sb("h", [P, T, D])
        xn = sb("xn", [P, T, D])
        xhi = sb("xhi", [P, KD, SEQ], F32R)
        xlo = sb("xlo", [P, KD, SEQ], F32R)
        ohi = sb("ohi", [P, KD, SEQ], F32R)
        olo = sb("olo", [P, KD, SEQ], F32R)
        phi = sb("phi", [P, 4, SEQ], F32R)
        plo = sb("plo", [P, 4, SEQ], F32R)
        pp = sb("pp", [P, T, D])
        tab = sb("tab", [P, C_COLS])
        vecT = sb("vecT", [P, V_COLS])
        ones = sb("ones", [P, SEQ])
        diag = sb("diag", [P, T, P])
        rB = sb("rB", [P, SEQ])
        rBq = sb("rBq", [P, SEQ])
        cosr = sb("cosr", [P, T, HD])
        sinr = sb("sinr", [P, T, HD])
        cwT = sb("cwT", [P, 2, 4, 2 * FT])
        cosd = sb("cosd", [P, T, HD])
        sind = sb("sind", [P, T, HD])
        posi = sb("posi", [P, T], I32)
        sinks = sb("sinks", [P, 16])
        stat = sb("stat", [P, 400])
        identb = sb("identb", [P, P], BF16)
        maskb = sb("maskb", [P, 2, P], BF16)
        zerob = sb("zerob", [P, P], BF16)
        scr = sb("scr", [P, 10368])
        ps = ctx.enter_context(nc.psum_tensor("ps", [P, 8, HALF], F32))

        ident = tab[:, C_ID:C_ID + P]

        def region(first, size, pattern=None, **kw):
            v = scr[:, first:first + size]
            return v.rearrange(pattern, **kw) if pattern else v

        ss = stat[:, 0:18]
        rstd = stat[:, 18:36]
        nhalf = stat[:, 36:44]
        nlam = stat[:, 44:45]
        subg = stat[:, 45:46]
        lam2 = stat[:, 46:48]
        posf = stat[:, 48:50]
        nsink = stat[:, 50:66]
        nmax = stat[:, 66:98].rearrange("p (b j) -> p b j", j=2)
        esum = stat[:, 98:130].rearrange("p (b j) -> p b j", j=2)
        rsum = stat[:, 130:162].rearrange("p (b j) -> p b j", j=2)
        mixc = stat[:, 162:178]
        oss = stat[:, 178:194].rearrange("p (s q d) -> p s q d", s=2, q=2)
        ors = stat[:, 194:210].rearrange("p (s q d) -> p s q d", s=2, q=2)
        sinkd = stat[:, 210:242].rearrange("p (b j) -> p b j", j=2)
        nmax1 = stat[:, 242:274].rearrange("p (b j) -> p b j", j=2)
        esum1 = stat[:, 274:306].rearrange("p (b j) -> p b j", j=2)
        rsum1 = stat[:, 306:338].rearrange("p (b j) -> p b j", j=2)
        nmax2 = stat[:, 338:346]
        esum2 = stat[:, 346:354]
        rsum2 = stat[:, 354:362]
        epsc = stat[:, 362:363]
        ssg = stat[:, 363:365]
        rboth = stat[:, 365:367]
        rtmp = stat[:, 367:369]
        minus1 = stat[:, 391:393]
        r2 = stat[:, 369:371]
        warm = stat[:, 371:391]

        qT = region(0, 2048, "p (a c) -> p a c", c=SEQ)
        kT = region(2048, 2048, "p (a c) -> p a c", c=SEQ)
        vtm = region(4096, 2048, "p (t c) -> p t c", t=T)
        rotA = region(6144, 1024, "p (t c) -> p t c", t=T)
        rotB = region(7168, 1024, "p (t c) -> p t c", t=T)
        Eb = region(8192, 1024, "p (b j c) -> p b j c", b=2, j=2)
        Ac = region(9216, 512, "p (b c) -> p b c", b=2)
        ATd = region(9728, 512, "p (b k c) -> p b k c", b=2, k=2)
        ATs = region(9216, 1024, "p (b k c) -> p b k c", b=2, k=4)
        junk = region(10240, P)
        stg = region(8192, 6 * P, "p (a c) -> p a c", a=6)
        pst = region(8960, 1024, "p (l t c) -> p l t c", l=2, t=2)
        trg = region(4096, 4 * P, "p (a c) -> p a c", a=4)
        lamb = region(4608, 4 * HD, "p (a d) -> p a d", a=4)
        cgv = region(0, 2048, "p (b g c) -> p b g c", b=2, g=2)
        sgl = region(2048, 1024, "p (b c) -> p b c", b=2)
        hid = region(3072, 1024, "p (b c) -> p b c", b=2)
        usc = region(4096, 2048, "p (b g c) -> p b g c", b=2, g=2)
        ga = pp[:, :, :].rearrange("p t (m c) -> p (t m) c", c=SEQ)
        gb = region(0, 2048, "p (m c) -> p m c", c=SEQ)
        mB = region(2048, 2048, "p (j c) -> p j c", c=HALF)
        qTa = region(2048, 1536, "p (a c) -> p a c", c=SEQ)
        kTa = region(3584, 1536, "p (a c) -> p a c", c=SEQ)
        va = region(5120, 1536, "p (t c) -> p t c", t=T)
        qTb = region(6656, 1024, "p (a c) -> p a c", c=SEQ)
        kTb = region(7680, 1024, "p (a c) -> p a c", c=SEQ)
        vb = region(8704, 1024, "p (t c) -> p t c", t=T)
        sbp = region(0, 512)
        sbm = region(512, 512)
        sbc = region(9728, 2 * (SEQ + 1), "p (j c) -> p j c", j=2)
        sba = region(1024, 512)
        ETs = region(1536, 512)
        dlL = region(6656, 1536, "p (b c) -> p b c", b=2)
        ETb = region(8192, 768)
        rel = region(0, 1536, "p (b c) -> p b c", b=3)
        rsq = region(1536, 1536, "p (b c) -> p b c", b=3)
        hg = pp
        gfin = region(6144, D)
        gmid = region(6144, D)

        raw_full = [sem(f"raw_full{s}") for s in range(RAW)]
        hi_ready = sem("hi_ready")
        hi_half = sem("hi_half")
        lo_ready = sem("lo_ready")
        weights_used = sem("weights_used")
        tile0_done = sem("tile0_done")
        bank_done = sem("bank_done")
        diag_ready = sem("diag_ready")
        rB_T = sem("rB_T")
        rB_ready = sem("rB_ready")
        rot_ready = sem("rot_ready")
        r2_ready = sem("r2_ready")
        ones_set = sem("ones_set")
        sum_ready = sem("sum_ready")
        prodp_ready = sem("prodp_ready")
        trig_loaded = sem("trig_loaded")
        gates_ready = sem("gates_ready")
        dilup_done = sem("dilup_done")
        prod_ready = sem("prod_ready")
        h_loaded = [sem(f"h_loaded{t}") for t in range(T)]
        ident_loaded = sem("ident_loaded")
        gain0_loaded = sem("gain0_loaded")
        gain0_T = sem("gain0_T")
        gain0_ready = sem("gain0_ready")
        table_loaded = sem("table_loaded")
        vecs_loaded = sem("vecs_loaded")
        p_loaded = sem("p_loaded")
        gmid_loaded = sem("gmid_loaded")
        hg_ready = sem("hg_ready")
        sumsqg_ready = sem("sumsqg_ready")
        h_final = sem("h_final")
        rboth_ready = sem("rboth_ready")
        gfin_loaded = sem("gfin_loaded")
        consts_set = sem("consts_set")
        vecs_T = sem("vecs_T")
        vecs_ready = sem("vecs_ready")
        pT_ready = sem("pT_ready")
        phi_ready = sem("phi_ready")
        plo_ready = sem("plo_ready")
        pp_ready = sem("pp_ready")
        trig_arg = sem("trig_arg")
        trig_ready = sem("trig_ready")
        lam_sums = sem("lam_sums")
        lam_exps = sem("lam_exps")
        h_ready = sem("h_ready")
        sumsq_ready = sem("sumsq_ready")
        rstd_ready = sem("rstd_ready")
        xT_ready = sem("xT_ready")
        xhi_ready = sem("xhi_ready")
        xlo_ready = sem("xlo_ready")
        rope_read = sem("rope_read")
        rope_ready = sem("rope_ready")
        v_ready = sem("v_ready")
        t_ready = sem("t_ready")
        t_free = sem("t_free")
        s_ready = sem("s_ready")
        max_ready = sem("max_ready")
        exp_ready = sem("exp_ready")
        mix_ready = sem("mix_ready")
        o_ready = sem("o_ready")
        o_read = sem("o_read")
        sinkarg_ready = sem("sinkarg_ready")
        sinkexp_ready = sem("sinkexp_ready")
        orstd_ready = sem("orstd_ready")
        on_ready = sem("on_ready")
        oT_ready = sem("oT_ready")
        ohi_ready = sem("ohi_ready")
        olo_ready = sem("olo_ready")
        mid_ready = [sem(f"mid_ready{l}") for l in range(2)]
        scaled = [sem(f"scaled{l}") for l in range(2)]
        tap_done = [sem(f"tap_done{l}") for l in range(2)]
        conv_done = [sem(f"conv_done{l}") for l in range(2)]
        silu_ready = [sem(f"silu_ready{l}") for l in range(2)]
        hid_ready = [sem(f"hid_ready{l}") for l in range(2)]
        hhi_ready = [sem(f"hhi_ready{l}") for l in range(2)]
        hlo_ready = [sem(f"hlo_ready{l}") for l in range(2)]
        gate_ready = sem("gate_ready")
        in2_read = sem("in2_read")
        sb_l = sem("sb_l")
        sb_sel = sem("sb_sel")
        merged = sem("merged")
        mhi_ready = sem("mhi_ready")
        mlo_ready = sem("mlo_ready")
        relu_ready = sem("relu_ready")
        sq_ready = sem("sq_ready")
        rhi_ready = sem("rhi_ready")
        rlo_ready = sem("rlo_ready")
        dve_step = sem("dve_step")
        act_step = sem("act_step")
        pool_step = sem("pool_step")
        out_ready = sem("out_ready")
        stored = sem("stored")

        def column(m, i):
            return slice(m, m + 1) if i is None else bass.ds(i * (2 * FFN_TURN) + m, 1)

        def rows(w, k0, kk, c0, n):
            return w[k0 * P:(k0 + kk) * P, c0:c0 + n].rearrange("(k p) n -> p k n", p=P)

        IN2 = []
        u = U0["in2"]
        IN2.append(("vb", 0, u, 2))
        u += 2
        for kind, cols in (("qb", 512), ("kb", 512)):
            for j in range(cols // 256):
                IN2.append((kind, j, u, 1))
                u += 1
        for kind in ("qa", "ka"):
            for j in range(3):
                IN2.append((kind, j, u, 1))
                u += 1
        IN2.append(("va0", 0, u, 2))
        IN2.append(("va1", 0, u + 2, 2))
        u += 3
        for j in range(8):
            IN2.append(("gl", j, u, 1))
            u += 1
        in2_bank, in2_need, in2_count = [], [], []
        last_use, next_bank, done = {}, 0, 0
        for kind, j, u, nb in IN2:
            if nb == 2 and next_bank % 2:
                next_bank += 1
            banks = [(next_bank + i) % 4 for i in range(nb)]
            next_bank += nb
            in2_bank.append(banks[0])
            in2_need.append(max(last_use.get(b, 0) for b in banks))
            done += nb
            in2_count.append(done)
            for b in banks:
                last_use[b] = done
        in2_at = {f"{kind}{j}": n for n, (kind, j, _, _) in enumerate(IN2)}

        SB_BLOCKS = [(pr, qt) for qt in range(2) for pr in range(4)]
        DIL_BLOCKS = [(j, qt) for qt in range(2) for j in range(4)]
        BLOCKS = [(qt, i) for qt in range(2) for i in range(4)]
        N_A = 8
        SWA_BLOCKS = [(g, qt, r, 2 * ip) for g in range(2) for qt in range(2) for r in range(2) for ip in range(2)]

        T_ORDER = [f"0{name}{t}" for name in ("q0", "k0") for t in range(T)]
        for s in range(1, N_A + 1):
            T_ORDER.append(f"0A{s - 1}")
            if s in (5, 6):
                T_ORDER.append(f"0q1{s - 5}")
        T_ORDER += ["0k10", "0k11"] + [f"0B{s}" for s in range(N_A)]
        T_ORDER += [f"1{name}{t}" for name in ("k", "q0") for t in range(T)]
        for s in range(2 * N_A):
            T_ORDER.append(f"1A{s}")
            if s in (5, 6):
                T_ORDER.append(f"1q1{s - 5}")
        T_ORDER += [f"2S{s}" for s in range(8)]
        for s, (j, qt) in enumerate(DIL_BLOCKS):
            T_ORDER += [f"2D{s}a", f"2D{s}b"][0:qt + 1]
        T_USE = {name: n for n, name in enumerate(T_ORDER)}
        PP_BANK = ((0, 2), (2, 0))

        TB, OB = 4, 5
        S_AT = {"A": 0, "B": 8, "1": 16, "S": 32, "D": 40}

        with nc.Block() as block:

            @block.sync
            def _(sp):
                sp.dma_start(h[:, 0, :], x[0, 0:P, :]).then_inc(h_loaded[0], 16)
                sp.dma_start(tab[:, 0:P], table[:, 0:P]).then_inc(ident_loaded, 16)
                sp.dma_start(stg[0:16, 5, :], attn_norm.rearrange("l (r c) -> (l r) c", c=P)).then_inc(gain0_loaded, 16)
                sp.dma_start(h[:, 1, :], x[0, P:2 * P, :]).then_inc(h_loaded[1], 16)

                def load_small():
                    sp.dma_start(posi[:, :], positions[0].rearrange("(t p) -> p t", p=P),
                                 allow_slow_non_contiguous=True).then_inc(trig_loaded, 16)
                    sp.dma_start(lamb[:, :, :], diff_lambda[0].partition_broadcast(P)).then_inc(trig_loaded, 16)
                    sp.dma_start(sinks[:, :], swa_sinks[0].partition_broadcast(P)).then_inc(trig_loaded, 16)
                    sp.dma_start(tab[:, P:C_COLS], table[:, P:C_COLS]).then_inc(table_loaded, 16)
                    for l in range(2):
                        sp.dma_start(pst[:, l], p[l, 0].rearrange("(t q) c -> q t c", q=P)).then_inc(p_loaded, 16)
                    vec_rows = [(ffn_norm, 0, 16), (ple_norm, 16, 16), (norm_mix_g_2, V_MIXG, 8), (norm_mlp_g_2, 40, 8),
                                (b_gate_2, V_BGATE, 16), (diff_subln, V_SUBLN, 1)]
                    for src, r0, n in vec_rows:
                        sp.dma_start(stg[r0:r0 + n, 0, :], src.rearrange("l (r c) -> (l r) c", c=P)).then_inc(vecs_loaded, 16)
                    sp.dma_start(stg[V_MID:V_MID + 8, 0, :], final_norm.rearrange("(r c) -> r c", c=P)).then_inc(vecs_loaded, 16)
                    for l in range(2):
                        sp.dma_start(stg[0:2 * 2 * FT, 1 + 2 * l, :],
                                     ffn_conv_w[l, 0:2].rearrange("t (m c) -> (t m) c", c=P)).then_inc(vecs_loaded, 16)
                        sp.dma_start(stg[0:2 * FT, 2 + 2 * l, :],
                                     ffn_conv_w[l, 2].rearrange("(m c) -> m c", c=P)).then_inc(vecs_loaded, 16)
                        sp.dma_start(stg[2 * FT:4 * FT, 2 + 2 * l, :],
                                     ffn_conv_b[l].rearrange("(m c) -> m c", c=P)).then_inc(vecs_loaded, 16)

                def load(u, src, kk, i=None):
                    if u >= RAW:
                        sp.wait_ge(lo_ready, at(u - RAW + 1, TURN, i))
                    sp.dma_start(raw[:, u % RAW, :].rearrange("p (k n) -> p k n", k=kk), src)\
                        .then_inc(raw_full[u % RAW], 16)

                def load_rows(stage, w, u0=0):
                    for j in range(4):
                        load(U0[stage] + j, rows(w, 2 * j, 2, 0, D), 2)

                def load_ffn(l):
                    u0 = U0[f"ffn{l}"]
                    up = ffn_w_up[l].rearrange("(k p) n -> p k n", p=P)
                    down = ffn_w_down[l].rearrange("(g k p) n -> g p k n", k=2, p=P)
                    load(u0, up[:, :, 0:256], KD)
                    load(u0 + 1, up[:, :, FF:FF + 256], KD)
                    with sp.Fori(0, 8 // FFN_TURN) as i:
                        gate_at = [sp.snap(i * (256 * FFN_TURN) + 256 * (1 + n)) for n in range(FFN_TURN)]
                        val_at = [sp.snap(i * (256 * FFN_TURN) + FF + 256 * (1 + n)) for n in range(FFN_TURN)]
                        down_at = [sp.snap(i * FFN_TURN + n) for n in range(FFN_TURN)]
                        for n in range(FFN_TURN):
                            u = u0 + 3 * (1 + n) - 1
                            for what, src in enumerate((up[:, :, bass.ds(gate_at[n], 256)], up[:, :, bass.ds(val_at[n], 256)],
                                                        down[bass.ds(down_at[n], 1)].rearrange("g p k n -> p (g k) n"))):
                                load(u + what, src, (KD, KD, 2)[what], i)
                    for n, it in enumerate((9, 10)):
                        load(u0 + 26 + 2 * n, up[:, :, 256 * it:256 * (it + 1)], KD)
                        load(u0 + 27 + 2 * n, up[:, :, FF + 256 * it:FF + 256 * (it + 1)], KD)
                    for n in range(3):
                        load(u0 + 30 + n, rows(ffn_w_down[l], 2 * (8 + n), 2, 0, D), 2)

                wq = diff_w_qkv[0]
                u = U0["qkv0"]
                for c0 in (0, D, 2 * D, HALF, D + HALF, 2 * D + HALF):
                    for j in range(2):
                        load(u, rows(wq, 4 * j, 4, c0, HALF), 4)
                        u += 1
                        if u == RAW:
                            load_small()
                load(U0["pp0"], rows(ple_w_proj[0], 0, 2, 0, D), 2)
                load_rows("wo0", diff_w_o[0])
                load_ffn(0)
                load_rows("gate0", ple_w_gate[0])
                u = U0["qkv1"]
                for c0 in (D, 0, HALF):
                    for j in range(2):
                        load(u, rows(swa_w_qkv[0], 4 * j, 4, c0, HALF), 4)
                        u += 1
                load(U0["pp1"], rows(ple_w_proj[1], 0, 2, 0, D), 2)
                load_rows("wo1", swa_w_o[0])
                load_ffn(1)
                load_rows("gate1", ple_w_gate[1])
                w = w_in_2[0]
                c_qa, c_ka, c_va = 0, 768, 1536
                c_qb, c_kb, c_vb, c_gl = 2304, 2816, 3328, 3840
                for kind, j, u, nb in IN2:
                    c0 = {"qb": c_qb, "kb": c_kb, "vb": c_vb, "qa": c_qa, "ka": c_ka, "va0": c_va,
                          "va1": c_va + HALF, "gl": c_gl}[kind]
                    if kind in ("vb", "va0"):
                        for i in range(2):
                            load(u + i, rows(w, 4 * i, 4, c0, HALF), 4)
                    else:
                        load(u, rows(w, 0, KD, c0 + 256 * j, 256), KD)
                for j in range(2):
                    load(U0["sbup"] + j, rows(w_up_sb_2[0], 0, 4, HALF * j, HALF), 4)
                load(U0["dilup"], rows(w_up_dil_2[0], 0, 2, 0, D), 2)
                load_rows("wout", w_out_2[0])
                u0 = U0["mlp"]
                up = w_mlp_in_2[0].rearrange("(k p) n -> p k n", p=P)
                down = w_mlp_out_2[0].rearrange("(g k p) n -> g p k n", k=2, p=P)
                load(u0, up[:, :, 0:256], KD)

                def mlp_units(it):
                    load(u0 + 2 * it - 1, up[:, :, 256 * it:256 * (it + 1)], KD)
                    load(u0 + 2 * it, rows(w_mlp_out_2[0], 2 * (it - 1), 2, 0, D), 2)

                mlp_units(1)
                with sp.Fori(0, 12 // MLP_TURN) as i:
                    up_at = [sp.snap(i * (256 * MLP_TURN) + 256 * (2 + n)) for n in range(MLP_TURN)]
                    down_at = [sp.snap(i * MLP_TURN + (1 + n)) for n in range(MLP_TURN)]
                    for n in range(MLP_TURN):
                        u = u0 + 2 * (2 + n) - 1
                        load(u, up[:, :, bass.ds(up_at[n], 256)], KD, i)
                        load(u + 1, down[bass.ds(down_at[n], 1)].rearrange("g p k n -> p (g k) n"), 2, i)
                mlp_units(14)
                mlp_units(15)
                load(u0 + 31, rows(w_mlp_out_2[0], 30, 2, 0, D), 2)
                for t in range(T):
                    sp.wait_ge(out_ready, t + 1)
                    sp.dma_start(out[0, t * P:(t + 1) * P, :], xn[:, t, :]).then_inc(stored, 16)
                sp.wait_ge(stored, 16 * T)

            @block.gpsimd
            def _(pool):
                steps = [0]

                def settle(ins):
                    steps[0] += 1
                    ins.then_inc(pool_step, 1)
                    pool.wait_ge(pool_step, steps[0])

                pool.memset(ones[:, :], 1.0).then_inc(ones_set, 1)
                pool.memset(minus1, -1.0)
                pool.memset(zerob[:, :], 0.0)
                settle(pool.memset(nhalf, -0.5))

                def norm_rstd(n):
                    for t in range(T):
                        c = 2 * n + t
                        r = rstd[:, c:c + 1]
                        pool.wait_ge(sumsq_ready, c + 1)
                        settle(pool.tensor_scalar(r, ss[:, c:c + 1], 1.0 / D, EPS, ALU.mult, ALU.add))
                        pool.tensor_tensor(r, r, nhalf[:, 0:1], ALU.pow).then_inc(rstd_ready, 1)
                        if n in (1, 4):
                            pool.wait_ge(ident_loaded, 16)
                            pool.wait_ge(rstd_ready, c + 1)
                            pool.tensor_scalar(diag[:, t, :], ident, r, None, ALU.mult).then_inc(diag_ready, 1)
                        if n == 7:
                            pool.wait_ge(rstd_ready, c + 1)
                            pool.tensor_tensor(r2[:, t:t + 1], r, r, ALU.mult).then_inc(r2_ready, 1)

                def rope_add(c, t, w):
                    pool.wait_ge(rope_read, 2 * c + t + 1)
                    pool.tensor_tensor(rotA[:, t, 0:w], rotA[:, t, 0:w], rotB[:, t, 0:w], ALU.add).then_inc(rope_ready, 1)

                def o_rstd(st, qt):
                    pool.wait_ge(o_read, 8 * st + 4 * qt + 4)
                    settle(pool.tensor_scalar(ors[:, st, qt, :], oss[:, st, qt, :], 1.0 / P, EPS, ALU.mult, ALU.add))
                    pool.tensor_tensor(ors[:, st, qt, :], ors[:, st, qt, :], nhalf[:, 0:4], ALU.pow)\
                        .then_inc(orstd_ready, 1)

                norm_rstd(0)
                for c in range(2):
                    for t in range(T):
                        rope_add(c, t, HALF)
                rope_add(2, 0, HALF)
                o_rstd(0, 0)
                rope_add(2, 1, HALF)
                rope_add(3, 0, HALF)
                o_rstd(0, 1)
                rope_add(3, 1, HALF)
                o_rstd(1, 0)
                o_rstd(1, 1)

                def gate_product(l):
                    pool.wait_ge(pp_ready, 4 * l + 4)
                    for b in range(3):
                        t, cols = b // 2, slice(b % 2 * HALF, (b % 2 + 1) * HALF)
                        pool.wait_ge(gate_ready, 4 * l + b + 1)
                        pool.tensor_tensor(xn[:, t, cols], xn[:, t, cols], pp[:, t, cols], ALU.mult).then_inc(prodp_ready, 1)

                norm_rstd(1)
                norm_rstd(2)
                gate_product(0)
                norm_rstd(3)
                for c, w in ((4, 256), (5, HALF)):
                    for t in range(T):
                        rope_add(c, t, w)
                def sink_arg(s):
                    g, qt, r, i = SWA_BLOCKS[s]
                    hd = 8 * g + 4 * r + i
                    pool.wait_ge(max_ready, S_AT["1"] + s + 1)
                    pool.tensor_tensor(sinkd[:, s], nmax1[:, s], sinks[:, hd:hd + 2], ALU.add).then_inc(sinkarg_ready, 1)

                sink_arg(0)
                for s in range(2 * N_A):
                    if s + 1 < 2 * N_A:
                        sink_arg(s + 1)
                    pool.wait_ge(exp_ready, S_AT["1"] + s + 1)
                    pool.wait_ge(sinkexp_ready, s + 1)
                    settle(pool.tensor_tensor(esum1[:, s], esum1[:, s], sinkd[:, s], ALU.add))
                    pool.tensor_tensor(rsum1[:, s], esum1[:, s], minus1, ALU.pow).then_inc(sum_ready, 1)
                    if s in (2, 4):
                        rope_add(6, s // 2 - 1, HALF)
                norm_rstd(4)
                norm_rstd(5)
                gate_product(1)
                norm_rstd(6)
                for t in range(T):
                    r, v = rstd[:, 12 + t:13 + t], rtmp[:, t:t + 1]
                    pool.wait_ge(rstd_ready, 13 + t)
                    pool.wait_ge(sumsqg_ready, t + 1)
                    settle(pool.tensor_scalar(v, ssg[:, t:t + 1], r, r, ALU.mult, ALU.mult))
                    settle(pool.tensor_scalar(v, v, 1.0 / D, EPS, ALU.mult, ALU.add))
                    settle(pool.tensor_tensor(v, v, nhalf[:, 0:1], ALU.pow))
                    pool.tensor_tensor(rboth[:, t:t + 1], v, r, ALU.mult).then_inc(rboth_ready, 1)
                    pool.wait_ge(rboth_ready, t + 1)
                    pool.tensor_scalar(diag[:, t, :], ident, rboth[:, t:t + 1], None, ALU.mult).then_inc(diag_ready, 1)
                for s, (pr, qt) in enumerate(SB_BLOCKS):
                    nk = P * (qt + 1)
                    pool.wait_ge(sb_l, s + 1)
                    for buf, fill in ((sbm, 1.0), (sbp, 0.0)):
                        v = buf[:, 0:2 * nk].rearrange("p (j c) -> p j c", j=2)[:, :, nk - P:nk]
                        pool.affine_select(out=v, in_=v, compare_op=ALU.is_gt, fill=fill, base=0,
                                           pattern=[[0, 2], [-1, P]], channel_multiplier=1).then_inc(sb_sel, 1)
                norm_rstd(7)
                norm_rstd(8)

            @block.scalar
            def _(act):
                split = [0]
                steps = [0]
                tcount = [0]

                def settle(ins):
                    steps[0] += 1
                    ins.then_inc(act_step, 1)
                    act.wait_ge(act_step, steps[0])

                def split_hi(u, i=None):
                    act.wait_ge(raw_full[u % RAW], at(16 * (u // RAW + 1), 16 * TURN // RAW, i))
                    if u >= RING:
                        act.wait_ge(weights_used, at(u - RING + 1, TURN, i))
                    act.activation(whi[:, u % RING, :], raw[:, u % RAW, :], ACT.Copy).then_inc(hi_ready, 1)

                half = [0]

                def split_half(count=1):
                    for _ in range(count):
                        u, a = split[0], half[0]
                        cols = slice(a * UNIT // 2, (a + 1) * UNIT // 2)
                        if a == 0:
                            act.wait_ge(raw_full[u % RAW], 16 * (u // RAW + 1))
                            act.wait_ge(weights_used, u - RING + 1)
                        ins = act.activation(whi[:, u % RING, cols], raw[:, u % RAW, cols], ACT.Copy)
                        ins.then_inc(hi_ready if a else hi_half, 1)
                        split[0] += a
                        half[0] = 1 - a

                def ahead(u):
                    if half[0]:
                        split_half()
                    while split[0] < min(u + RING, NU):
                        split_hi(split[0])
                        split[0] += 1

                def keep_ahead(u, i):
                    if i is None:
                        ahead(u)
                    else:
                        split_hi(u + RING - 1, i)

                def copy_T(dst, src, scale=1.0):
                    act.wait_ge(t_ready, tcount[0] + 1)
                    if scale == 1.0:
                        act.activation(dst, src, ACT.Copy).then_inc(t_free, 1)
                    else:
                        act.activation(dst, src, ACT.Copy, scale=scale).then_inc(t_free, 1)
                    tcount[0] += 1

                def tile_done(name, u, t):
                    if t == 0:
                        act.wait_ge(tile0_done, TM[name])
                    else:
                        act.wait_ge(weights_used, u + 1)

                def preload(n, func):
                    act.activation(warm[:, n:n + 1], nhalf[:, 0:1], func)

                def norm_hi(n):
                    for t in range(T):
                        for b in range(4):
                            act.wait_ge(xT_ready, KD * n + 4 * t + b + 1)
                            for k in (2 * b, 2 * b + 1):
                                g = GAIN[n] + k
                                act.activation(xhi[:, k, t * P:(t + 1) * P],
                                               ps[:, 4 + b, (k % 2) * SEQ + t * P:(k % 2) * SEQ + (t + 1) * P],
                                               ACT.Identity, scale=vecT[:, g:g + 1]).then_inc(xhi_ready, 1)

                def norm_sumsq(n):
                    for t in range(T):
                        if n == 0:
                            act.wait_ge(h_loaded[t], 16)
                        else:
                            act.wait_ge(h_ready, 4 * (n - 1) + 2 * t + 2)
                        c = 2 * n + t
                        act.activation(xn[:, t, :], h[:, t, :], ACT.Square, accum_out=ss[:, c:c + 1])\
                            .then_inc(sumsq_ready, 1)

                def rms_row(n):
                    act.wait_ge(rB_T, n + 1)
                    act.activation(rB[:, :], ps[:, (0, 0, 7)[n], 0:SEQ], ACT.Copy).then_inc(rB_ready, 1)
                    if n == 2:
                        act.activation(rBq[:, :], ps[:, 7, 0:SEQ], ACT.Copy, scale=0.125).then_inc(rB_ready, 1)

                def ple_proj(l, hf):
                    u = U0[f"pp{l}"]
                    if hf == 0:
                        act.wait_ge(tile0_done, TM[f"pp{l}"])
                    else:
                        act.wait_ge(weights_used, u + 1)
                    for t in range(T):
                        act.activation(pp[:, t, hf * HALF:(hf + 1) * HALF], ps[:, PP_BANK[l][hf] + t, :], ACT.Copy)\
                            .then_inc(pp_ready, 1)

                def res_done(name, u, t, hf):
                    if 2 * t + hf < 3:
                        act.wait_ge(bank_done, 3 * RES_ORDER.index(name) + 2 * t + hf + 1)
                    else:
                        act.wait_ge(weights_used, u + 1)

                def gate(l):
                    for t in range(T):
                        act.wait_ge(rstd_ready, 2 * (2 + 3 * l) + t + 1)
                        for hf in range(2):
                            res_done(f"gate{l}", U0[f"gate{l}"] + 3, t, hf)
                            c = 2 * (2 + 3 * l) + t
                            act.activation(xn[:, t, hf * HALF:(hf + 1) * HALF], ps[:, 2 * t + hf, :], ACT.Sigmoid,
                                           scale=rstd[:, c:c + 1]).then_inc(gate_ready, 1)

                def ffn(l):
                    u0 = U0[f"ffn{l}"]

                    def mid(it, gv, buf, i=None):
                        act.wait_ge(scaled[l], at(2 * it + gv + 1, 2 * FFN_TURN, i))
                        for j in range(2):
                            m = column(2 * it + j + FT * gv, i)
                            ins = act.activation(cgv[:, buf, gv, j * SEQ:(j + 1) * SEQ], usc[:, buf, gv, j * SEQ:(j + 1) * SEQ],
                                                 ACT.Identity, scale=cwT[:, l, 1, m], bias=cwT[:, l, 3, m])
                        ins.then_inc(mid_ready[l], 1)

                    def silu(buf, wait):
                        act.wait_ge(conv_done[l], wait)
                        act.activation(sgl[:, buf, :], cgv[:, buf, 0, :], ACT.Silu).then_inc(silu_ready[l], 1)

                    def hidden_hi(buf, wait):
                        act.wait_ge(hid_ready[l], wait)
                        act.activation(ohi[:, 2 * buf:2 * buf + 2, :].rearrange("p a c -> p (a c)"), hid[:, buf, :],
                                       ACT.Copy).then_inc(hhi_ready[l], 1)

                    def iteration(it, i=None, ug=None, after=None):
                        buf = it % 2
                        ug = u0 + 3 * it - 1 if ug is None else ug
                        for gv in range(2):
                            keep_ahead(ug + gv, i)
                            mid(it, gv, buf, i)
                        silu(buf, at(2 * it + 1, 2 * FFN_TURN, i))
                        if after is None:
                            keep_ahead(ug + 2, i)
                        else:
                            act.wait_ge(weights_used, after)
                        hidden_hi(buf, at(it + 1, FFN_TURN, i))

                    ahead(u0)
                    rms_row(l)
                    preload(2 * l, ACT.Silu)
                    mid(0, 0, 0)
                    ahead(u0 + 1)
                    mid(0, 1, 0)
                    silu(0, 1)
                    hidden_hi(0, 1)
                    with act.Fori(0, 8 // FFN_TURN) as i:
                        for n in range(FFN_TURN):
                            iteration(1 + n, i)
                    split[0] = u0 + 25 + RING
                    iteration(9, None, u0 + 26)
                    iteration(10, None, u0 + 28, u0 + 31)
                    ahead(u0 + 30)
                    ahead(u0 + 31)

                def block_exp(lset, s, nm, es, base):
                    act.wait_ge(max_ready, S_AT[lset] + s + 1)
                    for j in range(2):
                        ins = act.activation(Eb[:, s % 2, j, :], ps[:, base + j, 0:SEQ], ACT.Exp,
                                             bias=nm[:, j:j + 1], scale=1.0, accum_out=es[:, j:j + 1])
                    ins.then_inc(exp_ready, 1)

                def o_copy0(st, s):
                    qt, i = BLOCKS[s]
                    b = 8 * st + s
                    act.wait_ge(o_ready, b + 1)
                    c = (4 * st + i) * P
                    act.activation(junk, ps[:, OB, 0:P], ACT.Square, scale=rsum[:, b, 0:1],
                                   accum_out=oss[:, st, qt, i:i + 1])
                    act.activation(xn[:, qt, c:c + P], ps[:, OB, 0:P], ACT.Identity, scale=rsum[:, b, 0:1])\
                        .then_inc(o_read, 1)

                act.wait_ge(gain0_ready, 1)
                norm_hi(0)
                ahead(-1)
                norm_sumsq(0)
                act.wait_ge(trig_arg, 1)
                act.activation(trg[:, 0, :], trg[:, 0, :], ACT.Sin).then_inc(trig_ready, 1)
                act.wait_ge(lam_sums, 1)
                act.activation(lam2, lam2, ACT.Exp).then_inc(lam_exps, 1)
                u = U0["qkv0"]
                ahead(u)
                ahead(u + 1)
                ahead(u + 2)
                for b in range(2):
                    act.wait_ge(pT_ready, b + 1)
                    act.activation(phi[:, 2 * b:2 * b + 2, :].rearrange("p a c -> p (a c)"), ps[:, 6 + b, :], ACT.Copy)\
                        .then_inc(phi_ready, 1)
                ahead(u + 3)

                def copy_qk(dst, tiles, t, scale):
                    copy_T(dst[:, tiles, t * P:(t + 1) * P], ps[:, TB, :].rearrange("p (a c) -> p a c", c=P)[:, 0:tiles.stop - tiles.start, :], scale)

                def v_copy(c, name, u, banks):
                    for t in range(T):
                        tile_done(name, u, t)
                        act.activation(vtm[:, t, c:c + HALF], ps[:, banks + t, :], ACT.Copy, scale=rstd[:, t:t + 1])\
                            .then_inc(v_ready, 1)

                for t in range(T):
                    copy_qk(qT, slice(0, 4), t, 0.125)
                ahead(u + 4)
                for t in range(T):
                    copy_qk(kT, slice(0, 4), t, 1.0)
                ahead(u + 5)
                act.wait_ge(rstd_ready, 2)
                v_copy(0, "qkv0.2", u + 5, 0)

                def at_copy0(s):
                    copy_T(ATd[:, s % 2].rearrange("p k c -> p (k c)"), ps[:, TB, 0:2 * P])

                def o_hi(first, nt, count, qt, scaled):
                    act.wait_ge(oT_ready, count + 1)
                    src = ps[:, TB, 0:nt * P].rearrange("p (a c) -> p a c", c=P)
                    dst = ohi[:, first:first + nt, qt * P:(qt + 1) * P]
                    if scaled:
                        act.activation(dst, src, ACT.Identity, scale=subg).then_inc(ohi_ready, 1)
                    else:
                        act.activation(dst, src, ACT.Copy).then_inc(ohi_ready, 1)

                for s in range(N_A):
                    block_exp("A", s, nmax[:, s], esum[:, s], 6)
                    if s:
                        at_copy0(s - 1)
                    split_half()
                    if s:
                        o_copy0(0, s - 1)
                    if s in (5, 6):
                        copy_qk(qT, slice(4, 8), s - 5, 0.125)
                    if s == 6:
                        o_hi(0, 4, 0, 0, True)
                at_copy0(N_A - 1)
                split_half()
                o_copy0(0, N_A - 1)
                copy_qk(kT, slice(4, 8), 0, 1.0)
                split_half()
                copy_qk(kT, slice(4, 8), 1, 1.0)
                o_hi(0, 4, 1, 1, True)
                v_copy(HALF, "qkv0.5", u + 11, 2)
                for s in range(N_A):
                    if s:
                        at_copy0(s - 1)
                    block_exp("B", s, nmax[:, 8 + s], esum[:, 8 + s], 6)
                    if s < 6:
                        split_half()
                    if s == 2:
                        ple_proj(0, 0)
                    if s == 7:
                        o_hi(4, 4, 2, 0, True)
                    if s:
                        o_copy0(1, s - 1)
                    if s == 3:
                        ple_proj(0, 1)
                at_copy0(N_A - 1)
                o_copy0(1, N_A - 1)
                split_half()
                o_hi(4, 4, 3, 1, True)
                ahead(U0["wo0"] + 2)
                norm_hi(1)
                norm_sumsq(1)
                ahead(U0["wo0"] + 3)
                ffn(0)
                norm_hi(2)
                norm_sumsq(2)
                ahead(U0["ffn0"] + 32)
                preload(1, ACT.Sigmoid)
                for j in range(3):
                    ahead(U0["gate0"] + j)
                gate(0)

                norm_hi(3)
                norm_sumsq(3)
                u = U0["qkv1"]
                for j in (-1, 0, 1):
                    ahead(u + j)
                preload(5, ACT.Exp)
                for t in range(T):
                    copy_qk(kT, slice(0, 2), t, 1.0)
                ahead(u + 2)
                for t in range(T):
                    copy_qk(qT, slice(0, 4), t, 0.125)
                ahead(u + 3)

                def swa_exp(s):
                    act.wait_ge(max_ready, S_AT["1"] + s + 1)
                    for j in range(2):
                        ins = act.activation(Eb[:, s % 2, j, :], ps[:, 6 + s % 2, j * SEQ:(j + 1) * SEQ], ACT.Exp,
                                             bias=nmax1[:, s, j:j + 1], scale=1.0, accum_out=esum1[:, s, j:j + 1])
                    ins.then_inc(exp_ready, 1)
                    act.wait_ge(sinkarg_ready, s + 1)
                    act.activation(sinkd[:, s], sinkd[:, s], ACT.Exp).then_inc(sinkexp_ready, 1)

                swa_exp(0)
                for s in range(2 * N_A):
                    if s + 1 < 2 * N_A:
                        swa_exp(s + 1)
                    copy_T(ATs[:, s % 2].rearrange("p k c -> p (k c)"), ps[:, TB, :])
                    if s in (5, 9, 13):
                        o_hi(*((0, 4, 4, 0), (0, 4, 5, 1), (4, 4, 6, 0))[(s - 5) // 4], False)
                    if s in (5, 6):
                        copy_qk(qT, slice(4, 8), s - 5, 0.125)
                    if s == 7:
                        ple_proj(1, 0)
                    if s == 9:
                        ple_proj(1, 1)
                    if s in (0, 1, 2, 3, 4, 6, 10, 11, 15):
                        split_half()
                o_hi(4, 4, 7, 1, False)
                ahead(U0["wo1"] + 2)
                act.dma_start(gmid, final_norm.partition_broadcast(P)).then_inc(gmid_loaded, 16)
                norm_hi(4)
                norm_sumsq(4)
                ahead(U0["wo1"] + 3)
                ffn(1)
                norm_hi(5)
                norm_sumsq(5)
                ahead(U0["ffn1"] + 32)
                preload(3, ACT.Sigmoid)
                for j in range(3):
                    ahead(U0["gate1"] + j)
                gate(1)

                norm_hi(6)
                norm_sumsq(6)
                for t in range(T):
                    act.wait_ge(hg_ready, t + 1)
                    act.wait_ge(sumsq_ready, 13 + t)
                    act.activation(xn[:, t, :], hg[:, t, :], ACT.Square, accum_out=ssg[:, t:t + 1]).then_inc(sumsqg_ready, 1)
                for j in (-1, 0, 1):
                    ahead(U0["in2"] + j)
                rms_row(2)

                def sb_sigmoids(s):
                    pr, qt = SB_BLOCKS[s]
                    nk = P * (qt + 1)
                    act.wait_ge(s_ready, S_AT["S"] + s + 1)
                    for buf, sign in ((sbm, -1.0), (sbp, 1.0)):
                        ins = act.activation(buf[:, 0:2 * nk].rearrange("p (j c) -> p j c", j=2), ps[:, 6:8, 0:nk],
                                             ACT.Sigmoid, scale=sign)
                    ins.then_inc(sb_l, 1)

                def sb_copy(s):
                    pr, qt = SB_BLOCKS[s]
                    n = 2 * (qt + 1) * P
                    copy_T(ETs[:, 0:n], ps[:, TB, 0:n])

                def dil_exp(s):
                    j, qt = DIL_BLOCKS[s]
                    n = 3 * (qt + 1) * P
                    act.wait_ge(max_ready, MAX2 + s + 1)
                    act.activation(dlL[:, s % 2, 0:n], dlL[:, s % 2, 0:n], ACT.Exp, bias=nmax2[:, s:s + 1], scale=1.0,
                                   accum_out=esum2[:, s:s + 1]).then_inc(exp_ready, 1)

                def dil_copy(s):
                    j, qt = DIL_BLOCKS[s]
                    if qt:
                        copy_T(ETb[:, 0:HALF], ps[:, TB, :])
                        copy_T(ETb[:, HALF:HALF + 256], ps[:, TB, 0:256])
                    else:
                        copy_T(ETb[:, 0:3 * P], ps[:, TB, 0:3 * P])

                def gates(v, m0):
                    for m in range(8):
                        c = V_BGATE + m0 + m
                        ins = act.activation(v[:, m, :], v[:, m, :], ACT.Sigmoid, bias=vecT[:, c:c + 1], scale=1.0)
                        if m % 2:
                            ins.then_inc(gates_ready, 1)

                MAX2 = 32
                for n in range(1, 5):
                    ahead(IN2[n][2])
                for s in range(9):
                    if s:
                        sb_copy(s - 1)
                    if s < 8:
                        sb_sigmoids(s)
                    if s == 7:
                        o_hi(0, 4, 8, 0, False)
                    ahead(IN2[5 + s][2])
                o_hi(0, 4, 9, 1, False)
                preload(4, ACT.Exp)
                for s in range(9):
                    if s:
                        dil_copy(s - 1)
                    if s < 8:
                        dil_exp(s)
                    if s == 7:
                        o_hi(4, 2, 10, 0, False)
                    ahead(U0["gl2"] + 1 + s)
                act.wait_ge(in2_read, in2_count[-1])
                gates(gb, 8)
                o_hi(4, 2, 11, 1, False)
                ahead(U0["dilup"])
                gates(ga, 0)
                for j in range(4):
                    act.wait_ge(merged, j + 1)
                    act.activation(xhi[:, 2 * j:2 * j + 2, :].rearrange("p a c -> p (a c)"), mB[:, j, :], ACT.Copy)\
                        .then_inc(mhi_ready, 1)
                for j in range(3):
                    ahead(U0["wout"] + j)
                act.wait_ge(mlo_ready, 4)
                act.dma_start(gfin, norm_final_g_2.partition_broadcast(P)).then_inc(gfin_loaded, 16)
                norm_hi(7)
                norm_sumsq(7)
                ahead(U0["wout"] + 3)
                ahead(U0["mlp"])
                u0 = U0["mlp"]

                def relu_hi(it, i=None):
                    b = it % 3
                    act.wait_ge(weights_used, at(u0 + 2 * it if it else u0 + 1, TURN, i))
                    act.activation(rel[:, b, :], ps[:, 4 + b, :], ACT.Relu).then_inc(relu_ready, 1)
                    act.wait_ge(relu_ready, at(it + 1, MLP_TURN, i))
                    act.activation(ohi[:, 2 * b:2 * b + 2, :].rearrange("p a c -> p (a c)"), rel[:, b, :], ACT.Square)\
                        .then_inc(rhi_ready, 1)

                def mlp_iteration(it, i=None):
                    keep_ahead(u0 + 2 * it - 1, i)
                    relu_hi(it, i)
                    keep_ahead(u0 + 2 * it, i)

                relu_hi(0)
                mlp_iteration(1)
                with act.Fori(0, 12 // MLP_TURN) as i:
                    for n in range(MLP_TURN):
                        mlp_iteration(2 + n, i)
                split[0] = u0 + 27 + RING - 1
                mlp_iteration(14)
                mlp_iteration(15)
                norm_sumsq(8)

            @block.vector
            def _(dve):
                split = [0]
                steps = [0]

                def settle(ins):
                    steps[0] += 1
                    ins.then_inc(dve_step, 1)
                    dve.wait_ge(dve_step, steps[0])

                def split_lo(u, i=None):
                    dve.wait_ge(hi_ready, at(u + 1, TURN, i))
                    dve.tensor_tensor(wlo[:, u % RING, :], raw[:, u % RAW, :], whi[:, u % RING, :].bitcast(F32),
                                      ALU.subtract).then_inc(lo_ready, 1)

                half, halved = [0], [0]

                def split_half(count=1):
                    for _ in range(count):
                        u, a = split[0], half[0]
                        cols = slice(a * UNIT // 2, (a + 1) * UNIT // 2)
                        if a:
                            dve.wait_ge(hi_ready, u + 1)
                        else:
                            halved[0] += 1
                            dve.wait_ge(hi_half, halved[0])
                        ins = dve.tensor_tensor(wlo[:, u % RING, cols], raw[:, u % RAW, cols], whi[:, u % RING, cols].bitcast(F32),
                                                ALU.subtract)
                        if a:
                            ins.then_inc(lo_ready, 1)
                        split[0] += a
                        half[0] = 1 - a

                def ahead(u):
                    if half[0]:
                        split_half()
                    while split[0] < min(u + RING, NU):
                        split_lo(split[0])
                        split[0] += 1

                def keep_ahead(u, i):
                    if i is None:
                        ahead(u)
                    else:
                        split_lo(u + RING - 1, i)

                def tile_done(name, u, t):
                    if t == 0:
                        dve.wait_ge(tile0_done, TM[name])
                    else:
                        dve.wait_ge(weights_used, u + 1)

                def res_done(name, u, t, hf):
                    if 2 * t + hf < 3:
                        dve.wait_ge(bank_done, 3 * RES_ORDER.index(name) + 2 * t + hf + 1)
                    else:
                        dve.wait_ge(weights_used, u + 1)

                def residual(name, u, t, hf):
                    res_done(name, u, t, hf)
                    v = h[:, t, hf * HALF:(hf + 1) * HALF]
                    dve.tensor_tensor(v, ps[:, 2 * t + hf, :], v, ALU.add).then_inc(h_ready, 1)

                def norm_lo(n, t, hf):
                    for b in (2 * hf, 2 * hf + 1):
                        dve.wait_ge(xhi_ready, 2 * KD * n + KD * t + 2 * b + 2)
                        for k in (2 * b, 2 * b + 1):
                            g = GAIN[n] + k
                            c = (k % 2) * SEQ + t * P
                            dve.scalar_tensor_tensor(xlo[:, k, t * P:(t + 1) * P], ps[:, 4 + b, c:c + P], vecT[:, g:g + 1],
                                                     xhi[:, k, t * P:(t + 1) * P].bitcast(F32), ALU.mult, ALU.subtract)\
                                .then_inc(xlo_ready, 1)

                def boundary(add, n):
                    add(0, 0)
                    add(0, 1)
                    norm_lo(n, 0, 0)
                    add(1, 0)
                    norm_lo(n, 0, 1)
                    add(1, 1)
                    norm_lo(n, 1, 0)
                    norm_lo(n, 1, 1)

                def rotary(n):
                    for t in range(T):
                        c = 2 * n + t
                        dve.wait_ge(rstd_ready, c + 1)
                        dve.tensor_scalar(cosr[:, t, :], cosd[:, t, :], rstd[:, c:c + 1], None, ALU.mult)
                        ins = dve.tensor_scalar(sinr[:, t, :], sind[:, t, :], rstd[:, c:c + 1], None, ALU.mult)
                    settle(ins)

                def rope_mul(c, t, name, u, bank, heads):
                    w = heads * HD
                    tile_done(name, u, t)
                    if c:
                        dve.wait_ge(t_ready, ROPE_T[c - 1] + t + 1)
                    src = ps[:, bank + t, 0:w]
                    n = 1 if heads == 4 or name[3] == "0" else 2
                    i = heads // n
                    per_head = lambda v: v.rearrange("p (a i d) -> p a i d", a=n, d=HD)
                    paired = lambda v: v.rearrange("p (i a d) -> p a i d", a=n, d=HD)
                    wide = lambda v: v.unsqueeze(1).unsqueeze(1).broadcast_to([P, n, i, v.shape[-1]])
                    dve.tensor_tensor(paired(rotA[:, t, 0:w]), per_head(src), wide(cosr[:, t, :]), ALU.mult)
                    for hf in range(2):
                        a = hf * HD // 2
                        b = HD // 2 - a
                        ins = dve.tensor_tensor(paired(rotB[:, t, 0:w])[:, :, :, a:a + HD // 2],
                                                per_head(src)[:, :, :, b:b + HD // 2],
                                                wide(sinr[:, t, a:a + HD // 2]), ALU.mult)
                    if name == "qkv1.0":
                        ins = dve.tensor_scalar(vtm[:, t, 0:256], ps[:, bank + t, 256:512], rstd[:, 6 + t:7 + t], None, ALU.mult)
                    ins.then_inc(rope_read, 1)

                ROPE_T = [T_USE[n] for n in ("0q00", "0k00", "0q10", "0k10", "1k0", "1q00", "1q10")]

                def gate(l, t, hf):
                    cols = slice(hf * HALF, (hf + 1) * HALF)
                    if 2 * t + hf < 3:
                        dve.wait_ge(prodp_ready, 3 * l + 2 * t + hf + 1)
                    else:
                        dve.wait_ge(gate_ready, 4 * l + 4)
                        dve.tensor_tensor(xn[:, t, cols], xn[:, t, cols], pp[:, t, cols], ALU.mult).then_inc(prod_ready, 1)
                        dve.wait_ge(prod_ready, l + 1)
                    dve.tensor_tensor(h[:, t, cols], h[:, t, cols], xn[:, t, cols], ALU.add).then_inc(h_ready, 1)

                def ffn(l):
                    u0 = U0[f"ffn{l}"]

                    def taps(it, gv, i=None, ug=None):
                        buf = it % 2
                        bank = 4 + 2 * buf + gv
                        ug = u0 if ug is None else ug
                        dve.wait_ge(weights_used, at(ug + gv + 1, TURN, i))
                        dve.tensor_tensor(usc[:, buf, gv, :].rearrange("p (j c) -> p j c", j=2),
                                          ps[:, bank, :].rearrange("p (j c) -> p j c", j=2),
                                          rB[:, :].unsqueeze(1).broadcast_to([P, 2, SEQ]), ALU.mult).then_inc(scaled[l], 1)
                        dve.wait_ge(mid_ready[l], at(2 * it + gv + 1, 2 * FFN_TURN, i))
                        for j in range(2):
                            o = j * SEQ
                            m = column(2 * it + j + FT * gv, i)
                            v = cgv[:, buf, gv, o + 1:o + SEQ]
                            dve.scalar_tensor_tensor(v, usc[:, buf, gv, o:o + SEQ - 1], cwT[:, l, 0, m], v,
                                                     ALU.mult, ALU.add).then_inc(tap_done[l], 1)
                        for j in range(2):
                            o = j * SEQ
                            m = column(2 * it + j + FT * gv, i)
                            dve.wait_ge(tap_done[l], at(4 * it + 2 * gv + j + 1, 4 * FFN_TURN, i))
                            v = cgv[:, buf, gv, o:o + SEQ - 1]
                            ins = dve.scalar_tensor_tensor(v, usc[:, buf, gv, o + 1:o + SEQ], cwT[:, l, 2, m], v,
                                                           ALU.mult, ALU.add)
                        ins.then_inc(conv_done[l], 1)

                    def mult(buf, conv, n):
                        dve.wait_ge(conv_done[l], conv)
                        dve.wait_ge(silu_ready[l], n)
                        dve.tensor_tensor(hid[:, buf, :], sgl[:, buf, :], cgv[:, buf, 1, :], ALU.mult).then_inc(hid_ready[l], 1)

                    def hidden_lo(buf, n):
                        dve.wait_ge(hhi_ready[l], n)
                        dve.tensor_tensor(olo[:, 2 * buf:2 * buf + 2, :].rearrange("p a c -> p (a c)"), hid[:, buf, :],
                                          ohi[:, 2 * buf:2 * buf + 2, :].rearrange("p a c -> p (a c)").bitcast(F32),
                                          ALU.subtract).then_inc(hlo_ready[l], 1)

                    def iteration(it, i=None, ug=None):
                        buf = it % 2
                        straight = ug is not None
                        ug = ug if straight else u0 + 3 * it - 1
                        for gv in range(2):
                            keep_ahead(ug + gv, i)
                            taps(it, gv, i, ug)
                        mult(buf, at(2 * it + 2, 2 * FFN_TURN, i), at(it + 1, FFN_TURN, i))
                        if not straight:
                            keep_ahead(ug + 2, i)
                        hidden_lo(buf, at(it + 1, FFN_TURN, i))

                    ahead(u0)
                    dve.wait_ge(rB_ready, l + 1)
                    taps(0, 0)
                    ahead(u0 + 1)
                    taps(0, 1)
                    mult(0, 2, 1)
                    hidden_lo(0, 1)
                    with dve.Fori(0, 8 // FFN_TURN) as i:
                        for n in range(FFN_TURN):
                            iteration(1 + n, i)
                    split[0] = u0 + 25 + RING
                    iteration(9, None, u0 + 26)
                    iteration(10, None, u0 + 28)
                    ahead(u0 + 30)
                    ahead(u0 + 31)

                def block_max(lset, s, nm, base):
                    dve.wait_ge(s_ready, S_AT[lset] + s + 1)
                    dve.tensor_reduce(nm, ps[:, base:base + 2, 0:SEQ], AX.X, ALU.max, negate=True).then_inc(max_ready, 1)

                def block_mix(s):
                    dve.wait_ge(exp_ready, s + 1)
                    settle(dve.reciprocal(rsum[:, s], esum[:, s]))
                    settle(dve.scalar_tensor_tensor(mixc[:, s:s + 1], esum[:, s, 0:1], nlam, rsum[:, s, 1:2], ALU.mult, ALU.mult))
                    dve.scalar_tensor_tensor(Ac[:, s % 2, :], Eb[:, s % 2, 1, :], mixc[:, s:s + 1], Eb[:, s % 2, 0, :],
                                             ALU.mult, ALU.add).then_inc(mix_ready, 1)

                def o_norm(st, qt):
                    dve.wait_ge(orstd_ready, 2 * st + qt + 1)
                    v = xn[:, qt, st * HALF:(st + 1) * HALF].rearrange("p (d e) -> p d e", e=P)
                    dve.tensor_tensor(v, v, ors[:, st, qt, :].unsqueeze(2).broadcast_to([P, 4, P]), ALU.mult).then_inc(on_ready, 1)

                def o_lo(first, nt, count, qt, scaled):
                    dve.wait_ge(ohi_ready, count + 1)
                    src = ps[:, TB, 0:nt * P].rearrange("p (a c) -> p a c", c=P)
                    dst = olo[:, first:first + nt, qt * P:(qt + 1) * P]
                    hi = ohi[:, first:first + nt, qt * P:(qt + 1) * P].bitcast(F32)
                    if scaled:
                        dve.scalar_tensor_tensor(dst, src, subg, hi, ALU.mult, ALU.subtract).then_inc(olo_ready, 1)
                    else:
                        dve.tensor_tensor(dst, src, hi, ALU.subtract).then_inc(olo_ready, 1)

                dve.wait_ge(gain0_T, 1)
                dve.tensor_copy(vecT[:, V_ATTN:V_ATTN + 16], ps[:, 0, 0:16]).then_inc(gain0_ready, 1)
                dve.wait_ge(gain0_ready, 1)
                for t in range(T):
                    for hf in range(2):
                        norm_lo(0, t, hf)
                ahead(-2)

                ang = trg[:, 1, 0:2 * HD // 2].rearrange("p (t f) -> p t f", t=T)
                turns = trg[:, 2, :]
                both = trg[:, 0, :].rearrange("p (a t f) -> p a t f", a=2, t=T)
                dve.wait_ge(table_loaded, 16)
                dve.wait_ge(trig_loaded, 16 * 3)
                settle(dve.tensor_copy(posf, posi[:, :]))
                for t in range(T):
                    ins = dve.tensor_scalar(ang[:, t, :], tab[:, C_FREQ:C_FREQ + HD // 2], posf[:, t:t + 1], None, ALU.mult)
                settle(ins)
                flat = ang.rearrange("p t f -> p (t f)")
                MAGIC = 1.5 * 2.0 ** 23
                pieces = (6.28125, 0.0019350051879882812, 2 * math.pi - 6.28125 - 0.0019350051879882812)
                for a in range(2):
                    arg = trg[:, 0, a * HD:(a + 1) * HD]
                    settle(dve.tensor_scalar(turns[:, 0:HD], flat, 1.0 / (2 * math.pi), 0.25 * a, ALU.mult, ALU.add))
                    settle(dve.tensor_scalar(turns[:, 0:HD], turns[:, 0:HD], MAGIC, None, ALU.add))
                    settle(dve.tensor_scalar(turns[:, 0:HD], turns[:, 0:HD], MAGIC, None, ALU.subtract))
                    src = flat
                    for c in pieces:
                        settle(dve.scalar_tensor_tensor(arg, turns[:, 0:HD], -c, src, ALU.mult, ALU.add))
                        src = arg
                    if a:
                        settle(dve.tensor_scalar(arg, arg, math.pi / 2, None, ALU.add))
                    settle(dve.tensor_scalar(arg, arg, 3.1415925, -3.1415925, ALU.min, ALU.max))
                dve.tensor_copy(turns[:, 0:2], posf).then_inc(trig_arg, 1)
                settle(dve.tensor_tensor(trg[:, 3, :].rearrange("p (a d) -> p a d", a=2), lamb[:, 0::2, :], lamb[:, 1::2, :], ALU.mult))
                dve.tensor_reduce(lam2, trg[:, 3, :].rearrange("p (a d) -> p a d", a=2), AX.X, ALU.add).then_inc(lam_sums, 1)
                dve.tensor_scalar(nsink, sinks[:, :], -1.0, None, ALU.mult)
                ahead(-1)
                ahead(0)
                dve.wait_ge(trig_ready, 1)
                for t in range(T):
                    for a in range(2):
                        dve.tensor_copy(cosd[:, t, a * 32:a * 32 + 32], both[:, 1, t, :])
                        ins = dve.tensor_scalar(sind[:, t, a * 32:a * 32 + 32], both[:, 0, t, :], (-1.0, 1.0)[a], None, ALU.mult)
                settle(ins)
                dve.wait_ge(lam_exps, 1)
                settle(dve.scalar_tensor_tensor(nlam, lam2[:, 1:2], -LAM_INIT, lam2[:, 0:1], ALU.add, ALU.subtract))

                rotary(0)

                u = U0["qkv0"]
                ahead(u + 1)
                for t in range(T):
                    rope_mul(0, t, "qkv0.0", u + 1, 0, 8)
                dve.tensor_copy(identb[:, :], ident)
                dve.tensor_copy(maskb[:, :, :].rearrange("p a c -> p (a c)"), tab[:, C_SWA:C_SWA + 2 * P])
                dve.wait_ge(vecs_T, 1)
                dve.tensor_copy(vecT[:, 0:V_ROWS], ps[:, 5, 0:V_ROWS])
                for l in range(2):
                    for a in range(2):
                        c = 80 + (2 * l + a) * 4 * FT
                        ins = dve.tensor_copy(cwT[:, l, 2 * a:2 * a + 2, :].rearrange("p a m -> p (a m)"), ps[:, 5, c:c + 4 * FT])
                settle(ins)
                dve.tensor_tensor(vecT[:, V_MIX:V_MIX + KD], vecT[:, V_MID:V_MID + KD], vecT[:, V_MIXG:V_MIXG + KD], ALU.mult)
                dve.tensor_scalar(subg, vecT[:, V_SUBLN:V_SUBLN + 1], 1.0 - LAM_INIT, None, ALU.mult).then_inc(vecs_ready, 1)
                ahead(u + 2)
                for b in range(2):
                    dve.wait_ge(phi_ready, b + 1)
                    dve.tensor_tensor(plo[:, 2 * b:2 * b + 2, :].rearrange("p a c -> p (a c)"), ps[:, 6 + b, :],
                                      phi[:, 2 * b:2 * b + 2, :].rearrange("p a c -> p (a c)").bitcast(F32), ALU.subtract)\
                        .then_inc(plo_ready, 1)
                ahead(u + 3)
                for t in range(T):
                    rope_mul(1, t, "qkv0.1", u + 3, 2, 8)
                ahead(u + 4)
                ahead(u + 5)
                for s in range(N_A + 1):
                    if s:
                        block_mix(s - 1)
                    if s == N_A:
                        break
                    block_max("A", s, nmax[:, s], 6)
                    if s:
                        split_half()
                    if s in (3, 4):
                        rope_mul(2, s - 3, "qkv0.3", u + 7, 2, 8)
                    if s == 5:
                        o_norm(0, 0)
                    if s == 6:
                        o_lo(0, 4, 0, 0, True)
                rope_mul(3, 0, "qkv0.4", u + 9, 0, 8)
                split_half()
                rope_mul(3, 1, "qkv0.4", u + 9, 0, 8)
                o_norm(0, 1)
                split_half(2)
                o_lo(0, 4, 1, 1, True)
                for s in range(N_A + 1):
                    if s:
                        block_mix(8 + s - 1)
                    if s == N_A:
                        break
                    block_max("B", s, nmax[:, 8 + s], 6)
                    if s in range(1, 7):
                        split_half()
                    if s == 6:
                        o_norm(1, 0)
                    if s == 7:
                        o_lo(4, 4, 2, 0, True)
                split_half()
                o_norm(1, 1)
                o_lo(4, 4, 3, 1, True)
                ahead(U0["wo0"] + 2)
                boundary(lambda t, hf: residual("wo0", U0["wo0"] + 3, t, hf), 1)
                ahead(U0["wo0"] + 3)
                ffn(0)
                boundary(lambda t, hf: residual("ffn0", U0["ffn0"] + 32, t, hf), 2)
                ahead(U0["ffn0"] + 32)
                for j in range(3):
                    ahead(U0["gate0"] + j)
                boundary(lambda t, hf: gate(0, t, hf), 3)

                u = U0["qkv1"]
                ahead(u - 1)
                rotary(3)
                ahead(u)
                for t in range(T):
                    rope_mul(4, t, "qkv1.0", u + 1, 0, 4)
                ahead(u + 1)
                ahead(u + 2)
                for t in range(T):
                    rope_mul(5, t, "qkv1.1", u + 3, 2, 8)
                ahead(u + 3)

                def swa_max(s):
                    g, qt, r, i = SWA_BLOCKS[s]
                    hd = 8 * g + 4 * r + i
                    dve.wait_ge(s_ready, S_AT["1"] + s + 1)
                    sc = ps[:, 6 + s % 2, :].rearrange("p (j c) -> p j c", j=2)
                    settle(dve.tensor_reduce(nmax1[:, s], sc, AX.X, ALU.max, negate=True))
                    dve.tensor_tensor(nmax1[:, s], nmax1[:, s], nsink[:, hd:hd + 2], ALU.min).then_inc(max_ready, 1)

                def swa_out(s):
                    g, qt, r, i = SWA_BLOCKS[s]
                    c = (8 * g + 4 * r + i) * HD
                    dve.wait_ge(o_ready, S_AT["1"] + s + 1)
                    dve.wait_ge(sum_ready, s + 1)
                    dve.tensor_tensor(xn[:, qt, c:c + 2 * HD].rearrange("p (a d) -> p a d", d=HD),
                                      ps[:, OB, 0:2 * HD].rearrange("p (a d) -> p a d", d=HD),
                                      rsum1[:, s].unsqueeze(2).broadcast_to([P, 2, HD]), ALU.mult).then_inc(o_read, 1)

                swa_max(0)
                for s in range(2 * N_A):
                    if s + 1 < 2 * N_A:
                        swa_max(s + 1)
                    if s in (1, 2, 3, 4, 5, 7, 11, 12):
                        split_half()
                    if s:
                        swa_out(s - 1)
                    if s in (5, 9, 13):
                        o_lo(*((0, 4, 4, 0), (0, 4, 5, 1), (4, 4, 6, 0))[(s - 5) // 4], False)
                    if s in (2, 4):
                        rope_mul(6, s // 2 - 1, "qkv1.2", U0["qkv1"] + 5, 0, 8)
                split_half()
                swa_out(2 * N_A - 1)
                o_lo(4, 4, 7, 1, False)
                ahead(U0["wo1"] + 2)
                boundary(lambda t, hf: residual("wo1", U0["wo1"] + 3, t, hf), 4)
                ahead(U0["wo1"] + 3)
                ffn(1)
                boundary(lambda t, hf: residual("ffn1", U0["ffn1"] + 32, t, hf), 5)
                ahead(U0["ffn1"] + 32)
                for j in range(3):
                    ahead(U0["gate1"] + j)
                boundary(lambda t, hf: gate(1, t, hf), 6)

                dve.wait_ge(gmid_loaded, 16)
                for t in range(T):
                    dve.wait_ge(h_ready, 22 + 2 * t)
                    dve.tensor_tensor(hg[:, t, :], h[:, t, :], gmid, ALU.mult).then_inc(hg_ready, 1)
                ahead(U0["in2"] - 1)
                for t in range(T):
                    c = 12 + t
                    dve.wait_ge(rstd_ready, c + 1)
                    dve.wait_ge(hg_ready, t + 1)
                    dve.tensor_scalar(h[:, t, :], hg[:, t, :], rstd[:, c:c + 1], None, ALU.mult).then_inc(h_final, 1)
                ahead(U0["in2"])
                ahead(U0["in2"] + 1)

                def in2_evac(n):
                    kind, j, u, nb = IN2[n]
                    bank = in2_bank[n]
                    if nb == 2:
                        w = 256 if kind == "va1" else HALF
                        dst, c0 = (vb, 0) if kind == "vb" else (va, HALF if kind == "va1" else 0)
                        ul = u if kind == "va1" else u + 1
                        for t in range(T):
                            tile_done("in2." + kind, ul, t)
                            dve.tensor_scalar(dst[:, t, c0:c0 + w], ps[:, bank + t, 0:w], rboth[:, t:t + 1], None, ALU.mult)\
                                .then_inc(in2_read, 1)
                        return
                    dve.wait_ge(weights_used, u + 1)
                    dst = {"qa": qTa, "ka": kTa, "qb": qTb, "kb": kTb}[kind] if kind != "gl" else ga if j < 4 else gb
                    row = rBq if kind[0] == "q" else rB
                    dve.tensor_tensor(dst[:, 2 * (j % 4):2 * (j % 4) + 2, :], ps[:, bank, :].rearrange("p (m c) -> p m c", m=2),
                                      row[:, :].unsqueeze(1).broadcast_to([P, 2, SEQ]), ALU.mult).then_inc(in2_read, 1)

                def sb_block(s):
                    pr, qt = SB_BLOCKS[s]
                    nk = P * (qt + 1)
                    dve.wait_ge(sb_sel, 2 * s + 2)
                    for j in range(2):
                        ins = dve.tensor_tensor_scan(sbc[:, j, SEQ - nk:SEQ][:, ::-1], sbm[:, j * nk:(j + 1) * nk][:, ::-1],
                                                     ones[:, 0:nk], 1.0, ALU.mult, ALU.mult)
                    settle(ins)
                    pair = lambda v: v[:, 0:2 * nk].rearrange("p (j c) -> p j c", j=2)
                    dve.tensor_tensor(pair(sba), pair(sbp), sbc[:, :, SEQ - nk + 1:SEQ + 1], ALU.mult).then_inc(mix_ready, 1)

                def sb_out(s):
                    pr, qt = SB_BLOCKS[s]
                    dve.wait_ge(o_ready, S_AT["S"] + s + 1)
                    dve.tensor_copy(xn[:, qt, 2 * pr * HD:(2 * pr + 2) * HD], ps[:, OB, 0:2 * HD]).then_inc(o_read, 1)

                def dil_max(s):
                    j, qt = DIL_BLOCKS[s]
                    nk = P * (qt + 1)
                    dve.wait_ge(s_ready, S_AT["D"] + s + 1)
                    for g in range(3):
                        c0 = C_DIL + (g + 1) * SEQ - nk
                        ins = dve.scalar_tensor_tensor(dlL[:, s % 2, g * nk:(g + 1) * nk], tab[:, c0:c0 + nk], -SLOPES[4 * g + j],
                                                       ps[:, 6 + g // 2, (g % 2) * nk:(g % 2 + 1) * nk], ALU.mult, ALU.add)
                    settle(ins)
                    dve.tensor_reduce(nmax2[:, s:s + 1], dlL[:, s % 2, 0:3 * nk], AX.X, ALU.max, negate=True).then_inc(max_ready, 1)

                def dil_sum(s):
                    dve.wait_ge(exp_ready, 32 + s + 1)
                    settle(dve.reciprocal(rsum2[:, s:s + 1], esum2[:, s:s + 1]))

                def dil_out(s):
                    j, qt = DIL_BLOCKS[s]
                    dve.wait_ge(o_ready, S_AT["D"] + s + 1)
                    dve.tensor_scalar(xn[:, qt, HALF + j * HD:HALF + (j + 1) * HD], ps[:, OB, 0:HD], rsum2[:, s:s + 1], None,
                                      ALU.mult).then_inc(o_read, 1)

                settle(dve.tensor_copy(sbc[:, :, SEQ:SEQ + 1], ones[:, 0:2].unsqueeze(2)))
                for t in range(T):
                    dve.wait_ge(rboth_ready, t + 1)
                in2_evac(0)
                dve.wait_ge(rB_ready, 4)
                for n in range(1, 5):
                    ahead(IN2[n][2])
                    in2_evac(n)
                for s in range(9):
                    if s < 8:
                        sb_block(s)
                    if s == 7:
                        o_lo(0, 4, 8, 0, False)
                    ahead(IN2[5 + s][2])
                    if s:
                        sb_out(s - 1)
                    in2_evac(5 + s)
                o_lo(0, 4, 9, 1, False)
                for s in range(9):
                    if s < 8:
                        dil_max(s)
                        dil_sum(s)
                    if s == 7:
                        o_lo(4, 2, 10, 0, False)
                    ahead(U0["gl2"] + 1 + s)
                    if s:
                        dil_out(s - 1)
                    if s < 7:
                        in2_evac(in2_at["gl1"] + s)
                for j in range(4):
                    if j % 2 == 0:
                        dve.wait_ge(weights_used, U0["sbup"] + j // 2 + 1)
                    if j == 2:
                        o_lo(4, 2, 11, 1, False)
                        ahead(U0["dilup"])
                    dve.wait_ge(gates_ready, j + 1)
                    dve.tensor_tensor(mB[:, j, :], ps[:, j, :], gb[:, 2 * j:2 * j + 2, :].rearrange("p a c -> p (a c)"), ALU.mult)
                for j in range(4):
                    if j < 3:
                        dve.wait_ge(dilup_done, j + 1)
                    else:
                        dve.wait_ge(weights_used, U0["dilup"] + 1)
                    dve.wait_ge(gates_ready, 4 + j + 1)
                    v = ga[:, 2 * j:2 * j + 2, :].rearrange("p a c -> p (a c)")
                    settle(dve.tensor_tensor(v, ps[:, 4 + j, :], v, ALU.mult))
                    dve.tensor_tensor(mB[:, j, :], mB[:, j, :], v, ALU.add).then_inc(merged, 1)
                    dve.wait_ge(mhi_ready, j + 1)
                    dve.tensor_tensor(xlo[:, 2 * j:2 * j + 2, :].rearrange("p a c -> p (a c)"), mB[:, j, :],
                                      xhi[:, 2 * j:2 * j + 2, :].rearrange("p a c -> p (a c)").bitcast(F32), ALU.subtract)\
                        .then_inc(mlo_ready, 1)
                for j in range(3):
                    ahead(U0["wout"] + j)
                boundary(lambda t, hf: residual("wout", U0["wout"] + 3, t, hf), 7)
                ahead(U0["wout"] + 3)
                ahead(U0["mlp"])
                u0 = U0["mlp"]

                def square_lo(it, i=None):
                    b, n = it % 3, at(it + 1, MLP_TURN, i)
                    dve.wait_ge(relu_ready, n)
                    dve.tensor_tensor(rsq[:, b, :], rel[:, b, :], rel[:, b, :], ALU.mult).then_inc(sq_ready, 1)
                    dve.wait_ge(sq_ready, n)
                    dve.wait_ge(rhi_ready, n)
                    dve.tensor_tensor(olo[:, 2 * b:2 * b + 2, :].rearrange("p a c -> p (a c)"), rsq[:, b, :],
                                      ohi[:, 2 * b:2 * b + 2, :].rearrange("p a c -> p (a c)").bitcast(F32),
                                      ALU.subtract).then_inc(rlo_ready, 1)

                def mlp_iteration(it, i=None):
                    keep_ahead(u0 + 2 * it - 1, i)
                    square_lo(it, i)
                    keep_ahead(u0 + 2 * it, i)

                square_lo(0)
                mlp_iteration(1)
                with dve.Fori(0, 12 // MLP_TURN) as i:
                    for n in range(MLP_TURN):
                        mlp_iteration(2 + n, i)
                split[0] = u0 + 27 + RING - 1
                mlp_iteration(14)
                mlp_iteration(15)
                for t in range(T):
                    dve.wait_ge(r2_ready, t + 1)
                    for hf in range(2):
                        res_done("mlp", u0 + 31, t, hf)
                        v = h[:, t, hf * HALF:(hf + 1) * HALF]
                        dve.scalar_tensor_tensor(v, ps[:, 2 * t + hf, :], r2[:, t:t + 1], v, ALU.mult, ALU.add).then_inc(h_ready, 1)
                dve.wait_ge(gfin_loaded, 16)
                for t in range(T):
                    c = 16 + t
                    dve.wait_ge(rstd_ready, c + 1)
                    dve.scalar_tensor_tensor(xn[:, t, :], h[:, t, :], rstd[:, c:c + 1], gfin, ALU.mult, ALU.mult)\
                        .then_inc(out_ready, 1)

            @block.tensor
            def _(pe):
                tuse = [0]

                def mm(o, l, r, start, stop):
                    return pe.matmul(o, l, r, start=start, stop=stop, skip_group_check=True)

                def slot(ring, u, kk):
                    return ring[:, u % RING, :].rearrange("p (k n) -> p k n", k=kk)

                def tm_half(u, t, hi, lo, kk, bank, start, stop, xwait=None, uwait=None, k0=0, wait=None):
                    n = UNIT // kk
                    w = min(n, HALF)
                    nb = n // w
                    wh, wl = slot(whi, u, kk), slot(wlo, u, kk)
                    if t == 0:
                        pe.wait_ge(lo_ready, u + 1 if uwait is None else uwait)
                    if wait:
                        pe.wait_ge(*wait)
                    for k in range(kk):
                        if xwait is not None:
                            pe.wait_ge(xlo_ready, xwait + KD * t + k + 1)
                        xh = hi[:, k0 + k, t * P:(t + 1) * P]
                        xl = lo[:, k0 + k, t * P:(t + 1) * P]
                        for b in range(nb):
                            mm(ps[:, bank + b, 0:w], xh, wh[:, k, b * w:(b + 1) * w], start and k == 0, False)
                        for b in range(nb):
                            mm(ps[:, bank + b, 0:w], xh, wl[:, k, b * w:(b + 1) * w], False, False)
                        for b in range(nb):
                            ins = mm(ps[:, bank + b, 0:w], xl, wh[:, k, b * w:(b + 1) * w], False, stop and k == kk - 1)
                    if t == 1:
                        ins.then_inc(weights_used, 1)
                    elif stop:
                        ins.then_inc(tile0_done, 1)

                def fm_half(u, m, hi, lo, kk, bank, xwait=None, uwait=None, k0=0, last=1, signal=None):
                    wh, wl = slot(whi, u, kk), slot(wlo, u, kk)
                    if m == 0:
                        pe.wait_ge(lo_ready, u + 1 if uwait is None else uwait)
                    o = ps[:, bank, (m % 2) * SEQ:(m % 2 + 1) * SEQ]
                    for k in range(kk):
                        if xwait is not None and m == 0:
                            pe.wait_ge(xlo_ready, xwait + KD + max(k + 1, 2))
                        mm(o, wh[:, k, m * P:(m + 1) * P], hi[:, k0 + k, :], k == 0, False)
                        mm(o, wh[:, k, m * P:(m + 1) * P], lo[:, k0 + k, :], False, False)
                        ins = mm(o, wl[:, k, m * P:(m + 1) * P], hi[:, k0 + k, :], False, k == kk - 1)
                    if m == last:
                        ins.then_inc(weights_used, 1)
                    elif signal is not None:
                        ins.then_inc(signal, 1)

                def row_piece(u, t, b, hi, lo, kk, bank, c0, w, start, stop, k0=0, signal=None):
                    wh, wl = slot(whi, u, kk), slot(wlo, u, kk)
                    if t + b == 0:
                        pe.wait_ge(lo_ready, u + 1)
                    for k in range(kk):
                        xh = hi[:, k0 + k, t * P:(t + 1) * P]
                        xl = lo[:, k0 + k, t * P:(t + 1) * P]
                        mm(ps[:, bank, 0:w], xh, wh[:, k, c0:c0 + w], start and k == 0, False)
                        mm(ps[:, bank, 0:w], xh, wl[:, k, c0:c0 + w], False, False)
                        ins = mm(ps[:, bank, 0:w], xl, wh[:, k, c0:c0 + w], False, stop and k == kk - 1)
                    if signal is not None:
                        ins.then_inc(signal, 1)

                def norm_T(n, t, hf):
                    if n == 0:
                        pe.wait_ge(h_loaded[t], 16)
                    else:
                        pe.wait_ge(h_ready, 4 * (n - 1) + 2 * t + hf + 1)
                    for b in (2 * hf, 2 * hf + 1):
                        if t:
                            pe.wait_ge(xlo_ready, 2 * KD * n + 2 * b + 2)
                        for k in (2 * b, 2 * b + 1):
                            c = (k % 2) * SEQ + t * P
                            ins = pe.transpose(ps[:, 4 + b, c:c + P], h[:, t, k * P:(k + 1) * P], ident)
                        ins.then_inc(xT_ready, 1)

                def last_rows(u, hi, lo, k0, n, early=0):
                    for t in range(T):
                        for b in range(2):
                            row_piece(u, t, b, hi, lo, 2, 2 * t + b, b * HALF, HALF, False, True, k0,
                                      weights_used if t and b else bank_done)
                            if t and b == 0:
                                for hf in range(early):
                                    norm_T(n, 0, hf)

                def rows_unit(stage, j, hi, lo, t, w=None):
                    tm_half(U0[stage] + j, t, hi, lo, 2, 2 * t, j == 0, False, None, None, k0=2 * j, wait=w)

                def rms_row(bank):
                    for t in range(T):
                        tokens[0] += 1
                        pe.wait_ge(diag_ready, tokens[0])
                        ins = mm(ps[:, bank, t * P:(t + 1) * P], ones[:, 0:P], diag[:, t, :], True, True)
                    ins.then_inc(rB_T, 1)

                tokens = [0]
                t_prev = [None]

                def t_begin(name):
                    assert T_ORDER[tuse[0]] == name
                    if t_prev[0]:
                        pe.wait_ge(*t_prev[0])
                    tuse[0] += 1
                    t_prev[0] = (t_free, tuse[0])

                def qk_T(c, name, t, srcs):
                    t_begin(f"{name}{t}")
                    pe.wait_ge(rope_ready, 2 * c + t + 1)
                    for n, src in enumerate(srcs):
                        ins = pe.transpose(ps[:, TB, n * P:(n + 1) * P], src, ident)
                    ins.then_inc(t_ready, 1)

                def flat_tiles(t, n):
                    return [rotA[:, t, i * P:(i + 1) * P] for i in range(n)]

                pe.wait_ge(ident_loaded, 16)
                pe.wait_ge(gain0_loaded, 16)
                pe.transpose(ps[:, 0, 0:16], stg[0:16, 5, :], ident[0:16, 0:16]).then_inc(gain0_T, 1)

                for t in range(T):
                    for hf in range(2):
                        norm_T(0, t, hf)
                pe.wait_ge(gain0_ready, 1)
                u = U0["qkv0"]

                def chunk_half(base, c, j, t, xwait=None):
                    tm_half(base + 2 * c + j, t, xhi, xlo, 4, 2 * (c % 2) + t, j == 0, j == 1,
                            None if xwait is None else xwait + 4 * j, k0=4 * j)

                for j in range(2):
                    for t in range(T):
                        chunk_half(u, 0, j, t, 0)
                pe.wait_ge(p_loaded, 32)
                for b in range(2):
                    for k in range(2):
                        for t in range(T):
                            ins = pe.transpose(ps[:, 6 + b, k * SEQ + t * P:k * SEQ + (t + 1) * P],
                                               pst[:, b, t, k * P:(k + 1) * P], ident)
                    ins.then_inc(pT_ready, 1)
                pe.wait_ge(vecs_loaded, 16 * 13)
                pe.transpose(ps[:, 5, 0:V_ROWS], stg[0:V_ROWS, 0, :], ident[0:V_ROWS, 0:V_ROWS])
                n = 4 * FT
                for a in range(4):
                    ins = pe.transpose(ps[:, 5, 80 + a * n:80 + (a + 1) * n], stg[0:n, 1 + a, :], ident[0:n, 0:n])
                ins.then_inc(vecs_T, 1)
                for t in range(T):
                    chunk_half(u, 1, 0, t)
                for t in range(T):
                    qk_T(0, "0q0", t, flat_tiles(t, 4))
                for t in range(T):
                    chunk_half(u, 1, 1, t)
                pe.wait_ge(rope_read, 2)
                for t in range(T):
                    chunk_half(u, 2, 0, t)
                for t in range(T):
                    qk_T(1, "0k0", t, flat_tiles(t, 4))
                for t in range(T):
                    chunk_half(u, 2, 1, t)
                pe.wait_ge(plo_ready, 2)
                pe.wait_ge(vecs_ready, 1)

                def scores0(st, s, base):
                    qt, i = BLOCKS[s]
                    tile = 4 * st + i
                    if 8 * st + s:
                        pe.wait_ge(exp_ready, 8 * st + s)
                    for j in range(2):
                        r = slice(j * HD, (j + 1) * HD)
                        ins = mm(ps[:, base + j, 0:SEQ], qT[r, tile, qt * P:(qt + 1) * P], kT[r, tile, :], True, True)
                    ins.then_inc(s_ready, 1)

                def probs_T0(st, s):
                    b = 8 * st + s
                    t_begin("0" + "AB"[st] + str(s))
                    pe.wait_ge(mix_ready, b + 1)
                    for k in range(2):
                        ins = pe.transpose(ps[:, TB, k * P:(k + 1) * P], Ac[:, s % 2, k * P:(k + 1) * P], ident)
                    ins.then_inc(t_ready, 1)

                def pv0(st, s):
                    qt, i = BLOCKS[s]
                    b = 8 * st + s
                    c = (4 * st + i) * P
                    pe.wait_ge(t_free, T_USE["0" + "AB"[st] + str(s)] + 1)
                    pe.wait_ge(v_ready, 2 * st + 2)
                    if b:
                        pe.wait_ge(o_read, b)
                    for k in range(2):
                        ins = mm(ps[:, OB, 0:P], ATd[:, s % 2, k, :], vtm[:, k, c:c + P], k == 0, k == 1)
                    ins.then_inc(o_ready, 1)

                def o_T(nt, count, src, final):
                    pe.wait_ge(*t_prev[0])
                    pe.wait_ge(*final)
                    for n in range(nt):
                        ins = pe.transpose(ps[:, TB, n * P:(n + 1) * P], src(n), ident)
                    ins.then_inc(oT_ready, 1)
                    t_prev[0] = (olo_ready, count + 1)

                def o_T0(st, qt):
                    o_T(4, 2 * st + qt, lambda n: xn[:, qt, st * HALF + n * P:st * HALF + (n + 1) * P], (on_ready, 2 * st + qt + 1))

                pe.wait_ge(t_free, 4)
                halves = [(c, j, t) for c in (3, 4, 5) for j in range(2) for t in range(T)]

                def chunk_piece(u, j, t, a, bank):
                    done = None
                    if a:
                        done = weights_used if t else tile0_done if j else None
                    wh, wl = slot(whi, u, 4), slot(wlo, u, 4)
                    if t + a == 0:
                        pe.wait_ge(lo_ready, u + 1)
                    for k in (2 * a, 2 * a + 1):
                        xh, xl = xhi[:, 4 * j + k, t * P:(t + 1) * P], xlo[:, 4 * j + k, t * P:(t + 1) * P]
                        mm(ps[:, bank + t, :], xh, wh[:, k, :], j + k == 0, False)
                        mm(ps[:, bank + t, :], xh, wl[:, k, :], False, False)
                        ins = mm(ps[:, bank + t, :], xl, wh[:, k, :], False, j == 1 and k == 3)
                    if done is not None:
                        ins.then_inc(done, 1)

                def half(n, parts=(0, 1)):
                    c, j, t = halves[n]
                    if n == 0:
                        pe.wait_ge(rope_read, 4)
                    if n == 4:
                        pe.wait_ge(v_ready, 2)
                    if n == 8:
                        pe.wait_ge(rope_read, 6)
                    for a in parts:
                        chunk_piece(u + 2 * c + j, j, t, a, 2 * (c % 2))

                for s in range(N_A):
                    scores0(0, s, 6)
                    half(s, (0,))
                    if s:
                        probs_T0(0, s - 1)
                    half(s, (1,))
                    if s:
                        pv0(0, s - 1)
                    if s in (5, 6):
                        qk_T(2, "0q1", s - 5, flat_tiles(s - 5, 4))
                    if s == 6:
                        o_T0(0, 0)
                half(8, (0,))
                probs_T0(0, N_A - 1)
                half(8, (1,))
                pv0(0, N_A - 1)
                half(9)
                qk_T(3, "0k1", 0, flat_tiles(0, 4))
                half(10)
                qk_T(3, "0k1", 1, flat_tiles(1, 4))
                half(11, (0,))
                o_T0(0, 1)
                half(11, (1,))

                def ple_piece(l, n):
                    hf, t = n // 2, n % 2
                    signal = (tile0_done, weights_used)[hf] if t else None
                    row_piece(U0[f"pp{l}"], t, hf, phi, plo, 2, PP_BANK[l][hf] + t, hf * HALF, HALF, True, True, 2 * l, signal)

                def wo_piece(l, n):
                    j, t, b = n // 4, n // 2 % 2, n % 2
                    row_piece(U0[f"wo{l}"] + j, t, b, ohi, olo, 2, 2 * t + b, b * HALF, HALF, j == 0, False, 2 * j,
                              weights_used if t and b else None)

                def wo_rest(l, n):
                    for t in range(T):
                        rows_unit(f"wo{l}", 2, ohi, olo, t, (olo_ready, 4 * l + 3 + t))
                    last_rows(U0[f"wo{l}"] + 3, ohi, olo, 6, n, 2)
                    for hf in range(2):
                        norm_T(n, 1, hf)

                def piece0(n):
                    if n == 0:
                        pe.wait_ge(rope_read, 8)
                    if n == 2:
                        pe.wait_ge(v_ready, 4)
                    if n in (4, 6):
                        pe.wait_ge(pp_ready, n - 2)
                    if n == 4:
                        pe.wait_ge(olo_ready, 2)
                    if n < 4:
                        ple_piece(0, n)
                    else:
                        wo_piece(0, n - 4)

                pe.wait_ge(t_free, T_USE["0k11"] + 1)
                for s in range(N_A):
                    scores0(1, s, 6)
                    if s:
                        probs_T0(1, s - 1)
                    piece0(s)
                    if s == 7:
                        o_T0(1, 0)
                    if s:
                        pv0(1, s - 1)
                piece0(8)
                probs_T0(1, N_A - 1)
                piece0(9)
                pv0(1, N_A - 1)
                for n in (10, 11):
                    piece0(n)
                o_T0(1, 1)
                wo_rest(0, 1)

                def ffn(l):
                    u0 = U0[f"ffn{l}"]

                    def up(ug, buf, gv, i=None):
                        for m in range(2):
                            fm_half(ug, m, xhi, xlo, KD, 4 + 2 * buf + gv, None, at(ug + 1, TURN, i))

                    def down(ud, it, start, stop, i=None):
                        pe.wait_ge(hlo_ready[l], at(it + 1, FFN_TURN, i))
                        for t in range(T):
                            tm_half(ud, t, ohi, olo, 2, 2 * t, start, stop, None, at(ud + 1, TURN, i), k0=2 * (it % 2))

                    def iteration(it, i=None):
                        ug = u0 + 3 * it - 1
                        for gv in range(2):
                            up(ug + gv, it % 2, gv, i)
                        down(ug + 2, it - 1, False, False, i)

                    for m in range(2):
                        fm_half(u0, m, xhi, xlo, KD, 4, 2 * KD * (1 + 3 * l) if m == 0 else None)
                    fm_half(u0 + 1, 0, xhi, xlo, KD, 5)
                    rms_row(0)
                    fm_half(u0 + 1, 1, xhi, xlo, KD, 5)
                    pe.wait_ge(rB_ready, l + 1)
                    for c in range(T * D // P):
                        mm(ps[:, c // 4, c % 4 * P:(c % 4 + 1) * P], identb[:, :], zerob[:, :], True, False)
                    with pe.Fori(0, 8 // FFN_TURN) as i:
                        for n in range(FFN_TURN):
                            iteration(1 + n, i)
                    for n, it in enumerate((9, 10)):
                        for gv in range(2):
                            up(u0 + 26 + 2 * n + gv, it % 2, gv)
                    down(u0 + 30, 8, False, False)
                    down(u0 + 31, 9, False, False)
                    pe.wait_ge(hlo_ready[l], 11)
                    last_rows(u0 + 32, ohi, olo, 0, 2 + 3 * l, 2)

                def gate(l):
                    n = 2 + 3 * l
                    rows_unit(f"gate{l}", 0, xhi, xlo, 0, (xlo_ready, 2 * KD * n + 2))
                    for hf in range(2):
                        norm_T(n, 1, hf)
                    rows_unit(f"gate{l}", 0, xhi, xlo, 1, (xlo_ready, 2 * KD * n + KD + 2))
                    for j in (1, 2):
                        for t in range(T):
                            rows_unit(f"gate{l}", j, xhi, xlo, t, (xlo_ready, 2 * KD * n + KD * t + 2 * j + 2))
                    pe.wait_ge(xlo_ready, 2 * KD * (n + 1))
                    last_rows(U0[f"gate{l}"] + 3, xhi, xlo, 6, n + 1, 1)

                def first_chunk(n, unit):
                    unit(0, 0)
                    norm_T(n, 0, 1)
                    norm_T(n, 1, 0)
                    unit(0, 1)
                    norm_T(n, 1, 1)
                    unit(1, 0)
                    unit(1, 1)

                ffn(0)
                gate(0)

                u = U0["qkv1"]
                first_chunk(3, lambda j, t: chunk_half(u, 0, j, t, 2 * KD * 3))
                for t in range(T):
                    chunk_half(u, 1, 0, t)
                for t in range(T):
                    qk_T(4, "1k", t, flat_tiles(t, 2))
                for t in range(T):
                    chunk_half(u, 1, 1, t)
                pe.wait_ge(rope_read, 10)

                def q1_piece(j, n):
                    chunk_piece(u + 4 + j, j, n // 2, n % 2, 0)

                for n in range(3):
                    q1_piece(0, n)
                qk_T(5, "1q0", 0, flat_tiles(0, 4))
                q1_piece(0, 3)
                qk_T(5, "1q0", 1, flat_tiles(1, 4))

                def piece1(s):
                    if s < 4:
                        q1_piece(1, s)
                    if s in (5, 7, 8, 9):
                        n = (5, 7, 8, 9).index(s)
                        if n == 2:
                            pe.wait_ge(rope_read, 14)
                        ple_piece(1, n)
                    if s >= 11:
                        if s == 11:
                            pe.wait_ge(pp_ready, 8)
                            pe.wait_ge(olo_ready, 6)
                        wo_piece(1, s - 11)

                def o_T1(st, qt):
                    o_T(4, 4 + 2 * st + qt, lambda n: xn[:, qt, (4 * st + n) * P:(4 * st + n + 1) * P],
                        (o_read, S_AT["1"] + 8 * st + 4 * qt + 4))

                def scores1(s):
                    g, qt, r, i = SWA_BLOCKS[s]
                    rows_ = slice(r * HD, (r + 1) * HD)
                    if s == 0:
                        pe.wait_ge(t_free, T_USE["1q01"] + 1)
                        pe.wait_ge(rope_read, 12)
                    if s in (8, 12):
                        pe.wait_ge(t_free, T_USE[f"1q1{s // 4 - 2}"] + 1)
                    c = (1 - qt) * P
                    for j in range(2):
                        o = j * SEQ + c
                        mm(ps[:, 6 + s % 2, j * SEQ:(j + 1) * SEQ], qT[rows_, 4 * g + i + j, qt * P:(qt + 1) * P],
                           kT[rows_, g, :], True, False)
                        ins = mm(ps[:, 6 + s % 2, o:o + P], identb[:, :], maskb[:, qt, :], False, True)
                    ins.then_inc(s_ready, 1)

                def probs_T1(s):
                    t_begin(f"1A{s}")
                    pe.wait_ge(exp_ready, S_AT["1"] + s + 1)
                    for j in range(2):
                        for k in range(2):
                            n = 2 * j + k
                            ins = pe.transpose(ps[:, TB, n * P:(n + 1) * P], Eb[:, s % 2, j, k * P:(k + 1) * P], ident)
                    ins.then_inc(t_ready, 1)

                def pv1(s):
                    g, qt, r, i = SWA_BLOCKS[s]
                    c = (2 * g + r) * HD
                    pe.wait_ge(t_free, T_USE[f"1A{s}"] + 1)
                    pe.wait_ge(o_read, S_AT["1"] + s)
                    for j in range(2):
                        for k in range(2):
                            ins = mm(ps[:, OB, j * HD:(j + 1) * HD], ATs[:, s % 2, 2 * j + k, :], vtm[:, k, c:c + HD],
                                     k == 0, k == 1)
                    ins.then_inc(o_ready, 1)

                scores1(0)
                scores1(1)
                for s in range(2 * N_A):
                    probs_T1(s)
                    if s + 2 < 2 * N_A:
                        scores1(s + 2)
                    if s:
                        pv1(s - 1)
                    if s in (5, 9, 13):
                        o_T1((s - 5) // 8, (s - 5) // 4 % 2)
                    piece1(s)
                    if s in (5, 6):
                        qk_T(6, "1q1", s - 5, flat_tiles(s - 5, 4))
                pv1(2 * N_A - 1)
                for s in (16, 17, 18):
                    piece1(s)
                o_T1(1, 1)
                wo_rest(1, 4)
                ffn(1)
                gate(1)

                def in2(n, between=None):
                    kind, j, u, nb = IN2[n]
                    bank = in2_bank[n]
                    if in2_need[n]:
                        pe.wait_ge(in2_read, in2_need[n])
                    if kind in ("vb", "va0"):
                        for i in range(2):
                            for t in range(T):
                                tm_half(u + i, t, xhi, xlo, 4, bank + t, i == 0, i == 1, k0=4 * i)
                    elif kind == "va1":
                        for t in range(T):
                            tm_half(u, t, xhi, xlo, KD, bank + t, True, True)
                    else:
                        for m in range(2):
                            fm_half(u, m, xhi, xlo, KD, bank)
                            if between and m == 0:
                                between()

                def scores_sb(s):
                    pr, qt = SB_BLOCKS[s]
                    nk = P * (qt + 1)
                    for j in range(2):
                        r = slice(j * HD, (j + 1) * HD)
                        ins = mm(ps[:, 6 + j, 0:nk], qTb[r, pr, qt * P:(qt + 1) * P], kTb[r, pr, 0:nk], True, True)
                    ins.then_inc(s_ready, 1)

                def weights_T_sb(s):
                    pr, qt = SB_BLOCKS[s]
                    t_begin(f"2S{s}")
                    pe.wait_ge(mix_ready, 16 + s + 1)
                    for n in range(2 * (qt + 1)):
                        ins = pe.transpose(ps[:, TB, n * P:(n + 1) * P], sba[:, n * P:(n + 1) * P], ident)
                    ins.then_inc(t_ready, 1)

                def pv_sb(s):
                    pr, qt = SB_BLOCKS[s]
                    pe.wait_ge(t_free, T_USE[f"2S{s}"] + 1)
                    pe.wait_ge(o_read, S_AT["S"] + s)
                    for j in range(2):
                        c = (2 * pr + j) * HD
                        for k in range(qt + 1):
                            n = j * (qt + 1) + k
                            ins = mm(ps[:, OB, j * HD:(j + 1) * HD], ETs[:, n * P:(n + 1) * P], vb[:, k, c:c + HD],
                                     k == 0, k == qt)
                    ins.then_inc(o_ready, 1)

                u = U0["in2"]
                first_chunk(6, lambda j, t: tm_half(u + j, t, xhi, xlo, 4, t, j == 0, j == 1, 2 * KD * 6 + 4 * j, k0=4 * j))
                in2(1)
                rms_row(7)
                for n in range(2, 5):
                    in2(n)
                pe.wait_ge(in2_read, in2_count[4])
                for s in range(9):
                    if s:
                        weights_T_sb(s - 1)
                    if s < 8:
                        scores_sb(s)
                    if s == 7:
                        o_T(4, 8, lambda n: xn[:, 0, n * P:(n + 1) * P], (o_read, S_AT["S"] + 4))
                    in2(5 + s)
                    if s:
                        pv_sb(s - 1)
                o_T(4, 9, lambda n: xn[:, 1, n * P:(n + 1) * P], (o_read, S_AT["S"] + 8))

                def scores_dil(s):
                    j, qt = DIL_BLOCKS[s]
                    nk = P * (qt + 1)
                    for g in range(3):
                        hd = 4 * g + j
                        r = slice((hd % 2) * HD, (hd % 2 + 1) * HD)
                        ins = mm(ps[:, 6 + g // 2, (g % 2) * nk:(g % 2 + 1) * nk], qTa[r, hd // 2, qt * P:(qt + 1) * P],
                                 kTa[r, hd // 2, 0:nk], True, True)
                    ins.then_inc(s_ready, 1)

                def probs_T_dil(s, part):
                    j, qt = DIL_BLOCKS[s]
                    n = 3 * (qt + 1)
                    t_begin(f"2D{s}" + "ab"[part])
                    pe.wait_ge(exp_ready, 32 + s + 1)
                    for a in range(4 * part, min(n, 4 * part + 4)):
                        b = a - 4 * part
                        ins = pe.transpose(ps[:, TB, b * P:(b + 1) * P], dlL[:, s % 2, a * P:(a + 1) * P], ident)
                    ins.then_inc(t_ready, 1)

                def pv_dil(s):
                    j, qt = DIL_BLOCKS[s]
                    pe.wait_ge(t_free, T_USE[f"2D{s}" + "ab"[qt]] + 1)
                    pe.wait_ge(o_read, S_AT["D"] + s)
                    n = 3 * (qt + 1)
                    for a in range(n):
                        g, k = a // (qt + 1), a % (qt + 1)
                        c = (4 * g + j) * HD
                        ins = mm(ps[:, OB, 0:HD], ETb[:, a * P:(a + 1) * P], va[:, k, c:c + HD], a == 0, a == n - 1)
                    ins.then_inc(o_ready, 1)

                def sb_up(c, b):
                    for m in (2 * b, 2 * b + 1):
                        fm_half(U0["sbup"] + c, m, ohi, olo, 4, 2 * c + m // 2, last=3)

                pe.wait_ge(in2_read, in2_count[in2_at["va10"]])
                for s in range(9):
                    if s:
                        probs_T_dil(s - 1, 0)
                    if s < 8:
                        scores_dil(s)
                    if s and DIL_BLOCKS[s - 1][1]:
                        probs_T_dil(s - 1, 1)
                    if s < 7:
                        in2(in2_at["gl1"] + s)
                    else:
                        pe.wait_ge(in2_read, in2_count[-1])
                        sb_up(s - 7, 0)
                        if s == 7:
                            o_T(2, 10, lambda n: xn[:, 0, HALF + n * P:HALF + (n + 1) * P], (o_read, S_AT["D"] + 4))
                        sb_up(s - 7, 1)
                    if s:
                        pv_dil(s - 1)
                o_T(2, 11, lambda n: xn[:, 1, HALF + n * P:HALF + (n + 1) * P], (o_read, S_AT["D"] + 8))
                pe.wait_ge(olo_ready, 12)
                for m in range(8):
                    fm_half(U0["dilup"], m, ohi, olo, 2, 4 + m // 2, k0=4, last=7, signal=dilup_done if m in (1, 3, 5) else None)
                for j in range(3):
                    for t in range(T):
                        rows_unit("wout", j, xhi, xlo, t, (mlo_ready, j + 1))
                pe.wait_ge(mlo_ready, 4)
                last_rows(U0["wout"] + 3, xhi, xlo, 6, 7, 2)
                for hf in range(2):
                    norm_T(7, 1, hf)

                u0 = U0["mlp"]

                def mlp_up(u, it, i=None, xwait=None):
                    for m in range(2):
                        fm_half(u, m, xhi, xlo, KD, 4 + it % 3, xwait, at(u + 1, TURN, i))

                def mlp_down(u, it, start, stop, i=None):
                    pe.wait_ge(rlo_ready, at(it + 1, MLP_TURN, i))
                    for t in range(T):
                        tm_half(u, t, ohi, olo, 2, 2 * t, start, stop, None, at(u + 1, TURN, i), k0=2 * (it % 3))

                def mlp_iteration(it, i=None):
                    mlp_up(u0 + 2 * it - 1, it, i)
                    mlp_down(u0 + 2 * it, it - 1, it == 1, False, i)

                mlp_up(u0, 0, xwait=2 * KD * 7)
                mlp_iteration(1)
                with pe.Fori(0, 12 // MLP_TURN) as i:
                    for n in range(MLP_TURN):
                        mlp_iteration(2 + n, i)
                mlp_iteration(14)
                mlp_iteration(15)
                pe.wait_ge(rlo_ready, 16)
                last_rows(u0 + 31, ohi, olo, 0, None)


NAMES = ["x", "p", "positions", "attn_norm", "ffn_norm", "ple_norm", "final_norm", "diff_w_qkv", "diff_w_o",
         "diff_lambda", "diff_subln", "swa_w_qkv", "swa_w_o", "swa_sinks", "ffn_w_up", "ffn_conv_w", "ffn_conv_b",
         "ffn_w_down", "ple_w_proj", "ple_w_gate", "norm_mix_g_2", "w_in_2", "b_gate_2", "w_up_dil_2", "w_up_sb_2",
         "w_out_2", "norm_mlp_g_2", "w_mlp_in_2", "w_mlp_out_2", "norm_final_g_2"]


def kernel(**inputs):
    import concourse.bacc as bacc
    from concourse.bass_utils import run_bass_kernel_spmd

    nc = bacc.Bacc("TRN2", target_bir_lowering=False, num_devices=1)
    arrays, args = {}, []
    for name in NAMES:
        a = np.ascontiguousarray(inputs[name])
        arrays[f"in_{name}"] = a
        args.append(nc.dram_tensor(f"in_{name}", a.shape, mybir.dt.from_np(a.dtype), kind="ExternalInput").ap())
    table = constants()
    arrays["in_table"] = table
    args.append(nc.dram_tensor("in_table", table.shape, F32, kind="ExternalInput").ap())
    args.append(nc.dram_tensor("out_0", (1, SEQ, D), F32, kind="ExternalOutput").ap())
    three_layer_kernel(nc, *args)
    r = run_bass_kernel_spmd(nc, [arrays], core_ids=[0])
    return r.results[0]["out_0"]
```

```python
import math
from contextlib import ExitStack

import numpy as np
import concourse.bass as bass
from concourse import mybir

F32 = mybir.dt.float32
F32R = mybir.dt.float32r
BF16 = mybir.dt.bfloat16
I32 = mybir.dt.int32
ALU = mybir.AluOpType
ACT = mybir.ActivationFunctionType
AX = mybir.AxisListType

P = 128
SEQ = 256
T = SEQ // P
D = 1024
KD = D // P
HALF = 512
HD = 64
FF = 2816
FT = FF // P
EPS = 1e-6
UNIT = 2048
RAW = 3
TURN = 12
FFN_TURN = TURN // 3
MLP_TURN = TURN // 2
RING = 4
WARM0, WARM1 = 30, 36
LAM_INIT = 0.8 - 0.6 * math.exp(0.0)
DIL_GROUPS = ((128, 1), (512, 4), (2048, 16))
N_DIL = 12
SLOPES = [2.0 ** (-8.0 * (n + 1) / N_DIL) for n in range(N_DIL)]
NEG = -1e30
FAR = 1e33

STAGES = [("qkv0", 12), ("pp0", 1), ("wo0", 4), ("ffn0", 33), ("gate0", 4),
          ("qkv1", 6), ("pp1", 1), ("wo1", 4), ("ffn1", 33), ("gate1", 4),
          ("in2", 15), ("gl2", 8), ("sbup", 2), ("dilup", 1), ("wout", 4), ("mlp", 32)]
U0 = {}
_n = 0
for _name, _count in STAGES:
    U0[_name] = _n
    _n += _count
NU = _n

POOL_UNITS = [U0[f"ffn{l}"] + n for l in range(2) for n in (*range(1, 29, 3), 30, 32, 34)]

TM_ORDER = [f"qkv0.{c}" for c in range(6)] + ["pp0"] + [f"qkv1.{c}" for c in range(3)] + ["pp1"] \
    + ["in2.vb", "in2.va0", "in2.va1"]
TM = {name: i + 1 for i, name in enumerate(TM_ORDER)}
RES_ORDER = ["wo0", "ffn0", "gate0", "wo1", "ffn1", "gate1", "wout", "mlp"]

V_BGATE, V_SUBLN, V_MID, V_ROWS = 48, 64, 65, 73
V_ATTN = 80
V_MIX = 96
V_COLS = 104
GAIN = {0: V_ATTN, 1: 0, 2: 16, 3: V_ATTN + 8, 4: 8, 5: 24, 6: V_MIX, 7: 40}
V_MIXG = 32
C_ID = 0
C_SWA = C_ID + P
C_DIL = C_SWA + 2 * P
C_FREQ = C_DIL + 3 * SEQ
C_COLS = C_FREQ + HD // 2


def at(value, step, i):
    return value if i is None else i * step + value


def constants():
    t = np.zeros((P, C_COLS), np.float32)
    q = np.arange(P)[:, None]
    k = np.arange(P)[None, :]
    t[:, C_ID:C_ID + P] = np.eye(P)
    t[:, C_SWA:C_SWA + P] = np.where(k <= q, 0.0, NEG)
    t[:, C_SWA + P:C_SWA + 2 * P] = np.where(q <= k, 0.0, NEG)
    dist = P + q - np.arange(SEQ)[None, :]
    for g, (window, dil) in enumerate(DIL_GROUPS):
        ok = (dist >= 0) & (dist % dil == 0) & (dist <= window)
        t[:, C_DIL + g * SEQ:C_DIL + (g + 1) * SEQ] = np.where(ok, dist, FAR)
    t[:, C_FREQ:] = (10000.0 ** (-np.arange(0, HD, 2) / HD)).astype(np.float32)
    return t


def three_layer_kernel(nc, x, p, positions, attn_norm, ffn_norm, ple_norm, final_norm, diff_w_qkv,
                       diff_w_o, diff_lambda, diff_subln, swa_w_qkv, swa_w_o, swa_sinks, ffn_w_up,
                       ffn_conv_w, ffn_conv_b, ffn_w_down, ple_w_proj, ple_w_gate, norm_mix_g_2,
                       w_in_2, b_gate_2, w_up_dil_2, w_up_sb_2, w_out_2, norm_mlp_g_2, w_mlp_in_2,
                       w_mlp_out_2, norm_final_g_2, table, out):
    with ExitStack() as ctx:
        def sb(name, shape, dt=F32):
            return ctx.enter_context(nc.sbuf_tensor(name, shape, dt))

        def sem(name):
            return ctx.enter_context(nc.semaphore(name))

        raw = sb("raw", [P, RAW, UNIT])
        whi = sb("whi", [P, RING, UNIT], F32R)
        wlo = sb("wlo", [P, RING, UNIT], F32R)
        h = sb("h", [P, T, D])
        xn = sb("xn", [P, T, D])
        xhi = sb("xhi", [P, KD, SEQ], F32R)
        xlo = sb("xlo", [P, KD, SEQ], F32R)
        ohi = sb("ohi", [P, KD, SEQ], F32R)
        olo = sb("olo", [P, KD, SEQ], F32R)
        phi = sb("phi", [P, 4, SEQ], F32R)
        plo = sb("plo", [P, 4, SEQ], F32R)
        pp = sb("pp", [P, T, D])
        tab = sb("tab", [P, C_COLS])
        vecT = sb("vecT", [P, V_COLS])
        ones = sb("ones", [P, SEQ])
        diag = sb("diag", [P, T, P])
        rB = sb("rB", [P, SEQ])
        rBq = sb("rBq", [P, SEQ])
        cosr = sb("cosr", [P, T, HD])
        sinr = sb("sinr", [P, T, HD])
        cwT = sb("cwT", [P, 2, 4, 2 * FT])
        cosd = sb("cosd", [P, T, HD])
        sind = sb("sind", [P, T, HD])
        posi = sb("posi", [P, T], I32)
        sinks = sb("sinks", [P, 16])
        stat = sb("stat", [P, 400])
        identb = sb("identb", [P, P], BF16)
        maskb = sb("maskb", [P, 2, P], BF16)
        zerob = sb("zerob", [P, P], BF16)
        scr = sb("scr", [P, 10368])
        ps = ctx.enter_context(nc.psum_tensor("ps", [P, 8, HALF], F32))

        ident = tab[:, C_ID:C_ID + P]

        def region(first, size, pattern=None, **kw):
            v = scr[:, first:first + size]
            return v.rearrange(pattern, **kw) if pattern else v

        ss = stat[:, 0:18]
        rstd = stat[:, 18:36]
        nhalf = stat[:, 36:44]
        nlam = stat[:, 44:45]
        subg = stat[:, 45:46]
        lam2 = stat[:, 46:48]
        posf = stat[:, 48:50]
        nsink = stat[:, 50:66]
        nmax = stat[:, 66:98].rearrange("p (b j) -> p b j", j=2)
        esum = stat[:, 98:130].rearrange("p (b j) -> p b j", j=2)
        rsum = stat[:, 130:162].rearrange("p (b j) -> p b j", j=2)
        mixc = stat[:, 162:178]
        oss = stat[:, 178:194].rearrange("p (s q d) -> p s q d", s=2, q=2)
        ors = stat[:, 194:210].rearrange("p (s q d) -> p s q d", s=2, q=2)
        sinkd = stat[:, 210:242].rearrange("p (b j) -> p b j", j=2)
        nmax1 = stat[:, 242:274].rearrange("p (b j) -> p b j", j=2)
        esum1 = stat[:, 274:306].rearrange("p (b j) -> p b j", j=2)
        rsum1 = stat[:, 306:338].rearrange("p (b j) -> p b j", j=2)
        nmax2 = stat[:, 338:346]
        esum2 = stat[:, 346:354]
        rsum2 = stat[:, 354:362]
        ssg = stat[:, 363:365]
        rboth = stat[:, 365:367]
        rtmp = stat[:, 367:369]
        minus1 = stat[:, 391:393]
        ssl = stat[:, 393:397]
        r2 = stat[:, 369:371]
        warm = stat[:, 371:391]

        qT = region(0, 2048, "p (a c) -> p a c", c=SEQ)
        kT = region(2048, 2048, "p (a c) -> p a c", c=SEQ)
        vtm = region(4096, 2048, "p (t c) -> p t c", t=T)
        rotA = region(6144, 1024, "p (t c) -> p t c", t=T)
        rotB = region(7168, 1024, "p (t c) -> p t c", t=T)
        Eb = region(8192, 1024, "p (b j c) -> p b j c", b=2, j=2)
        Ac = region(9216, 512, "p (b c) -> p b c", b=2)
        ATd = region(9728, 512, "p (b k c) -> p b k c", b=2, k=2)
        ATs = region(9216, 1024, "p (b k c) -> p b k c", b=2, k=4)
        junk = region(10240, P)
        stg = region(8192, 6 * P, "p (a c) -> p a c", a=6)
        pst = region(8960, 1024, "p (l t c) -> p l t c", l=2, t=2)
        trg = region(4096, 4 * P, "p (a c) -> p a c", a=4)
        lamb = region(4608, 4 * HD, "p (a d) -> p a d", a=4)
        cgv = region(0, 2048, "p (b g c) -> p b g c", b=2, g=2)
        sgl = region(2048, 1024, "p (b c) -> p b c", b=2)
        hid = region(3072, 1024, "p (b c) -> p b c", b=2)
        usc = region(4096, 2048, "p (b g c) -> p b g c", b=2, g=2)
        ga = pp[:, :, :].rearrange("p t (m c) -> p (t m) c", c=SEQ)
        gb = region(0, 2048, "p (m c) -> p m c", c=SEQ)
        mB = region(2048, 2048, "p (j c) -> p j c", c=HALF)
        qTa = region(2048, 1536, "p (a c) -> p a c", c=SEQ)
        kTa = region(3584, 1536, "p (a c) -> p a c", c=SEQ)
        va = region(5120, 1536, "p (t c) -> p t c", t=T)
        qTb = region(6656, 1024, "p (a c) -> p a c", c=SEQ)
        kTb = region(7680, 1024, "p (a c) -> p a c", c=SEQ)
        vb = region(8704, 1024, "p (t c) -> p t c", t=T)
        sbp = region(0, 512)
        sbm = region(512, 512)
        sbc = region(9728, 2 * (SEQ + 1), "p (j c) -> p j c", j=2)
        sba = region(1024, 512)
        ETs = region(1536, 512)
        dlL = region(6656, 1536, "p (b c) -> p b c", b=2)
        ETb = region(8192, 768)
        rel = region(0, 1536, "p (b c) -> p b c", b=3)
        rsq = region(1536, 1536, "p (b c) -> p b c", b=3)
        hg = pp
        gfin = region(6144, D)
        gmid = region(6144, D)

        raw_full = [sem(f"raw_full{s}") for s in range(RAW)]
        first_half = sem("first_half")
        first_lo = sem("first_lo")
        hi_ready = sem("hi_ready")
        hi_half = sem("hi_half")
        lo_ready = sem("lo_ready")
        lo_pool = sem("lo_pool")
        weights_used = sem("weights_used")
        tile0_done = sem("tile0_done")
        bank_done = sem("bank_done")
        diag_ready = sem("diag_ready")
        rB_T = sem("rB_T")
        rB_ready = sem("rB_ready")
        r2_ready = sem("r2_ready")
        ones_set = sem("ones_set")
        zeros_set = sem("zeros_set")
        sum_ready = sem("sum_ready")
        prodp_ready = sem("prodp_ready")
        trig_loaded = sem("trig_loaded")
        gates_ready = sem("gates_ready")
        dilup_done = sem("dilup_done")
        prod_ready = sem("prod_ready")
        h_loaded = [sem(f"h_loaded{t}") for t in range(T)]
        ident_loaded = sem("ident_loaded")
        gain0_loaded = sem("gain0_loaded")
        gain0_T = sem("gain0_T")
        gain0_ready = sem("gain0_ready")
        table_loaded = sem("table_loaded")
        vecs_loaded = sem("vecs_loaded")
        p_loaded = sem("p_loaded")
        gmid_loaded = sem("gmid_loaded")
        hg_ready = sem("hg_ready")
        sumsqg_ready = sem("sumsqg_ready")
        rboth_ready = sem("rboth_ready")
        gfin_loaded = sem("gfin_loaded")
        vecs_T = sem("vecs_T")
        vecs_ready = sem("vecs_ready")
        pT_ready = sem("pT_ready")
        phi_ready = sem("phi_ready")
        plo_ready = sem("plo_ready")
        pp_ready = sem("pp_ready")
        trig_arg = sem("trig_arg")
        trig_ready = sem("trig_ready")
        lam_sums = sem("lam_sums")
        lam_exps = sem("lam_exps")
        h_ready = sem("h_ready")
        sumsq_ready = sem("sumsq_ready")
        rstd_ready = sem("rstd_ready")
        xT_ready = sem("xT_ready")
        xhi_ready = sem("xhi_ready")
        xlo_ready = sem("xlo_ready")
        rope_read = sem("rope_read")
        rope_ready = sem("rope_ready")
        v_ready = sem("v_ready")
        t_ready = sem("t_ready")
        t_free = sem("t_free")
        head_done = sem("head_done")
        s_ready = sem("s_ready")
        max_ready = sem("max_ready")
        exp_ready = sem("exp_ready")
        mix_ready = sem("mix_ready")
        o_ready = sem("o_ready")
        o_read = sem("o_read")
        sinkarg_ready = sem("sinkarg_ready")
        sinkexp_ready = sem("sinkexp_ready")
        orstd_ready = sem("orstd_ready")
        on_ready = sem("on_ready")
        oT_ready = sem("oT_ready")
        ohi_ready = sem("ohi_ready")
        olo_ready = sem("olo_ready")
        mid_ready = [sem(f"mid_ready{l}") for l in range(2)]
        scaled = [sem(f"scaled{l}") for l in range(2)]
        tap_done = [sem(f"tap_done{l}") for l in range(2)]
        conv_done = [sem(f"conv_done{l}") for l in range(2)]
        silu_ready = [sem(f"silu_ready{l}") for l in range(2)]
        hid_ready = [sem(f"hid_ready{l}") for l in range(2)]
        hhi_ready = [sem(f"hhi_ready{l}") for l in range(2)]
        hlo_ready = [sem(f"hlo_ready{l}") for l in range(2)]
        gate_ready = sem("gate_ready")
        in2_read = sem("in2_read")
        sb_l = sem("sb_l")
        sb_sel = sem("sb_sel")
        merged = sem("merged")
        mhi_ready = sem("mhi_ready")
        mlo_ready = sem("mlo_ready")
        relu_ready = sem("relu_ready")
        sq_ready = sem("sq_ready")
        rhi_ready = sem("rhi_ready")
        rlo_ready = sem("rlo_ready")
        dve_step = sem("dve_step")
        pool_step = sem("pool_step")
        gained = sem("gained")
        out_dve = sem("out_dve")
        out_act = sem("out_act")
        stored = sem("stored")

        def column(m, i):
            return slice(m, m + 1) if i is None else bass.ds(i * (2 * FFN_TURN) + m, 1)

        def unit_split(u, i=None):
            by_pool = sum(v <= u for v in POOL_UNITS)
            if u in POOL_UNITS:
                return lo_pool, at(by_pool, FFN_TURN, i)
            return lo_ready, at(u + 1 - by_pool, TURN if u >= U0["mlp"] else TURN - FFN_TURN, i)

        def rows(w, k0, kk, c0, n):
            return w[k0 * P:(k0 + kk) * P, c0:c0 + n].rearrange("(k p) n -> p k n", p=P)

        IN2 = []
        u = U0["in2"]
        IN2.append(("vb", 0, u, 2))
        u += 2
        for kind, cols in (("qb", 512), ("kb", 512)):
            for j in range(cols // 256):
                IN2.append((kind, j, u, 1))
                u += 1
        for kind in ("qa", "ka"):
            for j in range(3):
                IN2.append((kind, j, u, 1))
                u += 1
        IN2.append(("va0", 0, u, 2))
        IN2.append(("va1", 0, u + 2, 2))
        u += 3
        for j in range(8):
            IN2.append(("gl", j, u, 1))
            u += 1
        in2_bank, in2_need, in2_count = [], [], []
        last_use, next_bank, done = {}, 0, 0
        for kind, j, u, nb in IN2:
            if nb == 2 and next_bank % 2:
                next_bank += 1
            banks = [(next_bank + i) % 4 for i in range(nb)]
            next_bank += nb
            in2_bank.append(banks[0])
            in2_need.append(max(last_use.get(b, 0) for b in banks))
            done += nb
            in2_count.append(done)
            for b in banks:
                last_use[b] = done
        in2_at = {f"{kind}{j}": n for n, (kind, j, _, _) in enumerate(IN2)}

        SB_BLOCKS = [(pr, qt) for qt in range(2) for pr in range(4)]
        DIL_BLOCKS = [(j, qt) for qt in range(2) for j in range(4)]
        BLOCKS = [(qt, i) for qt in range(2) for i in range(4)]
        N_A = 8
        SWA_BLOCKS = [(g, qt, r, 2 * ip) for g in range(2) for qt in range(2) for r in range(2) for ip in range(2)]

        T_ORDER = [f"0{name}{t}" for name in ("q0", "k0") for t in range(T)]
        for s in range(N_A):
            T_ORDER.append(f"0A{s}")
            if s in (5, 6):
                T_ORDER.append(f"0q1{s - 5}")
        T_ORDER += ["0k10", "0k11"] + [f"0B{s}" for s in range(N_A)]
        T_ORDER += [f"1{name}{t}" for name in ("k", "q0") for t in range(T)]
        for s in range(2 * N_A):
            T_ORDER.append(f"1A{s}")
            if s in (4, 6):
                T_ORDER.append(f"1q1{s // 2 - 2}")
        T_ORDER += [f"2S{s}" for s in range(8)]
        for s, (j, qt) in enumerate(DIL_BLOCKS):
            T_ORDER += [f"2D{s}a", f"2D{s}b"][0:qt + 1]
        T_USE = {name: n for n, name in enumerate(T_ORDER)}
        PP_BANK = ((0, 2), (2, 0))

        TB, OB = 4, 5
        S_AT = {"A": 0, "B": 8, "1": 16, "S": 32, "D": 40}

        with nc.Block() as block:

            @block.sync
            def _(sp):
                sp.dma_start(h[:, 0, :], x[0, 0:P, :]).then_inc(h_loaded[0], 16)
                sp.dma_start(tab[:, 0:P], table[:, 0:P]).then_inc(ident_loaded, 16)
                sp.dma_start(stg[0:16, 5, :], attn_norm.rearrange("l (r c) -> (l r) c", c=P)).then_inc(gain0_loaded, 16)
                wq = diff_w_qkv[0]
                first = raw[:, 0, :].rearrange("p (k n) -> p k n", k=4)
                sp.dma_start(first[:, 0:2], rows(wq, 0, 2, 0, HALF)).then_inc(first_half, 16)
                sp.dma_start(first[:, 2:4], rows(wq, 2, 2, 0, HALF)).then_inc(raw_full[0], 16)
                sp.dma_start(h[:, 1, :], x[0, P:2 * P, :]).then_inc(h_loaded[1], 16)

                def load_small():
                    sp.dma_start(posi[:, :], positions[0].rearrange("(t p) -> p t", p=P),
                                 allow_slow_non_contiguous=True).then_inc(trig_loaded, 16)
                    sp.dma_start(lamb[:, :, :], diff_lambda[0].partition_broadcast(P)).then_inc(trig_loaded, 16)
                    sp.dma_start(sinks[:, :], swa_sinks[0].partition_broadcast(P)).then_inc(trig_loaded, 16)
                    sp.dma_start(tab[:, P:C_COLS], table[:, P:C_COLS]).then_inc(table_loaded, 16)
                    for l in range(2):
                        sp.dma_start(pst[:, l], p[l, 0].rearrange("(t q) c -> q t c", q=P)).then_inc(p_loaded, 16)
                    vec_rows = [(ffn_norm, 0, 16), (ple_norm, 16, 16), (norm_mix_g_2, V_MIXG, 8), (norm_mlp_g_2, 40, 8),
                                (b_gate_2, V_BGATE, 16), (diff_subln, V_SUBLN, 1)]
                    for src, r0, n in vec_rows:
                        sp.dma_start(stg[r0:r0 + n, 0, :], src.rearrange("l (r c) -> (l r) c", c=P)).then_inc(vecs_loaded, 16)
                    sp.dma_start(stg[V_MID:V_MID + 8, 0, :], final_norm.rearrange("(r c) -> r c", c=P)).then_inc(vecs_loaded, 16)
                    for l in range(2):
                        sp.dma_start(stg[0:2 * 2 * FT, 1 + 2 * l, :],
                                     ffn_conv_w[l, 0:2].rearrange("t (m c) -> (t m) c", c=P)).then_inc(vecs_loaded, 16)
                        sp.dma_start(stg[0:2 * FT, 2 + 2 * l, :],
                                     ffn_conv_w[l, 2].rearrange("(m c) -> m c", c=P)).then_inc(vecs_loaded, 16)
                        sp.dma_start(stg[2 * FT:4 * FT, 2 + 2 * l, :],
                                     ffn_conv_b[l].rearrange("(m c) -> m c", c=P)).then_inc(vecs_loaded, 16)

                def load(u, src, kk, i=None):
                    if u >= RAW:
                        sp.wait_ge(*unit_split(u - RAW, i))
                    sp.dma_start(raw[:, u % RAW, :].rearrange("p (k n) -> p k n", k=kk), src)\
                        .then_inc(raw_full[u % RAW], 16)

                def load_rows(stage, w):
                    for j in range(4):
                        load(U0[stage] + j, rows(w, 2 * j, 2, 0, D), 2)

                def load_ffn(l):
                    u0 = U0[f"ffn{l}"]
                    up = ffn_w_up[l].rearrange("(k p) n -> p k n", p=P)
                    down = ffn_w_down[l].rearrange("(g k p) n -> g p k n", k=2, p=P)
                    load(u0, up[:, :, 0:256], KD)
                    load(u0 + 1, up[:, :, FF:FF + 256], KD)
                    with sp.Fori(0, 8 // FFN_TURN) as i:
                        gate_at = [sp.snap(i * (256 * FFN_TURN) + 256 * (1 + n)) for n in range(FFN_TURN)]
                        val_at = [sp.snap(i * (256 * FFN_TURN) + FF + 256 * (1 + n)) for n in range(FFN_TURN)]
                        down_at = [sp.snap(i * FFN_TURN + n) for n in range(FFN_TURN)]
                        for n in range(FFN_TURN):
                            u = u0 + 3 * (1 + n) - 1
                            for what, src in enumerate((up[:, :, bass.ds(gate_at[n], 256)], up[:, :, bass.ds(val_at[n], 256)],
                                                        down[bass.ds(down_at[n], 1)].rearrange("g p k n -> p (g k) n"))):
                                load(u + what, src, (KD, KD, 2)[what], i)
                    for n, it in enumerate((9, 10)):
                        load(u0 + 26 + 2 * n, up[:, :, 256 * it:256 * (it + 1)], KD)
                        load(u0 + 27 + 2 * n, up[:, :, FF + 256 * it:FF + 256 * (it + 1)], KD)
                    for n in range(3):
                        load(u0 + 30 + n, rows(ffn_w_down[l], 2 * (8 + n), 2, 0, D), 2)

                u = U0["qkv0"]
                for c0 in (0, D, 2 * D, HALF, D + HALF, 2 * D + HALF):
                    for j in range(2):
                        if u:
                            load(u, rows(wq, 4 * j, 4, c0, HALF), 4)
                        u += 1
                        if u == RAW:
                            load_small()
                load(U0["pp0"], rows(ple_w_proj[0], 0, 2, 0, D), 2)
                load_rows("wo0", diff_w_o[0])
                load_ffn(0)
                load_rows("gate0", ple_w_gate[0])
                u = U0["qkv1"]
                for c0 in (D, 0, HALF):
                    for j in range(2):
                        load(u, rows(swa_w_qkv[0], 4 * j, 4, c0, HALF), 4)
                        u += 1
                load(U0["pp1"], rows(ple_w_proj[1], 0, 2, 0, D), 2)
                load_rows("wo1", swa_w_o[0])
                load_ffn(1)
                load_rows("gate1", ple_w_gate[1])
                w = w_in_2[0]
                c_qa, c_ka, c_va = 0, 768, 1536
                c_qb, c_kb, c_vb, c_gl = 2304, 2816, 3328, 3840
                for kind, j, u, nb in IN2:
                    c0 = {"qb": c_qb, "kb": c_kb, "vb": c_vb, "qa": c_qa, "ka": c_ka, "va0": c_va,
                          "va1": c_va + HALF, "gl": c_gl}[kind]
                    if kind in ("vb", "va0"):
                        for i in range(2):
                            load(u + i, rows(w, 4 * i, 4, c0, HALF), 4)
                    else:
                        load(u, rows(w, 0, KD, c0 + 256 * j, 256), KD)
                for j in range(2):
                    load(U0["sbup"] + j, rows(w_up_sb_2[0], 0, 4, HALF * j, HALF), 4)
                load(U0["dilup"], rows(w_up_dil_2[0], 0, 2, 0, D), 2)
                load_rows("wout", w_out_2[0])
                u0 = U0["mlp"]
                up = w_mlp_in_2[0].rearrange("(k p) n -> p k n", p=P)
                down = w_mlp_out_2[0].rearrange("(g k p) n -> g p k n", k=2, p=P)
                load(u0, up[:, :, 0:256], KD)

                def mlp_units(it):
                    load(u0 + 2 * it - 1, up[:, :, 256 * it:256 * (it + 1)], KD)
                    load(u0 + 2 * it, rows(w_mlp_out_2[0], 2 * (it - 1), 2, 0, D), 2)

                mlp_units(1)
                with sp.Fori(0, 12 // MLP_TURN) as i:
                    up_at = [sp.snap(i * (256 * MLP_TURN) + 256 * (2 + n)) for n in range(MLP_TURN)]
                    down_at = [sp.snap(i * MLP_TURN + (1 + n)) for n in range(MLP_TURN)]
                    for n in range(MLP_TURN):
                        u = u0 + 2 * (2 + n) - 1
                        load(u, up[:, :, bass.ds(up_at[n], 256)], KD, i)
                        load(u + 1, down[bass.ds(down_at[n], 1)].rearrange("g p k n -> p (g k) n"), 2, i)
                mlp_units(14)
                mlp_units(15)
                load(u0 + 31, rows(w_mlp_out_2[0], 30, 2, 0, D), 2)
                for t in range(T):
                    sp.wait_ge(out_dve, t + 1)
                    sp.dma_start(out[0, t * P:(t + 1) * P, 0:HALF], xn[:, t, 0:HALF]).then_inc(stored, 16)
                sp.wait_ge(stored, 16 * 2 * T)

            @block.gpsimd
            def _(pool):
                steps = [0]

                def settle(ins):
                    steps[0] += 1
                    ins.then_inc(pool_step, 1)
                    pool.wait_ge(pool_step, steps[0])

                pool.memset(ones[:, :], 1.0).then_inc(ones_set, 1)
                pool.memset(zerob[:, :], 0.0).then_inc(zeros_set, 1)
                pool.memset(minus1, -1.0)
                settle(pool.memset(nhalf, -0.5))

                def norm_rstd(n):
                    for t in range(T):
                        c = 2 * n + t
                        r = rstd[:, c:c + 1]
                        pool.wait_ge(sumsq_ready, c + 1)
                        settle(pool.tensor_scalar(r, ss[:, c:c + 1], 1.0 / D, EPS, ALU.mult, ALU.add))
                        pool.tensor_tensor(r, r, nhalf[:, 0:1], ALU.pow).then_inc(rstd_ready, 1)
                        if n in (1, 4):
                            pool.wait_ge(ident_loaded, 16)
                            pool.wait_ge(rstd_ready, c + 1)
                            pool.tensor_scalar(diag[:, t, :], ident, r, None, ALU.mult).then_inc(diag_ready, 1)
                        if n == 7:
                            pool.wait_ge(rstd_ready, c + 1)
                            pool.tensor_tensor(r2[:, t:t + 1], r, r, ALU.mult).then_inc(r2_ready, 1)

                def rope_add(c, t, w):
                    pool.wait_ge(rope_read, 2 * c + t + 1)
                    pool.tensor_tensor(rotA[:, t, 0:w], rotA[:, t, 0:w], rotB[:, t, 0:w], ALU.add).then_inc(rope_ready, 1)

                def o_rstd(st, qt):
                    pool.wait_ge(o_read, 8 * st + 4 * qt + 4)
                    settle(pool.tensor_scalar(ors[:, st, qt, :], oss[:, st, qt, :], 1.0 / P, EPS, ALU.mult, ALU.add))
                    pool.tensor_tensor(ors[:, st, qt, :], ors[:, st, qt, :], nhalf[:, 0:4], ALU.pow)\
                        .then_inc(orstd_ready, 1)

                def split_lo(u, i=None):
                    pool.wait_ge(hi_ready, at(u + 1, TURN, i))
                    pool.tensor_tensor(wlo[:, u % RING, :], raw[:, u % RAW, :], whi[:, u % RING, :].bitcast(F32),
                                       ALU.subtract).then_inc(lo_pool, 1)

                def split_ffn(l):
                    u0 = U0[f"ffn{l}"]
                    split_lo(u0 + 4)
                    with pool.Fori(0, 8 // FFN_TURN) as i:
                        for n in range(FFN_TURN):
                            split_lo(u0 + 7 + 3 * n, i)
                    split_lo(u0 + 30)
                    split_lo(u0 + 32)
                    split_lo(u0 + 34)

                norm_rstd(0)
                for c in range(2):
                    for t in range(T):
                        rope_add(c, t, HALF)
                rope_add(2, 0, HALF)
                rope_add(2, 1, HALF)
                o_rstd(0, 0)
                rope_add(3, 0, HALF)
                o_rstd(0, 1)
                rope_add(3, 1, HALF)
                o_rstd(1, 0)
                o_rstd(1, 1)

                def gate_product(l):
                    pool.wait_ge(pp_ready, 4 * l + 4)
                    for b in range(3):
                        t, cols = b // 2, slice(b % 2 * HALF, (b % 2 + 1) * HALF)
                        pool.wait_ge(gate_ready, 4 * l + b + 1)
                        pool.tensor_tensor(xn[:, t, cols], xn[:, t, cols], pp[:, t, cols], ALU.mult).then_inc(prodp_ready, 1)

                split_lo(U0["ffn0"] + 1)
                norm_rstd(1)
                split_ffn(0)
                norm_rstd(2)
                gate_product(0)
                norm_rstd(3)
                for c, w in ((4, 256), (5, HALF)):
                    for t in range(T):
                        rope_add(c, t, w)

                def sink_arg(s):
                    g, qt, r, i = SWA_BLOCKS[s]
                    hd = 8 * g + 4 * r + i
                    pool.wait_ge(max_ready, S_AT["1"] + s + 1)
                    pool.tensor_tensor(sinkd[:, s], nmax1[:, s], sinks[:, hd:hd + 2], ALU.add).then_inc(sinkarg_ready, 1)

                sink_arg(0)
                for s in range(2 * N_A):
                    if s + 1 < 2 * N_A:
                        sink_arg(s + 1)
                    pool.wait_ge(exp_ready, S_AT["1"] + s + 1)
                    pool.wait_ge(sinkexp_ready, s + 1)
                    settle(pool.tensor_tensor(esum1[:, s], esum1[:, s], sinkd[:, s], ALU.add))
                    pool.tensor_tensor(rsum1[:, s], esum1[:, s], minus1, ALU.pow).then_inc(sum_ready, 1)
                    if s in (1, 3):
                        rope_add(6, s // 2, HALF)
                split_lo(U0["ffn1"] + 1)
                norm_rstd(4)
                split_ffn(1)
                norm_rstd(5)
                gate_product(1)
                norm_rstd(6)
                for t in range(T):
                    r, v = rstd[:, 12 + t:13 + t], rtmp[:, t:t + 1]
                    pool.wait_ge(rstd_ready, 13 + t)
                    pool.wait_ge(sumsqg_ready, t + 1)
                    settle(pool.tensor_scalar(v, ssg[:, t:t + 1], r, r, ALU.mult, ALU.mult))
                    settle(pool.tensor_scalar(v, v, 1.0 / D, EPS, ALU.mult, ALU.add))
                    settle(pool.tensor_tensor(v, v, nhalf[:, 0:1], ALU.pow))
                    pool.tensor_tensor(rboth[:, t:t + 1], v, r, ALU.mult).then_inc(rboth_ready, 1)
                    pool.wait_ge(rboth_ready, t + 1)
                    pool.tensor_scalar(diag[:, t, :], ident, rboth[:, t:t + 1], None, ALU.mult).then_inc(diag_ready, 1)
                for s, (pr, qt) in enumerate(SB_BLOCKS):
                    nk = P * (qt + 1)
                    pool.wait_ge(sb_l, s + 1)
                    for buf, fill in ((sbm, 1.0), (sbp, 0.0)):
                        v = buf[:, 0:2 * nk].rearrange("p (j c) -> p j c", j=2)[:, :, nk - P:nk]
                        pool.affine_select(out=v, in_=v, compare_op=ALU.is_gt, fill=fill, base=0,
                                           pattern=[[0, 2], [-1, P]], channel_multiplier=1).then_inc(sb_sel, 1)
                norm_rstd(7)
                for t in range(T):
                    pool.wait_ge(sumsq_ready, 16 + 2 * t + 2)
                    r = rstd[:, 16 + t:17 + t]
                    settle(pool.tensor_tensor(r, ssl[:, 2 * t:2 * t + 1], ssl[:, 2 * t + 1:2 * t + 2], ALU.add))
                    settle(pool.tensor_scalar(r, r, 1.0 / D, EPS, ALU.mult, ALU.add))
                    pool.tensor_tensor(r, r, nhalf[:, 0:1], ALU.pow).then_inc(rstd_ready, 1)

            @block.scalar
            def _(act):
                split = [0]
                tcount = [0]

                def split_hi(u, i=None):
                    act.wait_ge(raw_full[u % RAW], at(16 * (u // RAW + 1), 16 * TURN // RAW, i))
                    if u >= RING:
                        act.wait_ge(weights_used, at(u - RING + 1, TURN, i))
                    act.activation(whi[:, u % RING, :], raw[:, u % RAW, :], ACT.Copy).then_inc(hi_ready, 1)

                half = [0]

                def split_half(count=1):
                    for _ in range(count):
                        u, a = split[0], half[0]
                        cols = slice(a * UNIT // 2, (a + 1) * UNIT // 2)
                        if a == 0:
                            act.wait_ge(raw_full[u % RAW], 16 * (u // RAW + 1))
                            act.wait_ge(weights_used, u - RING + 1)
                        ins = act.activation(whi[:, u % RING, cols], raw[:, u % RAW, cols], ACT.Copy)
                        ins.then_inc(hi_ready if a else hi_half, 1)
                        split[0] += a
                        half[0] = 1 - a

                def ahead(u):
                    if half[0]:
                        split_half()
                    while split[0] < min(u + RING, NU):
                        split_hi(split[0])
                        split[0] += 1

                def keep_ahead(u, i):
                    if i is None:
                        ahead(u)
                    else:
                        split_hi(u + RING - 1, i)

                def copy_T(dst, src, scale=1.0):
                    act.wait_ge(t_ready, tcount[0] + 1)
                    if scale == 1.0:
                        act.activation(dst, src, ACT.Copy).then_inc(t_free, 1)
                    else:
                        act.activation(dst, src, ACT.Copy, scale=scale).then_inc(t_free, 1)
                    tcount[0] += 1

                def tile_done(name, u, t):
                    if t == 0:
                        act.wait_ge(tile0_done, TM[name])
                    else:
                        act.wait_ge(weights_used, u + 1)

                def preload(n, func):
                    act.activation(warm[:, n:n + 1], nhalf[:, 0:1], func)

                def norm_hi(n, t, hf):
                    for b in (2 * hf, 2 * hf + 1):
                        act.wait_ge(xT_ready, KD * n + 4 * t + b + 1)
                        for k in (2 * b, 2 * b + 1):
                            g = GAIN[n] + k
                            act.activation(xhi[:, k, t * P:(t + 1) * P],
                                           ps[:, 4 + b, (k % 2) * SEQ + t * P:(k % 2) * SEQ + (t + 1) * P],
                                           ACT.Identity, scale=vecT[:, g:g + 1]).then_inc(xhi_ready, 1)

                def norm_sumsq(n, t):
                    if n == 0:
                        act.wait_ge(h_loaded[t], 16)
                    else:
                        act.wait_ge(h_ready, 4 * (n - 1) + 2 * t + 2)
                    c = 2 * n + t
                    act.activation(xn[:, t, :], h[:, t, :], ACT.Square, accum_out=ss[:, c:c + 1]).then_inc(sumsq_ready, 1)

                def boundary(n):
                    norm_hi(n, 0, 0)
                    norm_hi(n, 0, 1)
                    norm_sumsq(n, 0)
                    norm_hi(n, 1, 0)
                    norm_hi(n, 1, 1)
                    norm_sumsq(n, 1)

                def rms_row(n):
                    act.wait_ge(rB_T, n + 1)
                    act.activation(rB[:, :], ps[:, (0, 0, 7)[n], 0:SEQ], ACT.Copy).then_inc(rB_ready, 1)
                    if n == 2:
                        act.activation(rBq[:, :], ps[:, 7, 0:SEQ], ACT.Copy, scale=0.125).then_inc(rB_ready, 1)

                def ple_proj(l, hf):
                    u = U0[f"pp{l}"]
                    if hf == 0:
                        act.wait_ge(tile0_done, TM[f"pp{l}"])
                    else:
                        act.wait_ge(weights_used, u + 1)
                    for t in range(T):
                        act.activation(pp[:, t, hf * HALF:(hf + 1) * HALF], ps[:, PP_BANK[l][hf] + t, :], ACT.Copy)\
                            .then_inc(pp_ready, 1)

                def res_done(name, u, t, hf):
                    if 2 * t + hf < 3:
                        act.wait_ge(bank_done, 3 * RES_ORDER.index(name) + 2 * t + hf + 1)
                    else:
                        act.wait_ge(weights_used, u + 1)

                def gate(l, after):
                    n = 3 + 3 * l

                    def bank(t, hf):
                        c = 2 * (n - 1) + t
                        act.wait_ge(rstd_ready, c + 1)
                        res_done(f"gate{l}", U0[f"gate{l}"] + 3, t, hf)
                        act.activation(xn[:, t, hf * HALF:(hf + 1) * HALF], ps[:, 2 * t + hf, :], ACT.Sigmoid,
                                       scale=rstd[:, c:c + 1]).then_inc(gate_ready, 1)

                    bank(0, 0)
                    bank(0, 1)
                    norm_hi(n, 0, 0)
                    bank(1, 0)
                    norm_hi(n, 0, 1)
                    bank(1, 1)
                    ahead(after)
                    norm_hi(n, 1, 0)
                    norm_hi(n, 1, 1)
                    norm_sumsq(n, 0)
                    norm_sumsq(n, 1)

                def ffn(l):
                    u0 = U0[f"ffn{l}"]

                    def mid(it, gv, buf, i=None):
                        act.wait_ge(scaled[l], at(2 * it + gv + 1, 2 * FFN_TURN, i))
                        for j in range(2):
                            m = column(2 * it + j + FT * gv, i)
                            ins = act.activation(cgv[:, buf, gv, j * SEQ:(j + 1) * SEQ], usc[:, buf, gv, j * SEQ:(j + 1) * SEQ],
                                                 ACT.Identity, scale=cwT[:, l, 1, m], bias=cwT[:, l, 3, m])
                        ins.then_inc(mid_ready[l], 1)

                    def silu(buf, wait):
                        act.wait_ge(conv_done[l], wait)
                        act.activation(sgl[:, buf, :], cgv[:, buf, 0, :], ACT.Silu).then_inc(silu_ready[l], 1)

                    def hidden_hi(buf, wait):
                        act.wait_ge(hid_ready[l], wait)
                        act.activation(ohi[:, 2 * buf:2 * buf + 2, :].rearrange("p a c -> p (a c)"), hid[:, buf, :],
                                       ACT.Copy).then_inc(hhi_ready[l], 1)

                    def iteration(it, i=None, ug=None, after=None):
                        buf = it % 2
                        ug = u0 + 3 * it - 1 if ug is None else ug
                        for gv in range(2):
                            keep_ahead(ug + gv, i)
                            mid(it, gv, buf, i)
                        silu(buf, at(2 * it + 1, 2 * FFN_TURN, i))
                        if after is None:
                            keep_ahead(ug + 2, i)
                        else:
                            act.wait_ge(weights_used, after)
                        hidden_hi(buf, at(it + 1, FFN_TURN, i))

                    ahead(u0)
                    rms_row(l)
                    preload(2 * l, ACT.Silu)
                    mid(0, 0, 0)
                    ahead(u0 + 1)
                    mid(0, 1, 0)
                    silu(0, 1)
                    hidden_hi(0, 1)
                    with act.Fori(0, 8 // FFN_TURN) as i:
                        for n in range(FFN_TURN):
                            iteration(1 + n, i)
                    split[0] = u0 + 25 + RING
                    iteration(9, None, u0 + 26)
                    iteration(10, None, u0 + 28, u0 + 31)
                    ahead(u0 + 30)
                    ahead(u0 + 31)

                def block_exp(lset, s, nm, es):
                    act.wait_ge(max_ready, S_AT[lset] + s + 1)
                    for j in range(2):
                        ins = act.activation(Eb[:, s % 2, j, :], ps[:, 6 + s % 2, j * SEQ:(j + 1) * SEQ], ACT.Exp,
                                             bias=nm[:, j:j + 1], scale=1.0, accum_out=es[:, j:j + 1])
                    ins.then_inc(exp_ready, 1)

                def o_copy0(st, s):
                    qt, i = BLOCKS[s]
                    b = 8 * st + s
                    act.wait_ge(o_ready, b + 1)
                    c = (4 * st + i) * P
                    act.activation(junk, ps[:, OB, 0:P], ACT.Square, scale=rsum[:, b, 0:1],
                                   accum_out=oss[:, st, qt, i:i + 1])
                    act.activation(xn[:, qt, c:c + P], ps[:, OB, 0:P], ACT.Identity, scale=rsum[:, b, 0:1])\
                        .then_inc(o_read, 1)

                act.wait_ge(ones_set, 1)
                act.activation(warm[:, 6:7], ones[:, 0:1], ACT.Identity)
                act.wait_ge(gain0_ready, 1)
                for hf in range(2):
                    norm_hi(0, 0, hf)
                for a, (loaded, done) in enumerate(((first_half, hi_half), (raw_full[0], hi_ready))):
                    act.wait_ge(loaded, 16)
                    cols = slice(a * UNIT // 2, (a + 1) * UNIT // 2)
                    act.activation(whi[:, 0, cols], raw[:, 0, cols], ACT.Copy).then_inc(done, 1)
                split[0] = 1
                norm_sumsq(0, 0)
                for hf in range(2):
                    norm_hi(0, 1, hf)
                ahead(-2)
                norm_sumsq(0, 1)
                ahead(-1)
                ahead(0)
                act.wait_ge(trig_arg, 1)
                act.activation(trg[:, 0, :], trg[:, 0, :], ACT.Sin).then_inc(trig_ready, 1)
                act.wait_ge(lam_sums, 1)
                act.activation(lam2, lam2, ACT.Exp).then_inc(lam_exps, 1)
                u = U0["qkv0"]
                for b in range(2):
                    act.wait_ge(pT_ready, b + 1)
                    act.activation(phi[:, 2 * b:2 * b + 2, :].rearrange("p a c -> p (a c)"), ps[:, 6 + b, :], ACT.Copy)\
                        .then_inc(phi_ready, 1)
                for j in (1, 2, 3):
                    ahead(u + j)

                def copy_qk(dst, tiles, t, scale):
                    copy_T(dst[:, tiles, t * P:(t + 1) * P], ps[:, TB, :].rearrange("p (a c) -> p a c", c=P)[:, 0:tiles.stop - tiles.start, :], scale)

                def v_copy(c, name, u, banks):
                    for t in range(T):
                        tile_done(name, u, t)
                        act.activation(vtm[:, t, c:c + HALF], ps[:, banks + t, :], ACT.Copy, scale=rstd[:, t:t + 1])\
                            .then_inc(v_ready, 1)

                for t in range(T):
                    copy_qk(qT, slice(0, 4), t, 0.125)
                ahead(u + 4)
                ahead(u + 5)
                for t in range(T):
                    copy_qk(kT, slice(0, 4), t, 1.0)
                act.wait_ge(rstd_ready, 2)
                v_copy(0, "qkv0.2", u + 5, 0)

                def at_copy0(s):
                    copy_T(ATd[:, s % 2].rearrange("p k c -> p (k c)"), ps[:, TB, 0:2 * P])

                def o_hi(first, nt, count, qt, scaled):
                    act.wait_ge(oT_ready, count + 1)
                    src = ps[:, TB, 0:nt * P].rearrange("p (a c) -> p a c", c=P)
                    dst = ohi[:, first:first + nt, qt * P:(qt + 1) * P]
                    if scaled:
                        act.activation(dst, src, ACT.Identity, scale=subg).then_inc(ohi_ready, 1)
                    else:
                        act.activation(dst, src, ACT.Copy).then_inc(ohi_ready, 1)

                block_exp("A", 0, nmax[:, 0], esum[:, 0])
                for s in range(N_A):
                    if s + 1 < N_A:
                        block_exp("A", s + 1, nmax[:, s + 1], esum[:, s + 1])
                    at_copy0(s)
                    split_half()
                    if s in (5, 6):
                        copy_qk(qT, slice(4, 8), s - 5, 0.125)
                    if s == 7:
                        o_hi(0, 4, 0, 0, True)
                    if s:
                        o_copy0(0, s - 1)
                o_copy0(0, N_A - 1)
                split_half()
                copy_qk(kT, slice(4, 8), 0, 1.0)
                split_half()
                copy_qk(kT, slice(4, 8), 1, 1.0)
                o_hi(0, 4, 1, 1, True)
                block_exp("B", 0, nmax[:, 8], esum[:, 8])
                v_copy(HALF, "qkv0.5", u + 11, 2)
                for s in range(N_A):
                    if s + 1 < N_A:
                        block_exp("B", s + 1, nmax[:, 9 + s], esum[:, 9 + s])
                    at_copy0(s)
                    if s < 6:
                        split_half()
                    if s:
                        o_copy0(1, s - 1)
                    if s in (1, 3):
                        ple_proj(0, s // 2)
                o_copy0(1, N_A - 1)
                o_hi(4, 4, 2, 0, True)
                split_half()
                o_hi(4, 4, 3, 1, True)
                ahead(U0["wo0"] + 2)
                boundary(1)
                ahead(U0["wo0"] + 3)
                ffn(0)
                boundary(2)
                ahead(U0["ffn0"] + 32)
                ahead(U0["gate0"])
                preload(1, ACT.Sigmoid)
                for j in (1, 2):
                    ahead(U0["gate0"] + j)
                gate(0, U0["qkv1"] - 1)

                u = U0["qkv1"]
                for j in (0, 1):
                    ahead(u + j)
                preload(5, ACT.Exp)
                copy_qk(kT, slice(0, 2), 0, 1.0)
                ahead(u + 2)
                copy_qk(kT, slice(0, 2), 1, 1.0)
                for t in range(T):
                    copy_qk(qT, slice(0, 4), t, 0.125)
                ahead(u + 3)

                def swa_exp(s):
                    act.wait_ge(max_ready, S_AT["1"] + s + 1)
                    for j in range(2):
                        ins = act.activation(Eb[:, s % 2, j, :], ps[:, 6 + s % 2, j * SEQ:(j + 1) * SEQ], ACT.Exp,
                                             bias=nmax1[:, s, j:j + 1], scale=1.0, accum_out=esum1[:, s, j:j + 1])
                    ins.then_inc(exp_ready, 1)

                def sink_exp(s):
                    act.wait_ge(sinkarg_ready, s + 1)
                    act.activation(sinkd[:, s], sinkd[:, s], ACT.Exp).then_inc(sinkexp_ready, 1)

                swa_exp(0)
                sink_exp(0)
                for s in range(2 * N_A):
                    if s + 1 < 2 * N_A:
                        swa_exp(s + 1)
                    copy_T(ATs[:, s % 2].rearrange("p k c -> p (k c)"), ps[:, TB, :])
                    if s in (5, 9, 13):
                        o_hi(*((0, 4, 4, 0), (0, 4, 5, 1), (4, 4, 6, 0))[(s - 5) // 4], False)
                    if s + 1 < 2 * N_A:
                        sink_exp(s + 1)
                    if s in (4, 6):
                        copy_qk(qT, slice(4, 8), s // 2 - 2, 0.125)
                    if s in (4, 6):
                        ple_proj(1, s // 2 - 2)
                    if s % 4 in (0, 1):
                        split_half()
                o_hi(4, 4, 7, 1, False)
                ahead(U0["wo1"] + 2)
                act.dma_start(gmid, final_norm.partition_broadcast(P)).then_inc(gmid_loaded, 16)
                boundary(4)
                ahead(U0["wo1"] + 3)
                ffn(1)
                boundary(5)
                ahead(U0["ffn1"] + 32)
                ahead(U0["gate1"])
                preload(3, ACT.Sigmoid)
                for j in (1, 2):
                    ahead(U0["gate1"] + j)
                gate(1, U0["in2"] - 1)

                ahead(U0["in2"])
                for t in range(T):
                    act.wait_ge(hg_ready, t + 1)
                    act.wait_ge(sumsq_ready, 13 + t)
                    act.activation(xn[:, t, :], hg[:, t, :], ACT.Square, accum_out=ssg[:, t:t + 1]).then_inc(sumsqg_ready, 1)
                ahead(U0["in2"] + 1)
                rms_row(2)

                def sb_sigmoids(s):
                    pr, qt = SB_BLOCKS[s]
                    nk = P * (qt + 1)
                    act.wait_ge(s_ready, S_AT["S"] + s + 1)
                    for buf, sign in ((sbm, -1.0), (sbp, 1.0)):
                        ins = act.activation(buf[:, 0:2 * nk].rearrange("p (j c) -> p j c", j=2), ps[:, 6:8, 0:nk],
                                             ACT.Sigmoid, scale=sign)
                    ins.then_inc(sb_l, 1)

                def sb_copy(s):
                    pr, qt = SB_BLOCKS[s]
                    n = 2 * (qt + 1) * P
                    copy_T(ETs[:, 0:n], ps[:, TB, 0:n])

                def dil_exp(s):
                    j, qt = DIL_BLOCKS[s]
                    n = 3 * (qt + 1) * P
                    act.wait_ge(max_ready, MAX2 + s + 1)
                    act.activation(dlL[:, s % 2, 0:n], dlL[:, s % 2, 0:n], ACT.Exp, bias=nmax2[:, s:s + 1], scale=1.0,
                                   accum_out=esum2[:, s:s + 1]).then_inc(exp_ready, 1)

                def dil_copy(s):
                    j, qt = DIL_BLOCKS[s]
                    if qt:
                        copy_T(ETb[:, 0:HALF], ps[:, TB, :])
                        copy_T(ETb[:, HALF:HALF + 256], ps[:, TB, 0:256])
                    else:
                        copy_T(ETb[:, 0:3 * P], ps[:, TB, 0:3 * P])

                def gates(v, m0, tiles=range(8)):
                    for m in tiles:
                        c = V_BGATE + m0 + m
                        ins = act.activation(v[:, m, :], v[:, m, :], ACT.Sigmoid, bias=vecT[:, c:c + 1], scale=1.0)
                        if m % 2:
                            ins.then_inc(gates_ready, 1)

                MAX2 = 32
                for n in range(1, 5):
                    ahead(IN2[n][2])
                for s in range(9):
                    if s:
                        sb_copy(s - 1)
                    if s < 8:
                        sb_sigmoids(s)
                    if s == 7:
                        o_hi(0, 4, 8, 0, False)
                    ahead(IN2[5 + s][2])
                o_hi(0, 4, 9, 1, False)
                preload(4, ACT.Exp)
                for s in range(9):
                    if s:
                        dil_copy(s - 1)
                    if s < 8:
                        dil_exp(s)
                    if s == 7:
                        o_hi(4, 2, 10, 0, False)
                    ahead(U0["gl2"] + 1 + s)
                preload(7, ACT.Sigmoid)
                o_hi(4, 2, 11, 1, False)
                act.wait_ge(in2_read, in2_count[-1])
                gates(gb, 8)
                gates(ga, 0, range(6))
                for j in range(4):
                    if j == 1:
                        gates(ga, 0, range(6, 8))
                    act.wait_ge(merged, j + 1)
                    act.activation(xhi[:, 2 * j:2 * j + 2, :].rearrange("p a c -> p (a c)"), mB[:, j, :], ACT.Copy)\
                        .then_inc(mhi_ready, 1)
                ahead(U0["dilup"])
                for j in range(3):
                    ahead(U0["wout"] + j)
                act.wait_ge(mlo_ready, 4)
                act.dma_start(gfin, norm_final_g_2.partition_broadcast(P)).then_inc(gfin_loaded, 16)
                boundary(7)
                ahead(U0["wout"] + 3)
                ahead(U0["mlp"])
                u0 = U0["mlp"]

                def relu_hi(it, i=None):
                    b = it % 3
                    act.wait_ge(weights_used, at(u0 + 2 * it if it else u0 + 1, TURN, i))
                    act.activation(rel[:, b, :], ps[:, 4 + b, :], ACT.Relu).then_inc(relu_ready, 1)
                    act.wait_ge(relu_ready, at(it + 1, MLP_TURN, i))
                    act.activation(ohi[:, 2 * b:2 * b + 2, :].rearrange("p a c -> p (a c)"), rel[:, b, :], ACT.Square)\
                        .then_inc(rhi_ready, 1)

                def mlp_iteration(it, i=None):
                    keep_ahead(u0 + 2 * it - 1, i)
                    relu_hi(it, i)
                    keep_ahead(u0 + 2 * it, i)

                relu_hi(0)
                mlp_iteration(1)
                with act.Fori(0, 12 // MLP_TURN) as i:
                    for n in range(MLP_TURN):
                        mlp_iteration(2 + n, i)
                split[0] = u0 + 27 + RING - 1
                mlp_iteration(14)
                mlp_iteration(15)

                def last_squares(t, hf):
                    act.wait_ge(h_ready, 4 * 7 + 2 * t + hf + 1)
                    cols = slice(hf * HALF, (hf + 1) * HALF)
                    act.activation(xn[:, t, cols], h[:, t, cols], ACT.Square, accum_out=ssl[:, 2 * t + hf:2 * t + hf + 1])\
                        .then_inc(sumsq_ready, 1)

                def last_half(t):
                    act.wait_ge(rstd_ready, 17 + t)
                    act.wait_ge(gained, 2 * t + 2)
                    act.activation(xn[:, t, HALF:D], pp[:, t, HALF:D], ACT.Copy, scale=rstd[:, 16 + t:17 + t]).then_inc(out_act, 1)
                    act.wait_ge(out_act, t + 1)
                    act.dma_start(out[0, t * P:(t + 1) * P, HALF:D], xn[:, t, HALF:D]).then_inc(stored, 16)

                last_squares(0, 0)
                last_squares(0, 1)
                last_squares(1, 0)
                last_half(0)
                last_squares(1, 1)
                last_half(1)

            @block.vector
            def _(dve):
                split = [0]
                steps = [0]

                def settle(ins):
                    steps[0] += 1
                    ins.then_inc(dve_step, 1)
                    dve.wait_ge(dve_step, steps[0])

                def split_lo(u, i=None):
                    dve.wait_ge(hi_ready, at(u + 1, TURN, i))
                    dve.tensor_tensor(wlo[:, u % RING, :], raw[:, u % RAW, :], whi[:, u % RING, :].bitcast(F32),
                                      ALU.subtract).then_inc(lo_ready, 1)

                half, halved = [0], [0]

                def split_half(count=1):
                    for _ in range(count):
                        u, a = split[0], half[0]
                        assert u not in POOL_UNITS
                        cols = slice(a * UNIT // 2, (a + 1) * UNIT // 2)
                        if a:
                            dve.wait_ge(hi_ready, u + 1)
                        else:
                            halved[0] += 1
                            dve.wait_ge(hi_half, halved[0])
                        ins = dve.tensor_tensor(wlo[:, u % RING, cols], raw[:, u % RAW, cols], whi[:, u % RING, cols].bitcast(F32),
                                                ALU.subtract)
                        if a:
                            ins.then_inc(lo_ready, 1)
                        elif u == 0:
                            ins.then_inc(first_lo, 1)
                        split[0] += a
                        half[0] = 1 - a

                def ahead(u):
                    if half[0]:
                        split_half()
                    while split[0] < min(u + RING, NU):
                        if split[0] not in POOL_UNITS:
                            split_lo(split[0])
                        split[0] += 1

                def keep_ahead(u, i):
                    if i is None:
                        ahead(u)
                    elif u + RING - 1 not in POOL_UNITS:
                        split_lo(u + RING - 1, i)

                def tile_done(name, u, t):
                    if t == 0:
                        dve.wait_ge(tile0_done, TM[name])
                    else:
                        dve.wait_ge(weights_used, u + 1)

                def res_done(name, u, t, hf):
                    if 2 * t + hf < 3:
                        dve.wait_ge(bank_done, 3 * RES_ORDER.index(name) + 2 * t + hf + 1)
                    else:
                        dve.wait_ge(weights_used, u + 1)

                def residual(name, u, t, hf):
                    res_done(name, u, t, hf)
                    v = h[:, t, hf * HALF:(hf + 1) * HALF]
                    dve.tensor_tensor(v, ps[:, 2 * t + hf, :], v, ALU.add).then_inc(h_ready, 1)

                def norm_lo(n, t, hf):
                    for b in (2 * hf, 2 * hf + 1):
                        dve.wait_ge(xhi_ready, 2 * KD * n + KD * t + 2 * b + 2)
                        for k in (2 * b, 2 * b + 1):
                            g = GAIN[n] + k
                            c = (k % 2) * SEQ + t * P
                            dve.scalar_tensor_tensor(xlo[:, k, t * P:(t + 1) * P], ps[:, 4 + b, c:c + P], vecT[:, g:g + 1],
                                                     xhi[:, k, t * P:(t + 1) * P].bitcast(F32), ALU.mult, ALU.subtract)\
                                .then_inc(xlo_ready, 1)

                def boundary(add, n, units=(), first=(), second=()):
                    add(0, 0)
                    for u in first:
                        ahead(u)
                    add(0, 1)
                    for u in second:
                        ahead(u)
                    norm_lo(n, 0, 0)
                    add(1, 0)
                    norm_lo(n, 0, 1)
                    if not units:
                        norm_lo(n, 1, 0)
                    add(1, 1)
                    if units:
                        norm_lo(n, 1, 0)
                        for u in units:
                            ahead(u)
                    norm_lo(n, 1, 1)

                def rotary(n):
                    for t in range(T):
                        c = 2 * n + t
                        dve.wait_ge(rstd_ready, c + 1)
                        dve.tensor_scalar(cosr[:, t, :], cosd[:, t, :], rstd[:, c:c + 1], None, ALU.mult)
                        ins = dve.tensor_scalar(sinr[:, t, :], sind[:, t, :], rstd[:, c:c + 1], None, ALU.mult)
                    settle(ins)

                def rope_mul(c, t, name, u, bank, heads):
                    w = heads * HD
                    tile_done(name, u, t)
                    if c:
                        dve.wait_ge(t_ready, ROPE_T[c - 1] + t + 1)
                    src = ps[:, bank + t, 0:w]
                    n = 1 if heads == 4 or name[3] == "0" else 2
                    i = heads // n
                    per_head = lambda v: v.rearrange("p (a i d) -> p a i d", a=n, d=HD)
                    paired = lambda v: v.rearrange("p (i a d) -> p a i d", a=n, d=HD)
                    wide = lambda v: v.unsqueeze(1).unsqueeze(1).broadcast_to([P, n, i, v.shape[-1]])
                    dve.tensor_tensor(paired(rotA[:, t, 0:w]), per_head(src), wide(cosr[:, t, :]), ALU.mult)
                    for hf in range(2):
                        a = hf * HD // 2
                        b = HD // 2 - a
                        ins = dve.tensor_tensor(paired(rotB[:, t, 0:w])[:, :, :, a:a + HD // 2],
                                                per_head(src)[:, :, :, b:b + HD // 2],
                                                wide(sinr[:, t, a:a + HD // 2]), ALU.mult)
                    if name == "qkv1.0":
                        ins = dve.tensor_scalar(vtm[:, t, 0:256], ps[:, bank + t, 256:512], rstd[:, 6 + t:7 + t], None, ALU.mult)
                    ins.then_inc(rope_read, 1)

                ROPE_T = [T_USE[n] for n in ("0q00", "0k00", "0q10", "0k10", "1k0", "1q00", "1q10")]

                def gate(l, t, hf):
                    cols = slice(hf * HALF, (hf + 1) * HALF)
                    if 2 * t + hf < 3:
                        dve.wait_ge(prodp_ready, 3 * l + 2 * t + hf + 1)
                    else:
                        dve.wait_ge(gate_ready, 4 * l + 4)
                        dve.tensor_tensor(xn[:, t, cols], xn[:, t, cols], pp[:, t, cols], ALU.mult).then_inc(prod_ready, 1)
                        dve.wait_ge(prod_ready, l + 1)
                    dve.tensor_tensor(h[:, t, cols], h[:, t, cols], xn[:, t, cols], ALU.add).then_inc(h_ready, 1)

                def ffn(l):
                    u0 = U0[f"ffn{l}"]

                    def taps(it, gv, i=None, ug=None):
                        buf = it % 2
                        bank = 4 + 2 * buf + gv
                        ug = u0 if ug is None else ug
                        dve.wait_ge(weights_used, at(ug + gv + 1, TURN, i))
                        dve.tensor_tensor(usc[:, buf, gv, :].rearrange("p (j c) -> p j c", j=2),
                                          ps[:, bank, :].rearrange("p (j c) -> p j c", j=2),
                                          rB[:, :].unsqueeze(1).broadcast_to([P, 2, SEQ]), ALU.mult).then_inc(scaled[l], 1)
                        dve.wait_ge(mid_ready[l], at(2 * it + gv + 1, 2 * FFN_TURN, i))
                        for j in range(2):
                            o = j * SEQ
                            m = column(2 * it + j + FT * gv, i)
                            v = cgv[:, buf, gv, o + 1:o + SEQ]
                            dve.scalar_tensor_tensor(v, usc[:, buf, gv, o:o + SEQ - 1], cwT[:, l, 0, m], v,
                                                     ALU.mult, ALU.add).then_inc(tap_done[l], 1)
                        for j in range(2):
                            o = j * SEQ
                            m = column(2 * it + j + FT * gv, i)
                            dve.wait_ge(tap_done[l], at(4 * it + 2 * gv + j + 1, 4 * FFN_TURN, i))
                            v = cgv[:, buf, gv, o:o + SEQ - 1]
                            ins = dve.scalar_tensor_tensor(v, usc[:, buf, gv, o + 1:o + SEQ], cwT[:, l, 2, m], v,
                                                           ALU.mult, ALU.add)
                        ins.then_inc(conv_done[l], 1)

                    def mult(buf, conv, n):
                        dve.wait_ge(conv_done[l], conv)
                        dve.wait_ge(silu_ready[l], n)
                        dve.tensor_tensor(hid[:, buf, :], sgl[:, buf, :], cgv[:, buf, 1, :], ALU.mult).then_inc(hid_ready[l], 1)

                    def hidden_lo(buf, n):
                        dve.wait_ge(hhi_ready[l], n)
                        dve.tensor_tensor(olo[:, 2 * buf:2 * buf + 2, :].rearrange("p a c -> p (a c)"), hid[:, buf, :],
                                          ohi[:, 2 * buf:2 * buf + 2, :].rearrange("p a c -> p (a c)").bitcast(F32),
                                          ALU.subtract).then_inc(hlo_ready[l], 1)

                    def iteration(it, i=None, ug=None):
                        buf = it % 2
                        straight = ug is not None
                        ug = ug if straight else u0 + 3 * it - 1
                        for gv in range(2):
                            keep_ahead(ug + gv, i)
                            taps(it, gv, i, ug)
                        mult(buf, at(2 * it + 2, 2 * FFN_TURN, i), at(it + 1, FFN_TURN, i))
                        if not straight:
                            keep_ahead(ug + 2, i)
                        hidden_lo(buf, at(it + 1, FFN_TURN, i))

                    ahead(u0)
                    dve.wait_ge(rB_ready, l + 1)
                    taps(0, 0)
                    ahead(u0 + 1)
                    taps(0, 1)
                    mult(0, 2, 1)
                    hidden_lo(0, 1)
                    with dve.Fori(0, 8 // FFN_TURN) as i:
                        for n in range(FFN_TURN):
                            iteration(1 + n, i)
                    split[0] = u0 + 25 + RING
                    iteration(9, None, u0 + 26)
                    iteration(10, None, u0 + 28)
                    ahead(u0 + 30)
                    ahead(u0 + 31)

                def block_max(lset, s, nm):
                    dve.wait_ge(s_ready, S_AT[lset] + s + 1)
                    dve.tensor_reduce(nm, ps[:, 6 + s % 2, :].rearrange("p (j c) -> p j c", j=2), AX.X, ALU.max, negate=True).then_inc(max_ready, 1)

                def block_mix(s):
                    dve.wait_ge(exp_ready, s + 1)
                    settle(dve.reciprocal(rsum[:, s], esum[:, s]))
                    settle(dve.scalar_tensor_tensor(mixc[:, s:s + 1], esum[:, s, 0:1], nlam, rsum[:, s, 1:2], ALU.mult, ALU.mult))
                    dve.scalar_tensor_tensor(Ac[:, s % 2, :], Eb[:, s % 2, 1, :], mixc[:, s:s + 1], Eb[:, s % 2, 0, :],
                                             ALU.mult, ALU.add).then_inc(mix_ready, 1)

                def o_norm(st, qt):
                    dve.wait_ge(orstd_ready, 2 * st + qt + 1)
                    v = xn[:, qt, st * HALF:(st + 1) * HALF].rearrange("p (d e) -> p d e", e=P)
                    dve.tensor_tensor(v, v, ors[:, st, qt, :].unsqueeze(2).broadcast_to([P, 4, P]), ALU.mult).then_inc(on_ready, 1)

                def o_lo(first, nt, count, qt, scaled):
                    dve.wait_ge(ohi_ready, count + 1)
                    src = ps[:, TB, 0:nt * P].rearrange("p (a c) -> p a c", c=P)
                    dst = olo[:, first:first + nt, qt * P:(qt + 1) * P]
                    hi = ohi[:, first:first + nt, qt * P:(qt + 1) * P].bitcast(F32)
                    if scaled:
                        dve.scalar_tensor_tensor(dst, src, subg, hi, ALU.mult, ALU.subtract).then_inc(olo_ready, 1)
                    else:
                        dve.tensor_tensor(dst, src, hi, ALU.subtract).then_inc(olo_ready, 1)

                dve.wait_ge(gain0_T, 1)
                dve.tensor_copy(vecT[:, V_ATTN:V_ATTN + 16], ps[:, 0, 0:16]).then_inc(gain0_ready, 1)
                dve.wait_ge(gain0_ready, 1)
                for hf in range(2):
                    norm_lo(0, 0, hf)
                split_half(2)
                for hf in range(2):
                    norm_lo(0, 1, hf)
                ahead(-2)
                ahead(-1)

                ang = trg[:, 1, 0:2 * HD // 2].rearrange("p (t f) -> p t f", t=T)
                turns = trg[:, 2, :]
                both = trg[:, 0, :].rearrange("p (a t f) -> p a t f", a=2, t=T)
                dve.wait_ge(table_loaded, 16)
                dve.wait_ge(trig_loaded, 16 * 3)
                settle(dve.tensor_copy(posf, posi[:, :]))
                for t in range(T):
                    ins = dve.tensor_scalar(ang[:, t, :], tab[:, C_FREQ:C_FREQ + HD // 2], posf[:, t:t + 1], None, ALU.mult)
                settle(ins)
                flat = ang.rearrange("p t f -> p (t f)")
                MAGIC = 1.5 * 2.0 ** 23
                pieces = (6.28125, 0.0019350051879882812, 2 * math.pi - 6.28125 - 0.0019350051879882812)
                for a in range(2):
                    arg = trg[:, 0, a * HD:(a + 1) * HD]
                    settle(dve.tensor_scalar(turns[:, 0:HD], flat, 1.0 / (2 * math.pi), 0.25 * a, ALU.mult, ALU.add))
                    settle(dve.tensor_scalar(turns[:, 0:HD], turns[:, 0:HD], MAGIC, None, ALU.add))
                    settle(dve.tensor_scalar(turns[:, 0:HD], turns[:, 0:HD], MAGIC, None, ALU.subtract))
                    src = flat
                    for c in pieces:
                        settle(dve.scalar_tensor_tensor(arg, turns[:, 0:HD], -c, src, ALU.mult, ALU.add))
                        src = arg
                    if a:
                        settle(dve.tensor_scalar(arg, arg, math.pi / 2, None, ALU.add))
                    settle(dve.tensor_scalar(arg, arg, 3.1415925, -3.1415925, ALU.min, ALU.max))
                dve.tensor_copy(turns[:, 0:2], posf).then_inc(trig_arg, 1)
                settle(dve.tensor_tensor(trg[:, 3, :].rearrange("p (a d) -> p a d", a=2), lamb[:, 0::2, :], lamb[:, 1::2, :], ALU.mult))
                dve.tensor_reduce(lam2, trg[:, 3, :].rearrange("p (a d) -> p a d", a=2), AX.X, ALU.add).then_inc(lam_sums, 1)
                dve.tensor_scalar(nsink, sinks[:, :], -1.0, None, ALU.mult)
                ahead(0)
                dve.wait_ge(trig_ready, 1)
                for t in range(T):
                    for a in range(2):
                        dve.tensor_copy(cosd[:, t, a * 32:a * 32 + 32], both[:, 1, t, :])
                        ins = dve.tensor_scalar(sind[:, t, a * 32:a * 32 + 32], both[:, 0, t, :], (-1.0, 1.0)[a], None, ALU.mult)
                settle(ins)
                dve.wait_ge(lam_exps, 1)
                settle(dve.scalar_tensor_tensor(nlam, lam2[:, 1:2], -LAM_INIT, lam2[:, 0:1], ALU.add, ALU.subtract))

                rotary(0)

                u = U0["qkv0"]
                for t in range(T):
                    rope_mul(0, t, "qkv0.0", u + 1, 0, 8)
                ahead(u + 1)
                for b in range(2):
                    dve.wait_ge(phi_ready, b + 1)
                    dve.tensor_tensor(plo[:, 2 * b:2 * b + 2, :].rearrange("p a c -> p (a c)"), ps[:, 6 + b, :],
                                      phi[:, 2 * b:2 * b + 2, :].rearrange("p a c -> p (a c)").bitcast(F32), ALU.subtract)\
                        .then_inc(plo_ready, 1)
                dve.tensor_copy(identb[:, :], ident)
                dve.tensor_copy(maskb[:, :, :].rearrange("p a c -> p (a c)"), tab[:, C_SWA:C_SWA + 2 * P])
                dve.wait_ge(vecs_T, 1)
                dve.tensor_copy(vecT[:, 0:V_ROWS], ps[:, 5, 0:V_ROWS])
                for l in range(2):
                    for a in range(2):
                        c = 80 + (2 * l + a) * 4 * FT
                        ins = dve.tensor_copy(cwT[:, l, 2 * a:2 * a + 2, :].rearrange("p a m -> p (a m)"), ps[:, 5, c:c + 4 * FT])
                settle(ins)
                dve.tensor_tensor(vecT[:, V_MIX:V_MIX + KD], vecT[:, V_MID:V_MID + KD], vecT[:, V_MIXG:V_MIXG + KD], ALU.mult)
                dve.tensor_scalar(subg, vecT[:, V_SUBLN:V_SUBLN + 1], 1.0 - LAM_INIT, None, ALU.mult).then_inc(vecs_ready, 1)
                ahead(u + 2)
                for t in range(T):
                    rope_mul(1, t, "qkv0.1", u + 3, 2, 8)
                ahead(u + 3)
                ahead(u + 4)
                ahead(u + 5)
                for s in range(2):
                    block_max("A", s, nmax[:, s])
                block_mix(0)
                for s in range(N_A):
                    if s + 1 < N_A:
                        block_mix(s + 1)
                    if s + 2 < N_A:
                        block_max("A", s + 2, nmax[:, s + 2])
                    if s:
                        split_half()
                    if s in (3, 4):
                        rope_mul(2, s - 3, "qkv0.3", u + 7, 2, 8)
                    if s == 6:
                        o_norm(0, 0)
                    if s == 7:
                        o_lo(0, 4, 0, 0, True)
                rope_mul(3, 0, "qkv0.4", u + 9, 0, 8)
                split_half()
                rope_mul(3, 1, "qkv0.4", u + 9, 0, 8)
                o_norm(0, 1)
                split_half(2)
                o_lo(0, 4, 1, 1, True)
                for s in range(2):
                    block_max("B", s, nmax[:, 8 + s])
                block_mix(8)
                for s in range(N_A):
                    if s + 1 < N_A:
                        block_mix(9 + s)
                    if s + 2 < N_A:
                        block_max("B", s + 2, nmax[:, 10 + s])
                    if s in range(1, 7):
                        split_half()
                    if s == 6:
                        o_norm(1, 0)
                    if s == 7:
                        o_lo(4, 4, 2, 0, True)
                split_half()
                o_norm(1, 1)
                o_lo(4, 4, 3, 1, True)
                ahead(U0["wo0"] + 2)
                boundary(lambda t, hf: residual("wo0", U0["wo0"] + 3, t, hf), 1)
                ahead(U0["wo0"] + 3)
                ffn(0)
                boundary(lambda t, hf: residual("ffn0", U0["ffn0"] + 32, t, hf), 2)
                ahead(U0["ffn0"] + 32)
                for j in range(3):
                    ahead(U0["gate0"] + j)
                boundary(lambda t, hf: gate(0, t, hf), 3, (U0["qkv1"] - 1,))

                u = U0["qkv1"]
                rotary(3)
                ahead(u)
                for t in range(T):
                    rope_mul(4, t, "qkv1.0", u + 1, 0, 4)
                ahead(u + 1)
                ahead(u + 2)
                for t in range(T):
                    rope_mul(5, t, "qkv1.1", u + 3, 2, 8)

                def swa_max(s):
                    g, qt, r, i = SWA_BLOCKS[s]
                    hd = 8 * g + 4 * r + i
                    dve.wait_ge(s_ready, S_AT["1"] + s + 1)
                    sc = ps[:, 6 + s % 2, :].rearrange("p (j c) -> p j c", j=2)
                    settle(dve.tensor_reduce(nmax1[:, s], sc, AX.X, ALU.max, negate=True))
                    dve.tensor_tensor(nmax1[:, s], nmax1[:, s], nsink[:, hd:hd + 2], ALU.min).then_inc(max_ready, 1)

                def swa_out(s):
                    g, qt, r, i = SWA_BLOCKS[s]
                    c = (8 * g + 4 * r + i) * HD
                    dve.wait_ge(o_ready, S_AT["1"] + s + 1)
                    dve.wait_ge(sum_ready, s + 1)
                    dve.tensor_tensor(xn[:, qt, c:c + 2 * HD].rearrange("p (a d) -> p a d", d=HD),
                                      ps[:, OB, 0:2 * HD].rearrange("p (a d) -> p a d", d=HD),
                                      rsum1[:, s].unsqueeze(2).broadcast_to([P, 2, HD]), ALU.mult).then_inc(o_read, 1)

                swa_max(0)
                swa_max(1)
                ahead(u + 3)
                for s in range(2 * N_A):
                    if s % 4 in (1, 2):
                        split_half()
                    if s:
                        swa_out(s - 1)
                    if s + 2 < 2 * N_A:
                        swa_max(s + 2)
                    if s in (5, 9, 13):
                        o_lo(*((0, 4, 4, 0), (0, 4, 5, 1), (4, 4, 6, 0))[(s - 5) // 4], False)
                    if s in (1, 3):
                        rope_mul(6, s // 2, "qkv1.2", U0["qkv1"] + 5, 0, 8)
                swa_out(2 * N_A - 1)
                o_lo(4, 4, 7, 1, False)
                boundary(lambda t, hf: residual("wo1", U0["wo1"] + 3, t, hf), 4, first=(U0["wo1"] + 2,))
                ahead(U0["wo1"] + 3)
                ffn(1)
                boundary(lambda t, hf: residual("ffn1", U0["ffn1"] + 32, t, hf), 5)
                ahead(U0["ffn1"] + 32)
                for j in range(3):
                    ahead(U0["gate1"] + j)
                boundary(lambda t, hf: gate(1, t, hf), 6, (U0["in2"] - 1,))

                dve.wait_ge(gmid_loaded, 16)
                for t in range(T):
                    dve.wait_ge(h_ready, 22 + 2 * t)
                    dve.tensor_tensor(hg[:, t, :], h[:, t, :], gmid, ALU.mult).then_inc(hg_ready, 1)
                ahead(U0["in2"])
                for t in range(T):
                    c = 12 + t
                    dve.wait_ge(rstd_ready, c + 1)
                    dve.wait_ge(hg_ready, t + 1)
                    dve.tensor_scalar(h[:, t, :], hg[:, t, :], rstd[:, c:c + 1], None, ALU.mult)
                ahead(U0["in2"] + 1)

                def in2_evac(n):
                    kind, j, u, nb = IN2[n]
                    bank = in2_bank[n]
                    if nb == 2:
                        w = 256 if kind == "va1" else HALF
                        dst, c0 = (vb, 0) if kind == "vb" else (va, HALF if kind == "va1" else 0)
                        ul = u if kind == "va1" else u + 1
                        for t in range(T):
                            tile_done("in2." + kind, ul, t)
                            dve.tensor_scalar(dst[:, t, c0:c0 + w], ps[:, bank + t, 0:w], rboth[:, t:t + 1], None, ALU.mult)\
                                .then_inc(in2_read, 1)
                        return
                    dve.wait_ge(weights_used, u + 1)
                    dst = {"qa": qTa, "ka": kTa, "qb": qTb, "kb": kTb}[kind] if kind != "gl" else ga if j < 4 else gb
                    row = rBq if kind[0] == "q" else rB
                    dve.tensor_tensor(dst[:, 2 * (j % 4):2 * (j % 4) + 2, :], ps[:, bank, :].rearrange("p (m c) -> p m c", m=2),
                                      row[:, :].unsqueeze(1).broadcast_to([P, 2, SEQ]), ALU.mult).then_inc(in2_read, 1)

                def sb_block(s):
                    pr, qt = SB_BLOCKS[s]
                    nk = P * (qt + 1)
                    dve.wait_ge(sb_sel, 2 * s + 2)
                    for j in range(2):
                        ins = dve.tensor_tensor_scan(sbc[:, j, SEQ - nk:SEQ][:, ::-1], sbm[:, j * nk:(j + 1) * nk][:, ::-1],
                                                     ones[:, 0:nk], 1.0, ALU.mult, ALU.mult)
                    settle(ins)
                    pair = lambda v: v[:, 0:2 * nk].rearrange("p (j c) -> p j c", j=2)
                    dve.tensor_tensor(pair(sba), pair(sbp), sbc[:, :, SEQ - nk + 1:SEQ + 1], ALU.mult).then_inc(mix_ready, 1)

                def sb_out(s):
                    pr, qt = SB_BLOCKS[s]
                    dve.wait_ge(o_ready, S_AT["S"] + s + 1)
                    dve.tensor_copy(xn[:, qt, 2 * pr * HD:(2 * pr + 2) * HD], ps[:, OB, 0:2 * HD]).then_inc(o_read, 1)

                def dil_max(s):
                    j, qt = DIL_BLOCKS[s]
                    nk = P * (qt + 1)
                    dve.wait_ge(s_ready, S_AT["D"] + s + 1)
                    for g in range(3):
                        c0 = C_DIL + (g + 1) * SEQ - nk
                        ins = dve.scalar_tensor_tensor(dlL[:, s % 2, g * nk:(g + 1) * nk], tab[:, c0:c0 + nk], -SLOPES[4 * g + j],
                                                       ps[:, 6 + g // 2, (g % 2) * nk:(g % 2 + 1) * nk], ALU.mult, ALU.add)
                    settle(ins)
                    dve.tensor_reduce(nmax2[:, s:s + 1], dlL[:, s % 2, 0:3 * nk], AX.X, ALU.max, negate=True).then_inc(max_ready, 1)

                def dil_sum(s):
                    dve.wait_ge(exp_ready, 32 + s + 1)
                    settle(dve.reciprocal(rsum2[:, s:s + 1], esum2[:, s:s + 1]))

                def dil_out(s):
                    j, qt = DIL_BLOCKS[s]
                    dve.wait_ge(o_ready, S_AT["D"] + s + 1)
                    dve.tensor_scalar(xn[:, qt, HALF + j * HD:HALF + (j + 1) * HD], ps[:, OB, 0:HD], rsum2[:, s:s + 1], None,
                                      ALU.mult).then_inc(o_read, 1)

                settle(dve.tensor_copy(sbc[:, :, SEQ:SEQ + 1], ones[:, 0:2].unsqueeze(2)))
                for t in range(T):
                    dve.wait_ge(rboth_ready, t + 1)
                in2_evac(0)
                dve.wait_ge(rB_ready, 4)
                for n in range(1, 5):
                    ahead(IN2[n][2])
                    in2_evac(n)
                for s in range(9):
                    if s < 8:
                        sb_block(s)
                    if s == 7:
                        o_lo(0, 4, 8, 0, False)
                    ahead(IN2[5 + s][2])
                    if s:
                        sb_out(s - 1)
                    in2_evac(5 + s)
                o_lo(0, 4, 9, 1, False)
                for s in range(9):
                    if s < 8:
                        dil_max(s)
                        dil_sum(s)
                    if s == 7:
                        o_lo(4, 2, 10, 0, False)
                    if s == 8:
                        dil_out(7)
                    ahead(U0["gl2"] + 1 + s)
                    if 0 < s < 8:
                        dil_out(s - 1)
                    if s < 7:
                        in2_evac(in2_at["gl1"] + s)
                o_lo(4, 2, 11, 1, False)
                for j in range(4):
                    if j % 2 == 0:
                        dve.wait_ge(weights_used, U0["sbup"] + j // 2 + 1)
                    dve.wait_ge(gates_ready, j + 1)
                    dve.tensor_tensor(mB[:, j, :], ps[:, j, :], gb[:, 2 * j:2 * j + 2, :].rearrange("p a c -> p (a c)"), ALU.mult)

                def merge_lo(j):
                    dve.wait_ge(mhi_ready, j + 1)
                    dve.tensor_tensor(xlo[:, 2 * j:2 * j + 2, :].rearrange("p a c -> p (a c)"), mB[:, j, :],
                                      xhi[:, 2 * j:2 * j + 2, :].rearrange("p a c -> p (a c)").bitcast(F32),
                                      ALU.subtract).then_inc(mlo_ready, 1)

                for j in range(4):
                    if j < 3:
                        dve.wait_ge(dilup_done, j + 1)
                    else:
                        dve.wait_ge(weights_used, U0["dilup"] + 1)
                    dve.wait_ge(gates_ready, 4 + j + 1)
                    v = ga[:, 2 * j:2 * j + 2, :].rearrange("p a c -> p (a c)")
                    ins = dve.tensor_tensor(v, ps[:, 4 + j, :], v, ALU.mult)
                    if j == 1:
                        merge_lo(0)
                    settle(ins)
                    dve.tensor_tensor(mB[:, j, :], mB[:, j, :], v, ALU.add).then_inc(merged, 1)
                    if j > 1:
                        merge_lo(j - 1)
                merge_lo(3)
                ahead(U0["dilup"])
                for j in range(2):
                    ahead(U0["wout"] + j)
                boundary(lambda t, hf: residual("wout", U0["wout"] + 3, t, hf), 7, second=(U0["wout"] + 2,))
                ahead(U0["wout"] + 3)
                u0 = U0["mlp"]

                def square_lo(it, i=None):
                    b, n = it % 3, at(it + 1, MLP_TURN, i)
                    dve.wait_ge(relu_ready, n)
                    dve.tensor_tensor(rsq[:, b, :], rel[:, b, :], rel[:, b, :], ALU.mult).then_inc(sq_ready, 1)
                    dve.wait_ge(sq_ready, n)
                    dve.wait_ge(rhi_ready, n)
                    dve.tensor_tensor(olo[:, 2 * b:2 * b + 2, :].rearrange("p a c -> p (a c)"), rsq[:, b, :],
                                      ohi[:, 2 * b:2 * b + 2, :].rearrange("p a c -> p (a c)").bitcast(F32),
                                      ALU.subtract).then_inc(rlo_ready, 1)

                def mlp_iteration(it, i=None):
                    keep_ahead(u0 + 2 * it - 1, i)
                    square_lo(it, i)
                    keep_ahead(u0 + 2 * it, i)

                square_lo(0)
                ahead(U0["mlp"])
                mlp_iteration(1)
                with dve.Fori(0, 12 // MLP_TURN) as i:
                    for n in range(MLP_TURN):
                        mlp_iteration(2 + n, i)
                split[0] = u0 + 27 + RING - 1
                mlp_iteration(14)
                mlp_iteration(15)
                dve.wait_ge(gfin_loaded, 16)

                def last_residual(t, hf):
                    dve.wait_ge(r2_ready, t + 1)
                    res_done("mlp", u0 + 31, t, hf)
                    v = h[:, t, hf * HALF:(hf + 1) * HALF]
                    dve.scalar_tensor_tensor(v, ps[:, 2 * t + hf, :], r2[:, t:t + 1], v, ALU.mult, ALU.add).then_inc(h_ready, 1)

                def last_gain(t, hf):
                    cols = slice(hf * HALF, (hf + 1) * HALF)
                    dve.wait_ge(h_ready, 4 * 7 + 2 * t + hf + 1)
                    dve.tensor_tensor(pp[:, t, cols], h[:, t, cols], gfin[:, cols], ALU.mult).then_inc(gained, 1)

                def last_half(t):
                    dve.wait_ge(rstd_ready, 17 + t)
                    dve.wait_ge(gained, 2 * t + 1)
                    dve.tensor_scalar(xn[:, t, 0:HALF], pp[:, t, 0:HALF], rstd[:, 16 + t:17 + t], None, ALU.mult).then_inc(out_dve, 1)

                for hf in range(2):
                    last_residual(0, hf)
                    last_gain(0, hf)
                last_residual(1, 0)
                last_residual(1, 1)
                last_half(0)
                last_gain(1, 0)
                last_gain(1, 1)
                last_half(1)

            @block.tensor
            def _(pe):
                tuse = [0]

                def mm(o, l, r, start, stop):
                    return pe.matmul(o, l, r, start=start, stop=stop, skip_group_check=True)

                def slot(ring, u, kk):
                    return ring[:, u % RING, :].rearrange("p (k n) -> p k n", k=kk)

                def tm_half(u, t, hi, lo, kk, bank, start, stop, xwait=None, i=None, k0=0, wait=None):
                    n = UNIT // kk
                    w = min(n, HALF)
                    nb = n // w
                    wh, wl = slot(whi, u, kk), slot(wlo, u, kk)
                    if t == 0:
                        pe.wait_ge(*unit_split(u, i))
                    if wait:
                        pe.wait_ge(*wait)
                    for k in range(kk):
                        if xwait is not None:
                            pe.wait_ge(xlo_ready, xwait + KD * t + k + 1)
                        xh = hi[:, k0 + k, t * P:(t + 1) * P]
                        xl = lo[:, k0 + k, t * P:(t + 1) * P]
                        for b in range(nb):
                            mm(ps[:, bank + b, 0:w], xh, wh[:, k, b * w:(b + 1) * w], start and k == 0, False)
                        for b in range(nb):
                            mm(ps[:, bank + b, 0:w], xh, wl[:, k, b * w:(b + 1) * w], False, False)
                        for b in range(nb):
                            ins = mm(ps[:, bank + b, 0:w], xl, wh[:, k, b * w:(b + 1) * w], False, stop and k == kk - 1)
                    if t == 1:
                        ins.then_inc(weights_used, 1)
                    elif stop:
                        ins.then_inc(tile0_done, 1)

                def fm_half(u, m, hi, lo, kk, bank, xwait=None, i=None, k0=0, last=1, signal=None, part=None):
                    wh, wl = slot(whi, u, kk), slot(wlo, u, kk)
                    if m == 0:
                        pe.wait_ge(*unit_split(u, i))
                    o = ps[:, bank, (m % 2) * SEQ:(m % 2 + 1) * SEQ]
                    for k in range(kk) if part is None else part:
                        if xwait is not None and m == 0:
                            pe.wait_ge(xlo_ready, xwait + KD + max(k + 1, 2))
                        mm(o, wh[:, k, m * P:(m + 1) * P], hi[:, k0 + k, :], k == 0, False)
                        mm(o, wh[:, k, m * P:(m + 1) * P], lo[:, k0 + k, :], False, False)
                        ins = mm(o, wl[:, k, m * P:(m + 1) * P], hi[:, k0 + k, :], False, k == kk - 1)
                    if m == last and k == kk - 1:
                        ins.then_inc(weights_used, 1)
                    elif signal is not None:
                        ins.then_inc(signal, 1)

                def row_piece(u, t, b, hi, lo, kk, bank, c0, w, start, stop, k0=0, signal=None, by=1):
                    wh, wl = slot(whi, u, kk), slot(wlo, u, kk)
                    if t + b == 0:
                        pe.wait_ge(*unit_split(u))
                    for k in range(kk):
                        xh = hi[:, k0 + k, t * P:(t + 1) * P]
                        xl = lo[:, k0 + k, t * P:(t + 1) * P]
                        mm(ps[:, bank, 0:w], xh, wh[:, k, c0:c0 + w], start and k == 0, False)
                        mm(ps[:, bank, 0:w], xh, wl[:, k, c0:c0 + w], False, False)
                        ins = mm(ps[:, bank, 0:w], xl, wh[:, k, c0:c0 + w], False, stop and k == kk - 1)
                    if signal is not None:
                        ins.then_inc(signal, by)

                def norm_T(n, t, hf):
                    if n == 0:
                        pe.wait_ge(h_loaded[t], 16)
                    else:
                        pe.wait_ge(h_ready, 4 * (n - 1) + 2 * t + hf + 1)
                    for b in (2 * hf, 2 * hf + 1):
                        if t:
                            pe.wait_ge(xlo_ready, 2 * KD * n + 2 * b + 2)
                        for k in (2 * b, 2 * b + 1):
                            c = (k % 2) * SEQ + t * P
                            ins = pe.transpose(ps[:, 4 + b, c:c + P], h[:, t, k * P:(k + 1) * P], ident)
                        ins.then_inc(xT_ready, 1)

                BY_BANK = [(j, t, b) for t in range(T) for b in range(2) for j in range(2)]

                def last_rows(u, hi, lo, k0s, n, places, order=BY_BANK, before=()):
                    for i, (j, t, b) in enumerate(order):
                        for piece, step in before:
                            if piece == i:
                                step()
                        row_piece(u + j, t, b, hi, lo, 2, 2 * t + b, b * HALF, HALF, False, j == 1, k0s[j],
                                  None if j == 0 else weights_used if t and b else bank_done, 2 if t and b else 1)
                        if i in places:
                            norm_T(n, *divmod(places.index(i), 2))

                def rows_unit(stage, j, hi, lo, t, w=None):
                    tm_half(U0[stage] + j, t, hi, lo, 2, 2 * t, j == 0, False, None, None, k0=2 * j, wait=w)

                def rms_row(bank):
                    for t in range(T):
                        tokens[0] += 1
                        pe.wait_ge(diag_ready, tokens[0])
                        ins = mm(ps[:, bank, t * P:(t + 1) * P], ones[:, 0:P], diag[:, t, :], True, True)
                    ins.then_inc(rB_T, 1)

                tokens = [0]
                t_prev = [None]

                def t_begin(name):
                    assert T_ORDER[tuse[0]] == name
                    if t_prev[0]:
                        pe.wait_ge(*t_prev[0])
                    tuse[0] += 1
                    t_prev[0] = (t_free, tuse[0])

                def qk_T(c, name, t, srcs):
                    t_begin(f"{name}{t}")
                    pe.wait_ge(rope_ready, 2 * c + t + 1)
                    for n, src in enumerate(srcs):
                        ins = pe.transpose(ps[:, TB, n * P:(n + 1) * P], src, ident)
                    ins.then_inc(t_ready, 1)

                def flat_tiles(t, n):
                    return [rotA[:, t, i * P:(i + 1) * P] for i in range(n)]

                def keep_busy(n):
                    for _ in range(n):
                        mm(ps[:, 3, 0:P], zerob[:, :], zerob[:, :], True, True)

                pe.wait_ge(zeros_set, 1)
                keep_busy(WARM0)
                pe.wait_ge(ident_loaded, 16)
                pe.wait_ge(gain0_loaded, 16)
                pe.transpose(ps[:, 0, 0:16], stg[0:16, 5, :], ident[0:16, 0:16]).then_inc(gain0_T, 1)

                for hf in range(2):
                    norm_T(0, 0, hf)
                keep_busy(WARM1)
                pe.wait_ge(gain0_ready, 1)
                u = U0["qkv0"]

                def chunk_half(base, c, j, t, xwait=None):
                    tm_half(base + 2 * c + j, t, xhi, xlo, 4, 2 * (c % 2) + t, j == 0, j == 1,
                            None if xwait is None else xwait + 4 * j, k0=4 * j)

                def chunk_piece(u, j, t, a, bank):
                    done = None
                    if a:
                        done = weights_used if t else tile0_done if j else None
                    wh, wl = slot(whi, u, 4), slot(wlo, u, 4)
                    if u == 0 and t + a == 0:
                        pe.wait_ge(first_lo, 1)
                    elif t + a == 0 or u + t == 0:
                        pe.wait_ge(*unit_split(u))
                    for k in (2 * a, 2 * a + 1):
                        if u == 0:
                            pe.wait_ge(xlo_ready, KD * t + k + 1)
                        xh, xl = xhi[:, 4 * j + k, t * P:(t + 1) * P], xlo[:, 4 * j + k, t * P:(t + 1) * P]
                        mm(ps[:, bank + t, :], xh, wh[:, k, :], j + k == 0, False)
                        mm(ps[:, bank + t, :], xh, wl[:, k, :], False, False)
                        ins = mm(ps[:, bank + t, :], xl, wh[:, k, :], False, j == 1 and k == 3)
                    if done is not None:
                        ins.then_inc(done, 1)

                for hf in range(2):
                    norm_T(0, 1, hf)
                for t in range(T):
                    for a in range(2):
                        chunk_piece(0, 0, t, a, 0)
                for t in range(T):
                    chunk_half(u, 0, 1, t, 0)
                pe.wait_ge(p_loaded, 32)
                for b in range(2):
                    for k in range(2):
                        for t in range(T):
                            ins = pe.transpose(ps[:, 6 + b, k * SEQ + t * P:k * SEQ + (t + 1) * P],
                                               pst[:, b, t, k * P:(k + 1) * P], ident)
                    ins.then_inc(pT_ready, 1)
                pe.wait_ge(vecs_loaded, 16 * 13)
                pe.transpose(ps[:, 5, 0:V_ROWS], stg[0:V_ROWS, 0, :], ident[0:V_ROWS, 0:V_ROWS])
                n = 4 * FT
                for a in range(4):
                    ins = pe.transpose(ps[:, 5, 80 + a * n:80 + (a + 1) * n], stg[0:n, 1 + a, :], ident[0:n, 0:n])
                ins.then_inc(vecs_T, 1)
                for j in range(2):
                    for t in range(T):
                        chunk_half(u, 1, j, t)
                for t in range(T):
                    qk_T(0, "0q0", t, flat_tiles(t, 4))
                for t in range(T):
                    chunk_half(u, 2, 0, t)
                for t in range(T):
                    chunk_half(u, 2, 1, t)
                    qk_T(1, "0k0", t, flat_tiles(t, 4))
                pe.wait_ge(plo_ready, 2)
                pe.wait_ge(vecs_ready, 1)

                def scores0(st, s, j):
                    qt, i = BLOCKS[s]
                    tile = 4 * st + i
                    b = 8 * st + s
                    if j:
                        pe.wait_ge(head_done, b + 1)
                    elif b > 1:
                        pe.wait_ge(exp_ready, b - 1)
                    r = slice(j * HD, (j + 1) * HD)
                    mm(ps[:, 6 + s % 2, j * SEQ:(j + 1) * SEQ], qT[r, tile, qt * P:(qt + 1) * P], kT[r, tile, :], True, True)\
                        .then_inc(s_ready if j else head_done, 1)

                def first_scores0(st):
                    for j in range(2):
                        for s in range(2):
                            scores0(st, s, j)

                def probs_T0(st, s):
                    b = 8 * st + s
                    t_begin("0" + "AB"[st] + str(s))
                    pe.wait_ge(mix_ready, b + 1)
                    for k in range(2):
                        ins = pe.transpose(ps[:, TB, k * P:(k + 1) * P], Ac[:, s % 2, k * P:(k + 1) * P], ident)
                    ins.then_inc(t_ready, 1)

                def pv0(st, s):
                    qt, i = BLOCKS[s]
                    b = 8 * st + s
                    c = (4 * st + i) * P
                    pe.wait_ge(t_free, T_USE["0" + "AB"[st] + str(s)] + 1)
                    pe.wait_ge(v_ready, 2 * st + 2)
                    if b:
                        pe.wait_ge(o_read, b)
                    for k in range(2):
                        ins = mm(ps[:, OB, 0:P], ATd[:, s % 2, k, :], vtm[:, k, c:c + P], k == 0, k == 1)
                    ins.then_inc(o_ready, 1)

                def o_T(nt, count, src, final):
                    pe.wait_ge(*t_prev[0])
                    pe.wait_ge(*final)
                    for n in range(nt):
                        ins = pe.transpose(ps[:, TB, n * P:(n + 1) * P], src(n), ident)
                    ins.then_inc(oT_ready, 1)
                    t_prev[0] = (olo_ready, count + 1)

                def o_T0(st, qt):
                    o_T(4, 2 * st + qt, lambda n: xn[:, qt, st * HALF + n * P:st * HALF + (n + 1) * P], (on_ready, 2 * st + qt + 1))

                pe.wait_ge(t_free, 4)
                halves = [(c, j, t) for c in (3, 4, 5) for j in range(2) for t in range(T)]

                def half(n, parts=(0, 1)):
                    c, j, t = halves[n]
                    if n == 0:
                        pe.wait_ge(rope_read, 4)
                    if n == 4:
                        pe.wait_ge(v_ready, 2)
                    if n == 8:
                        pe.wait_ge(rope_read, 6)
                    for a in parts:
                        chunk_piece(u + 2 * c + j, j, t, a, 2 * (c % 2))

                first_scores0(0)
                half(0)
                for s in range(N_A):
                    probs_T0(0, s)
                    if s + 2 < N_A:
                        scores0(0, s + 2, 0)
                    half(s + 1, (0,))
                    if s + 2 < N_A:
                        scores0(0, s + 2, 1)
                    if s in (5, 6):
                        qk_T(2, "0q1", s - 5, flat_tiles(s - 5, 4))
                    if s == 7:
                        o_T0(0, 0)
                    if s:
                        pv0(0, s - 1)
                    half(s + 1, (1,))
                pv0(0, N_A - 1)
                half(9)
                qk_T(3, "0k1", 0, flat_tiles(0, 4))
                half(10)
                qk_T(3, "0k1", 1, flat_tiles(1, 4))
                half(11, (0,))
                o_T0(0, 1)

                def ple_piece(l, n):
                    hf, t = n // 2, n % 2
                    signal = (tile0_done, weights_used)[hf] if t else None
                    row_piece(U0[f"pp{l}"], t, hf, phi, plo, 2, PP_BANK[l][hf] + t, hf * HALF, HALF, True, True, 2 * l, signal)

                def wo_piece(l, n):
                    j, t, b = n // 4, n // 2 % 2, n % 2
                    row_piece(U0[f"wo{l}"] + j, t, b, ohi, olo, 2, 2 * t + b, b * HALF, HALF, j == 0, False, 2 * j,
                              weights_used if t and b else None)

                def wo_rest(l, n, last_T):
                    last_rows(U0[f"wo{l}"] + 2, ohi, olo, (4, 6), n, (3, 4, 6),
                              before=((0, lambda: pe.wait_ge(olo_ready, 4 * l + 3)), (1, last_T),
                                      (3, lambda: pe.wait_ge(olo_ready, 4 * l + 4))))

                def first_ups(u, n, between=None):
                    fm_half(u, 0, xhi, xlo, KD, 4, 2 * KD * n, part=range(0, 4))
                    norm_T(n, 1, 1)
                    fm_half(u + 1, 0, xhi, xlo, KD, 5, part=range(0, 4))
                    fm_half(u, 0, xhi, xlo, KD, 4, 2 * KD * n, part=range(4, KD))
                    fm_half(u, 1, xhi, xlo, KD, 4)
                    fm_half(u + 1, 0, xhi, xlo, KD, 5, part=range(4, KD))
                    if between:
                        between()
                    fm_half(u + 1, 1, xhi, xlo, KD, 5)

                def piece0(n):
                    if n == 0:
                        pe.wait_ge(rope_read, 8)
                    if n == 2:
                        pe.wait_ge(v_ready, 4)
                    if n in (4, 6):
                        pe.wait_ge(pp_ready, n - 2)
                    if n == 4:
                        pe.wait_ge(olo_ready, 2)
                    if n < 4:
                        ple_piece(0, n)
                    else:
                        wo_piece(0, n - 4)

                pe.wait_ge(t_free, T_USE["0k11"] + 1)
                first_scores0(1)
                half(11, (1,))
                piece0(0)
                for s in range(N_A):
                    probs_T0(1, s)
                    if s + 2 < N_A:
                        scores0(1, s + 2, 0)
                    if s:
                        pv0(1, s - 1)
                    if s + 2 < N_A:
                        scores0(1, s + 2, 1)
                    piece0(s + 1)
                pv0(1, N_A - 1)
                o_T0(1, 0)
                for n in range(9, 12):
                    piece0(n)
                wo_rest(0, 1, lambda: o_T0(1, 1))

                def ffn(l):
                    u0 = U0[f"ffn{l}"]

                    def up(ug, buf, gv, i=None):
                        for m in range(2):
                            fm_half(ug, m, xhi, xlo, KD, 4 + 2 * buf + gv, None, i)

                    def down(ud, it, start, stop, i=None):
                        pe.wait_ge(hlo_ready[l], at(it + 1, FFN_TURN, i))
                        for t in range(T):
                            tm_half(ud, t, ohi, olo, 2, 2 * t, start, stop, None, i, k0=2 * (it % 2))

                    def iteration(it, i=None):
                        ug = u0 + 3 * it - 1
                        for gv in range(2):
                            up(ug + gv, it % 2, gv, i)
                        down(ug + 2, it - 1, False, False, i)

                    first_ups(u0, 1 + 3 * l, lambda: rms_row(0))
                    pe.wait_ge(rB_ready, l + 1)
                    for bank in range(T * D // HALF):
                        mm(ps[:, bank, 0:P], identb[:, :], zerob[:, :], True, False)
                    with pe.Fori(0, 8 // FFN_TURN) as i:
                        for n in range(FFN_TURN):
                            iteration(1 + n, i)
                    for n, it in enumerate((9, 10)):
                        for gv in range(2):
                            up(u0 + 26 + 2 * n + gv, it % 2, gv)
                    down(u0 + 30, 8, False, False)
                    pe.wait_ge(hlo_ready[l], 10)
                    last_rows(u0 + 31, ohi, olo, (2, 0), 2 + 3 * l, (5, 6, 7),
                              [(0, 0, 0), (0, 0, 1), (0, 1, 0), (1, 0, 0), (1, 0, 1), (1, 1, 0), (0, 1, 1), (1, 1, 1)],
                              ((3, lambda: pe.wait_ge(hlo_ready[l], 11)),))

                def gate(l):
                    n = 2 + 3 * l
                    rows_unit(f"gate{l}", 0, xhi, xlo, 0, (xlo_ready, 2 * KD * n + 2))
                    norm_T(n, 1, 1)
                    rows_unit(f"gate{l}", 0, xhi, xlo, 1, (xlo_ready, 2 * KD * n + KD + 2))
                    for t in range(T):
                        rows_unit(f"gate{l}", 1, xhi, xlo, t, (xlo_ready, 2 * KD * n + KD * t + 4))
                    last_rows(U0[f"gate{l}"] + 2, xhi, xlo, (4, 6), n + 1, (6, 7), before=((0, lambda: pe.wait_ge(xlo_ready, 2 * KD * (n + 1))),))

                def first_chunk(n, unit):
                    unit(0, 0)
                    norm_T(n, 1, 0)
                    unit(1, 0)
                    norm_T(n, 1, 1)
                    unit(0, 1)
                    unit(1, 1)

                ffn(0)
                gate(0)

                u = U0["qkv1"]
                first_chunk(3, lambda j, t: chunk_half(u, 0, j, t, 2 * KD * 3))
                for t in range(T):
                    chunk_half(u, 1, 0, t)
                for t in range(T):
                    qk_T(4, "1k", t, flat_tiles(t, 2))
                    chunk_half(u, 1, 1, t)
                pe.wait_ge(rope_read, 10)

                def q1_piece(j, n):
                    chunk_piece(u + 4 + j, j, n // 2, n % 2, 0)

                for n in range(3):
                    q1_piece(0, n)
                qk_T(5, "1q0", 0, flat_tiles(0, 4))
                q1_piece(0, 3)
                qk_T(5, "1q0", 1, flat_tiles(1, 4))
                q1_piece(1, 0)

                def piece1(s):
                    if s < 2:
                        q1_piece(1, s + 2)
                    elif s < 6:
                        if s == 4:
                            pe.wait_ge(rope_read, 14)
                        ple_piece(1, s - 2)
                    elif 7 <= s < 15:
                        if s == 7:
                            pe.wait_ge(pp_ready, 8)
                        if s in (7, 11):
                            pe.wait_ge(olo_ready, 5 + s // 11)
                        wo_piece(1, (0, 1, 4, 5, 2, 3, 6, 7)[s - 7])

                def o_T1(st, qt):
                    o_T(4, 4 + 2 * st + qt, lambda n: xn[:, qt, (4 * st + n) * P:(4 * st + n + 1) * P],
                        (o_read, S_AT["1"] + 8 * st + 4 * qt + 4))

                def scores1(s):
                    g, qt, r, i = SWA_BLOCKS[s]
                    rows_ = slice(r * HD, (r + 1) * HD)
                    if s == 0:
                        pe.wait_ge(t_free, T_USE["1q01"] + 1)
                        pe.wait_ge(rope_read, 12)
                    if s in (8, 12):
                        pe.wait_ge(t_free, T_USE[f"1q1{s // 4 - 2}"] + 1)
                    c = (1 - qt) * P
                    pair = ps[:, 6 + s % 2, :].rearrange("p (j c) -> p j c", j=2)
                    for j in range(2):
                        mm(pair[:, j, :], qT[rows_, 4 * g + i + j, qt * P:(qt + 1) * P], kT[rows_, g, :], j == 0, False)
                    mm(pair[:, :, c:c + P], identb[:, :], maskb[:, qt, :].unsqueeze(1).broadcast_to([P, 2, P]), False, True)\
                        .then_inc(s_ready, 1)

                def probs_T1(s):
                    t_begin(f"1A{s}")
                    pe.wait_ge(exp_ready, S_AT["1"] + s + 1)
                    for j in range(2):
                        for k in range(2):
                            n = 2 * j + k
                            ins = pe.transpose(ps[:, TB, n * P:(n + 1) * P], Eb[:, s % 2, j, k * P:(k + 1) * P], ident)
                    ins.then_inc(t_ready, 1)

                def pv1(s):
                    g, qt, r, i = SWA_BLOCKS[s]
                    c = (2 * g + r) * HD
                    pe.wait_ge(t_free, T_USE[f"1A{s}"] + 1)
                    pe.wait_ge(o_read, S_AT["1"] + s)
                    for j in range(2):
                        for k in range(2):
                            ins = mm(ps[:, OB, j * HD:(j + 1) * HD], ATs[:, s % 2, 2 * j + k, :], vtm[:, k, c:c + HD],
                                     k == 0, k == 1)
                    ins.then_inc(o_ready, 1)

                scores1(0)
                scores1(1)
                q1_piece(1, 1)
                for s in range(2 * N_A):
                    probs_T1(s)
                    if s + 2 < 2 * N_A:
                        scores1(s + 2)
                    if s in (4, 6):
                        qk_T(6, "1q1", s // 2 - 2, flat_tiles(s // 2 - 2, 4))
                    if s:
                        pv1(s - 1)
                    if s in (5, 9, 13):
                        o_T1((s - 5) // 8, (s - 5) // 4 % 2)
                    piece1(s)
                pv1(2 * N_A - 1)
                wo_rest(1, 4, lambda: o_T1(1, 1))
                ffn(1)
                gate(1)

                def in2(n, between=None):
                    kind, j, u, nb = IN2[n]
                    bank = in2_bank[n]
                    if in2_need[n]:
                        pe.wait_ge(in2_read, in2_need[n])
                    if kind in ("vb", "va0"):
                        for i in range(2):
                            for t in range(T):
                                tm_half(u + i, t, xhi, xlo, 4, bank + t, i == 0, i == 1, k0=4 * i)
                    elif kind == "va1":
                        for t in range(T):
                            tm_half(u, t, xhi, xlo, KD, bank + t, True, True)
                    else:
                        for m in range(2):
                            fm_half(u, m, xhi, xlo, KD, bank)
                            if between and m == 0:
                                between()

                def scores_sb(s):
                    pr, qt = SB_BLOCKS[s]
                    nk = P * (qt + 1)
                    for j in range(2):
                        r = slice(j * HD, (j + 1) * HD)
                        ins = mm(ps[:, 6 + j, 0:nk], qTb[r, pr, qt * P:(qt + 1) * P], kTb[r, pr, 0:nk], True, True)
                    ins.then_inc(s_ready, 1)

                def weights_T_sb(s):
                    pr, qt = SB_BLOCKS[s]
                    t_begin(f"2S{s}")
                    pe.wait_ge(mix_ready, 16 + s + 1)
                    for n in range(2 * (qt + 1)):
                        ins = pe.transpose(ps[:, TB, n * P:(n + 1) * P], sba[:, n * P:(n + 1) * P], ident)
                    ins.then_inc(t_ready, 1)

                def pv_sb(s):
                    pr, qt = SB_BLOCKS[s]
                    pe.wait_ge(t_free, T_USE[f"2S{s}"] + 1)
                    pe.wait_ge(o_read, S_AT["S"] + s)
                    for j in range(2):
                        c = (2 * pr + j) * HD
                        for k in range(qt + 1):
                            n = j * (qt + 1) + k
                            ins = mm(ps[:, OB, j * HD:(j + 1) * HD], ETs[:, n * P:(n + 1) * P], vb[:, k, c:c + HD],
                                     k == 0, k == qt)
                    ins.then_inc(o_ready, 1)

                u = U0["in2"]
                first_chunk(6, lambda j, t: tm_half(u + j, t, xhi, xlo, 4, t, j == 0, j == 1, 2 * KD * 6 + 4 * j, k0=4 * j))
                in2(1)
                rms_row(7)
                for n in range(2, 5):
                    in2(n)

                def first_scores():
                    pe.wait_ge(in2_read, in2_count[4])
                    scores_sb(0)

                for s in range(9):
                    if s:
                        weights_T_sb(s - 1)
                    if 0 < s < 8:
                        scores_sb(s)
                    if s == 7:
                        o_T(4, 8, lambda n: xn[:, 0, n * P:(n + 1) * P], (o_read, S_AT["S"] + 4))
                    in2(5 + s, None if s else first_scores)
                    if s:
                        pv_sb(s - 1)
                o_T(4, 9, lambda n: xn[:, 1, n * P:(n + 1) * P], (o_read, S_AT["S"] + 8))

                def scores_dil(s):
                    j, qt = DIL_BLOCKS[s]
                    nk = P * (qt + 1)
                    for g in range(3):
                        hd = 4 * g + j
                        r = slice((hd % 2) * HD, (hd % 2 + 1) * HD)
                        ins = mm(ps[:, 6 + g // 2, (g % 2) * nk:(g % 2 + 1) * nk], qTa[r, hd // 2, qt * P:(qt + 1) * P],
                                 kTa[r, hd // 2, 0:nk], True, True)
                    ins.then_inc(s_ready, 1)

                def probs_T_dil(s, part):
                    j, qt = DIL_BLOCKS[s]
                    n = 3 * (qt + 1)
                    t_begin(f"2D{s}" + "ab"[part])
                    pe.wait_ge(exp_ready, 32 + s + 1)
                    for a in range(4 * part, min(n, 4 * part + 4)):
                        b = a - 4 * part
                        ins = pe.transpose(ps[:, TB, b * P:(b + 1) * P], dlL[:, s % 2, a * P:(a + 1) * P], ident)
                    ins.then_inc(t_ready, 1)

                def pv_dil(s):
                    j, qt = DIL_BLOCKS[s]
                    pe.wait_ge(t_free, T_USE[f"2D{s}" + "ab"[qt]] + 1)
                    pe.wait_ge(o_read, S_AT["D"] + s)
                    n = 3 * (qt + 1)
                    for a in range(n):
                        g, k = a // (qt + 1), a % (qt + 1)
                        c = (4 * g + j) * HD
                        ins = mm(ps[:, OB, 0:HD], ETb[:, a * P:(a + 1) * P], va[:, k, c:c + HD], a == 0, a == n - 1)
                    ins.then_inc(o_ready, 1)

                def sb_up(c, m):
                    bank = 2 * c + m // 2
                    if m % 2 == 0:
                        pe.wait_ge(in2_read, last_use[bank])
                    fm_half(U0["sbup"] + c, m, ohi, olo, 4, bank, last=3)

                pe.wait_ge(in2_read, in2_count[in2_at["va10"]])
                def o_T_dil(qt):
                    o_T(2, 10 + qt, lambda n: xn[:, qt, HALF + n * P:HALF + (n + 1) * P], (o_read, S_AT["D"] + 4 * qt + 4))

                for s in range(8):
                    if s:
                        probs_T_dil(s - 1, 0)
                    scores_dil(s)
                    if s and DIL_BLOCKS[s - 1][1]:
                        probs_T_dil(s - 1, 1)
                    if s < 7:
                        in2(in2_at["gl1"] + s)
                    else:
                        sb_up(0, 0)
                        sb_up(0, 1)
                        o_T_dil(0)
                        sb_up(0, 2)
                        sb_up(0, 3)
                    if s:
                        pv_dil(s - 1)
                probs_T_dil(7, 0)
                sb_up(1, 0)
                probs_T_dil(7, 1)
                sb_up(1, 1)
                pv_dil(7)
                sb_up(1, 2)
                o_T_dil(1)
                sb_up(1, 3)
                pe.wait_ge(olo_ready, 12)
                for m in range(8):
                    fm_half(U0["dilup"], m, ohi, olo, 2, 4 + m // 2, k0=4, last=7, signal=dilup_done if m in (1, 3, 5) else None)
                for j in range(2):
                    for t in range(T):
                        rows_unit("wout", j, xhi, xlo, t, (mlo_ready, j + 1))
                last_rows(U0["wout"] + 2, xhi, xlo, (4, 6), 7, (2, 4, 6), before=((0, lambda: pe.wait_ge(mlo_ready, 4)),))

                u0 = U0["mlp"]

                def mlp_up(u, it, i=None):
                    for m in range(2):
                        fm_half(u, m, xhi, xlo, KD, 4 + it % 3, None, i)

                def mlp_down(u, it, start, stop, i=None):
                    pe.wait_ge(rlo_ready, at(it + 1, MLP_TURN, i))
                    for t in range(T):
                        tm_half(u, t, ohi, olo, 2, 2 * t, start, stop, None, i, k0=2 * (it % 3))

                def mlp_iteration(it, i=None):
                    mlp_up(u0 + 2 * it - 1, it, i)
                    mlp_down(u0 + 2 * it, it - 1, it == 1, False, i)

                first_ups(u0, 7)
                mlp_down(u0 + 2, 0, True, False)
                with pe.Fori(0, 12 // MLP_TURN) as i:
                    for n in range(MLP_TURN):
                        mlp_iteration(2 + n, i)
                mlp_iteration(14)
                mlp_iteration(15)
                pe.wait_ge(rlo_ready, 16)
                for t in range(T):
                    for b in range(2):
                        row_piece(u0 + 31, t, b, ohi, olo, 2, 2 * t + b, b * HALF, HALF, False, True, 0,
                                  weights_used if t and b else bank_done)


NAMES = ["x", "p", "positions", "attn_norm", "ffn_norm", "ple_norm", "final_norm", "diff_w_qkv", "diff_w_o",
         "diff_lambda", "diff_subln", "swa_w_qkv", "swa_w_o", "swa_sinks", "ffn_w_up", "ffn_conv_w", "ffn_conv_b",
         "ffn_w_down", "ple_w_proj", "ple_w_gate", "norm_mix_g_2", "w_in_2", "b_gate_2", "w_up_dil_2", "w_up_sb_2",
         "w_out_2", "norm_mlp_g_2", "w_mlp_in_2", "w_mlp_out_2", "norm_final_g_2"]


def kernel(**inputs):
    import concourse.bacc as bacc
    from concourse.bass_utils import run_bass_kernel_spmd

    nc = bacc.Bacc("TRN2", target_bir_lowering=False, num_devices=1)
    arrays, args = {}, []
    for name in NAMES:
        a = np.ascontiguousarray(inputs[name])
        arrays[f"in_{name}"] = a
        args.append(nc.dram_tensor(f"in_{name}", a.shape, mybir.dt.from_np(a.dtype), kind="ExternalInput").ap())
    table = constants()
    arrays["in_table"] = table
    args.append(nc.dram_tensor("in_table", table.shape, F32, kind="ExternalInput").ap())
    args.append(nc.dram_tensor("out_0", (1, SEQ, D), F32, kind="ExternalOutput").ap())
    three_layer_kernel(nc, *args)
    r = run_bass_kernel_spmd(nc, [arrays], core_ids=[0])
    return r.results[0]["out_0"]
```
